# Optimizing a Trainium2 kernel written in Bass

```python
import math
import jax
import jax.numpy as jnp
from jax import lax
import numpy as np

D_MODEL = 1024
BATCH = 1
SEQ = 256
DEPTH = 1

A_HEADS = 8
A_HEAD_DIM = 64
A_WIDTH = A_HEADS * A_HEAD_DIM
MOBA_BLOCK = 256
MOBA_TOPK = 3
MOBA_Q_CHUNK = 32
REL_BUCKETS = 32
REL_MAX_DIST = 128
B_HEADS = 8
B_HEAD_DIM = 64
B_WIDTH = B_HEADS * B_HEAD_DIM
DECAY_LORA = 64
AAA_LORA = 64
GATE_LORA = 160
GN_EPS = 64e-5
COL_A = 3 * A_WIDTH
COL_B = 3 * B_WIDTH + DECAY_LORA + AAA_LORA + GATE_LORA
COL_G = 2 * D_MODEL
TOTAL_IN = COL_A + COL_B + COL_G
PEER_HEADS = 8
PEER_NKEYS = 128
PEER_EXPERTS = PEER_NKEYS * PEER_NKEYS
PEER_TOPK = 16
PEER_QDIM = 256
PEER_HALF = PEER_QDIM // 2
PEER_CHUNK = 128
RMS_EPS = 1e-6
NEG = -1e30

kernel_name = 'moba_rwkv7_peer_hybrid'

def rmsnorm(x, g):
    xf = x.astype(jnp.float32)
    y = xf * lax.rsqrt(jnp.mean(xf * xf, axis=-1, keepdims=True) + RMS_EPS)
    return (y * g.astype(jnp.float32)).astype(x.dtype)

def rel_bucket(dist):
    n = jnp.maximum(dist, 0)
    max_exact = REL_BUCKETS // 2
    nf = jnp.maximum(n, 1).astype(jnp.float32)
    large = max_exact + (jnp.log(nf / max_exact) / math.log(REL_MAX_DIST / max_exact)
                         * (REL_BUCKETS - max_exact)).astype(jnp.int32)
    large = jnp.minimum(large, REL_BUCKETS - 1)
    return jnp.where(n < max_exact, n, large)

def moba_attention(q, k, v, rel_bias):
    bsz, seq, heads, hd = q.shape
    n_blocks = -(-seq // MOBA_BLOCK)
    seq_pad = n_blocks * MOBA_BLOCK
    padw = ((0, 0), (0, seq_pad - seq), (0, 0), (0, 0))
    qh = jnp.pad(q, padw).transpose(0, 2, 1, 3)
    kh = jnp.pad(k, padw).transpose(0, 2, 1, 3)
    vh = jnp.pad(v, padw).transpose(0, 2, 1, 3)
    kb = kh.reshape(bsz, heads, n_blocks, MOBA_BLOCK, hd)
    vb = vh.reshape(bsz, heads, n_blocks, MOBA_BLOCK, hd)
    kbar = jnp.mean(kb.astype(jnp.float32), axis=3).astype(q.dtype)
    n_sel = min(MOBA_TOPK, n_blocks)
    scale = 1.0 / math.sqrt(hd)
    b_ix = jnp.arange(bsz)[:, None, None, None]
    h_ix = jnp.arange(heads)[None, :, None, None]
    blk_pos = jnp.arange(MOBA_BLOCK)

    def one_chunk(c):
        q0 = c * MOBA_Q_CHUNK
        blk = q0 // MOBA_BLOCK
        qc = lax.dynamic_slice_in_dim(qh, q0, MOBA_Q_CHUNK, axis=2)
        qpos = q0 + jnp.arange(MOBA_Q_CHUNK)
        k_own = lax.dynamic_slice_in_dim(kh, blk * MOBA_BLOCK, MOBA_BLOCK, axis=2)
        v_own = lax.dynamic_slice_in_dim(vh, blk * MOBA_BLOCK, MOBA_BLOCK, axis=2)
        dist_own = qpos[:, None] - (blk * MOBA_BLOCK + blk_pos)[None, :]
        s_own = (jnp.einsum('bhqd,bhkd->bhqk', qc, k_own).astype(jnp.float32) * scale
                 + rel_bias[:, rel_bucket(dist_own)].astype(jnp.float32)[None])
        s_own = jnp.where(dist_own >= 0, s_own, NEG)
        gate = jnp.einsum('bhqd,bhnd->bhqn', qc, kbar).astype(jnp.float32)
        gate = jnp.where(jnp.arange(n_blocks) < blk, gate, -jnp.inf)
        _, sel = lax.top_k(gate, n_sel)
        valid = sel < blk
        k_g = kb[b_ix, h_ix, sel]
        v_g = vb[b_ix, h_ix, sel]
        dist_sel = qpos[:, None, None] - (sel[..., None] * MOBA_BLOCK + blk_pos)
        bias_sel = rel_bias[h_ix[..., None], rel_bucket(dist_sel)].astype(jnp.float32)
        s_sel = jnp.einsum('bhqd,bhqnkd->bhqnk', qc, k_g).astype(jnp.float32) * scale + bias_sel
        s_sel = jnp.where(valid[..., None], s_sel, NEG)
        logits = jnp.concatenate(
            [s_own, s_sel.reshape(bsz, heads, MOBA_Q_CHUNK, n_sel * MOBA_BLOCK)], axis=-1)
        p = jax.nn.softmax(logits, axis=-1).astype(v.dtype)
        p_own = p[..., :MOBA_BLOCK]
        p_sel = p[..., MOBA_BLOCK:].reshape(bsz, heads, MOBA_Q_CHUNK, n_sel, MOBA_BLOCK)
        return (jnp.einsum('bhqk,bhkd->bhqd', p_own, v_own)
                + jnp.einsum('bhqnk,bhqnkd->bhqd', p_sel, v_g))

    out = lax.map(one_chunk, jnp.arange(seq_pad // MOBA_Q_CHUNK))
    out = out.transpose(1, 0, 3, 2, 4).reshape(bsz, seq_pad, heads * hd)
    return out[:, :seq]

def rwkv7_time_mix(pb, w0, w_lora_up, a0, a_lora_up, g_lora_up, k_k, k_a, r_k, lnx_g, lnx_b):
    f32 = jnp.float32
    bsz, seq, _ = pb.shape
    o1 = 3 * B_WIDTH
    r, k, v, xw, xa, xg = jnp.split(
        pb, [B_WIDTH, 2 * B_WIDTH, o1, o1 + DECAY_LORA, o1 + DECAY_LORA + AAA_LORA], axis=-1)
    w = -jax.nn.softplus(-(w0 + jnp.tanh(xw) @ w_lora_up).astype(f32)) - 0.5
    decay = jnp.exp(-jnp.exp(w))
    a = jax.nn.sigmoid((a0 + xa @ a_lora_up).astype(f32))
    g = (jax.nn.sigmoid(xg) @ g_lora_up).astype(f32)

    def heads(t):
        return t.astype(f32).reshape(bsz, seq, B_HEADS, B_HEAD_DIM)

    r, k, v, decay, a = heads(r), heads(k), heads(v), heads(decay), heads(a)
    kk = k * k_k.astype(f32).reshape(B_HEADS, B_HEAD_DIM)
    kk = kk / jnp.maximum(jnp.sqrt(jnp.sum(kk * kk, axis=-1, keepdims=True)), 1e-12)
    k = k * (1.0 + (a - 1.0) * k_a.astype(f32).reshape(B_HEADS, B_HEAD_DIM))

    def step(state, inp):
        r_t, w_t, k_t, v_t, kk_t, a_t = inp
        sk = jnp.einsum('bhij,bhj->bhi', state, kk_t)
        state = (state * w_t[:, :, None, :]
                 - sk[..., None] * (kk_t * a_t)[:, :, None, :]
                 + v_t[..., None] * k_t[:, :, None, :])
        return state, jnp.einsum('bhij,bhj->bhi', state, r_t)

    xs = tuple(jnp.moveaxis(t, 1, 0) for t in (r, decay, k, v, kk, a))
    s0 = jnp.zeros((bsz, B_HEADS, B_HEAD_DIM, B_HEAD_DIM), f32)
    _, o = lax.scan(step, s0, xs)
    o = jnp.moveaxis(o, 0, 1)
    mu = jnp.mean(o, axis=-1, keepdims=True)
    var = jnp.mean(jnp.square(o - mu), axis=-1, keepdims=True)
    o = ((o - mu) * lax.rsqrt(var + GN_EPS)).reshape(bsz, seq, B_WIDTH)
    o = o * lnx_g.astype(f32) + lnx_b.astype(f32)
    bonus = (jnp.sum(r * k * r_k.astype(f32), axis=-1, keepdims=True) * v).reshape(bsz, seq, B_WIDTH)
    return ((o + bonus) * g).astype(pb.dtype)

def hybrid_mixer(xn, w_in, rel_bias, rwkv_mu, w0, w_lora_up, a0, a_lora_up, g_lora_up,
                 k_k, k_a, r_k, lnx_g, lnx_b, w_proj_a, w_proj_b, w_out):
    bsz, seq, _ = xn.shape
    p = xn @ w_in
    pa, pb, pg = jnp.split(p, [COL_A, COL_A + COL_B], axis=-1)
    q, k, v = (t.reshape(bsz, seq, A_HEADS, A_HEAD_DIM) for t in jnp.split(pa, 3, axis=-1))
    o_a = moba_attention(q, k, v, rel_bias)
    pb_prev = jnp.pad(pb, ((0, 0), (1, 0), (0, 0)))[:, :seq]
    pb_mix = pb + rwkv_mu * (pb_prev - pb)
    o_b = rwkv7_time_mix(pb_mix, w0, w_lora_up, a0, a_lora_up, g_lora_up,
                         k_k, k_a, r_k, lnx_g, lnx_b)
    gate_a, gate_b = jnp.split(jax.nn.sigmoid(pg.astype(jnp.float32)), 2, axis=-1)
    y = (gate_a * (o_a @ w_proj_a).astype(jnp.float32)
         + gate_b * (o_b @ w_proj_b).astype(jnp.float32))
    return y.astype(xn.dtype) @ w_out

def peer_ffn(xn, peer_wq, peer_subkeys, peer_u, peer_v):
    f32 = jnp.float32
    bsz, seq, d = xn.shape
    n_tok = bsz * seq
    xt = xn.reshape(n_tok, d)
    q = (xt @ peer_wq).reshape(n_tok, PEER_HEADS, 2, PEER_HALF)
    s = jnp.einsum('thpc,hpnc->thpn', q, peer_subkeys).astype(f32)
    top_s, top_i = lax.top_k(s, PEER_TOPK)
    kk2 = PEER_TOPK * PEER_TOPK
    cand_s = (top_s[:, :, 0, :, None] + top_s[:, :, 1, None, :]).reshape(n_tok, PEER_HEADS, kk2)
    cand_i = (top_i[:, :, 0, :, None] * PEER_NKEYS + top_i[:, :, 1, None, :]).reshape(n_tok, PEER_HEADS, kk2)
    best_s, best_pos = lax.top_k(cand_s, PEER_TOPK)
    idx = jnp.take_along_axis(cand_i, best_pos, axis=-1)
    gates = jax.nn.softmax(best_s, axis=-1)
    n_ch = n_tok // PEER_CHUNK
    xr = xt.reshape(n_ch, PEER_CHUNK, d)
    ir = idx.reshape(n_ch, PEER_CHUNK, PEER_HEADS, PEER_TOPK)
    gr = gates.reshape(n_ch, PEER_CHUNK, PEER_HEADS, PEER_TOPK)

    def one_chunk(args):
        xc, ic, gc = args
        u_g = peer_u[ic]
        h = jax.nn.gelu(jnp.einsum('chkd,cd->chk', u_g, xc).astype(f32), approximate=False) * gc
        v_g = peer_v[ic]
        return jnp.einsum('chk,chkd->cd', h.astype(peer_v.dtype), v_g)

    out = lax.map(one_chunk, (xr, ir, gr))
    return out.reshape(bsz, seq, d).astype(xn.dtype)

def setup_inputs(seed: int = 0) -> dict:
    key = jax.random.key(seed)
    ks = jax.random.split(key, 26)
    f32 = jnp.float32
    L = DEPTH

    def nrm(k, shape, scale):
        return jax.random.normal(k, shape, f32) * scale

    ratio = jnp.arange(B_WIDTH, dtype=f32) / (B_WIDTH - 1)
    return {
        'x': nrm(ks[0], (BATCH, SEQ, D_MODEL), 1.0),
        'norm1_g': 1.0 + nrm(ks[1], (L, D_MODEL), 0.02),
        'w_in': nrm(ks[2], (L, D_MODEL, TOTAL_IN), D_MODEL ** -0.5),
        'rwkv_mu': jax.random.uniform(ks[3], (L, COL_B), f32),
        'w0': (-6.5 + 5.0 * ratio ** 0.85)[None, :] + nrm(ks[4], (L, B_WIDTH), 0.1),
        'w_lora_up': nrm(ks[5], (L, DECAY_LORA, B_WIDTH), 0.1),
        'a0': nrm(ks[6], (L, B_WIDTH), 0.1),
        'a_lora_up': nrm(ks[7], (L, AAA_LORA, B_WIDTH), AAA_LORA ** -0.5),
        'g_lora_up': nrm(ks[8], (L, GATE_LORA, B_WIDTH), GATE_LORA ** -0.5),
        'k_k': 0.85 + nrm(ks[9], (L, B_WIDTH), 0.05),
        'k_a': 1.0 + nrm(ks[10], (L, B_WIDTH), 0.05),
        'r_k': nrm(ks[11], (L, B_HEADS, B_HEAD_DIM), 0.1),
        'lnx_g': 1.0 + nrm(ks[12], (L, B_WIDTH), 0.02),
        'lnx_b': nrm(ks[13], (L, B_WIDTH), 0.02),
        'w_proj_a': nrm(ks[14], (L, A_WIDTH, D_MODEL), A_WIDTH ** -0.5),
        'w_proj_b': nrm(ks[15], (L, B_WIDTH, D_MODEL), B_WIDTH ** -0.5),
        'w_out': nrm(ks[16], (L, D_MODEL, D_MODEL), D_MODEL ** -0.5),
        'norm2_g': 1.0 + nrm(ks[17], (L, D_MODEL), 0.02),
        'peer_wq': nrm(ks[18], (L, D_MODEL, PEER_HEADS * PEER_QDIM), D_MODEL ** -0.5),
        'peer_subkeys': nrm(ks[19], (L, PEER_HEADS, 2, PEER_NKEYS, PEER_HALF), PEER_HALF ** -0.5),
        'peer_u': nrm(ks[20], (L, PEER_EXPERTS, D_MODEL), D_MODEL ** -0.5),
        'peer_v': nrm(ks[21], (L, PEER_EXPERTS, D_MODEL), 0.5),
        'rel_bias': nrm(ks[22], (A_HEADS, REL_BUCKETS), 0.5),
        'normf_g': 1.0 + nrm(ks[23], (D_MODEL,), 0.02),
    }

def reference(x, norm1_g, w_in, rwkv_mu, w0, w_lora_up, a0, a_lora_up, g_lora_up, k_k, k_a,
              r_k, lnx_g, lnx_b, w_proj_a, w_proj_b, w_out, norm2_g, peer_wq, peer_subkeys,
              peer_u, peer_v, rel_bias, normf_g):
    h = x
    for l in range(DEPTH):
        xn = rmsnorm(h, norm1_g[l])
        h = h + hybrid_mixer(xn, w_in[l], rel_bias, rwkv_mu[l], w0[l], w_lora_up[l], a0[l],
                             a_lora_up[l], g_lora_up[l], k_k[l], k_a[l], r_k[l], lnx_g[l],
                             lnx_b[l], w_proj_a[l], w_proj_b[l], w_out[l])
        xn = rmsnorm(h, norm2_g[l])
        h = h + peer_ffn(xn, peer_wq[l], peer_subkeys[l], peer_u[l], peer_v[l])
    return rmsnorm(h, normf_g)


_drawn_inputs = setup_inputs


def setup_inputs(seed=0):
    import zlib

    import numpy as np

    out = dict(_drawn_inputs(seed))
    spreads = {}
    factors = {'lnx_g': 2.976, 'lnx_b': 2.873, 'normf_g': 2.902}
    for name, (base, spread) in spreads.items():
        noise = np.random.default_rng([zlib.crc32(name.encode()), seed]).standard_normal(out[name].shape)
        drawn = base * np.exp(spread * noise) if base else spread * noise
        out[name] = jnp.asarray(drawn.astype(out[name].dtype))
    for name, factor in factors.items():
        out[name] = (out[name] * factor).astype(out[name].dtype)
    return out
```

```python
import math
from contextlib import ExitStack

import concourse.bass as bass
from concourse import mybir

F32 = mybir.dt.float32
F32R = mybir.dt.float32r
BF16 = mybir.dt.bfloat16
U32 = mybir.dt.uint32
ALU = mybir.AluOpType
ACT = mybir.ActivationFunctionType
AX_X = mybir.AxisListType.X

P = 128
T = 256
NT = T // P
D = 1024
KT = D // P
HEADS = 8
HD = 64
W = HEADS * HD
CT = W // P
LORA = 64
GLORA = 160
NB_IN = 28
NB_GATE = 16
NKEYS = 128
TOPK = 16
RMS_EPS = 1e-6
GN_EPS = 64e-5
NEG = -1e30
LOWEST = -3.0e38
RAW = 4
SPLIT = 2
HALF = NKEYS // 2

V_N1, V_N2, V_NF = 0, 8, 16
V_W0, V_A0, V_KK, V_KA, V_RK, V_LG, V_LB = 24, 28, 32, 36, 40, 44, 48
V_MU = 52
NMIX = 15
NVEC = V_MU + NMIX

C_ID, C_ONE, C_BLK, C_IOTA, C_M4, C_NM1, C_NM1T, C_LV = 0, 128, 256, 384, 512, 1024, 1152, 1280
LEVELS = [2, 4, 8, 16, 32, 64]
NCONST = C_LV + 128 * len(LEVELS)


def block_program(nc, x, w_in, w_proj, w_out, w_q, u_t, v_t, vecs, lora_wa, lora_g, rel_bias_t, bucket_onehot,
                  consts, subkeys_t, out):
    with ExitStack() as ctx:
        def sb(name, shape, dt=F32):
            return ctx.enter_context(nc.sbuf_tensor(name, shape, dt))

        def sem(name):
            return ctx.enter_context(nc.semaphore(name))

        arena_at = -(-nc.sbuf_base // 32) * 32
        arena = sb("arena", [P, P * T])
        xT = sb("xT", [P, KT, T])
        xh = sb("xh", [P, KT, T], F32R)
        xl = sb("xl", [P, KT, T], F32R)
        raw = sb("raw", [P, RAW, D])
        hi = sb("hi", [P, SPLIT, D], F32R)
        lo = sb("lo", [P, SPLIT, D], F32R)
        con = sb("con", [P, NCONST])
        vec = sb("vec", [P, NVEC])
        i1T = sb("i1T", [P, T])
        i2T = sb("i2T", [P, T])
        gT = sb("gT", [P, T])
        oh1 = sb("oh1", [P, 2, 4, P])
        oh2 = sb("oh2", [P, 2, 4, P])
        gh = sb("gh", [P, SPLIT, T], F32R)
        gl = sb("gl", [P, SPLIT, T], F32R)
        small = sb("small", [P, 64])

        PS = ctx.enter_context(nc.psum_tensor("PS", [P, 8, 512], F32))
        bias_dram = nc.dram_tensor("bias_rows", [HEADS, P, 512], F32, kind="Internal").ap()

        ident = con[:, C_ID:C_ID + P]
        ones = con[:, C_ONE:C_ONE + P]
        blk = con[:, C_BLK:C_BLK + P]
        iota = con[:, C_IOTA:C_IOTA + P]
        mask4 = con[:, C_M4:C_M4 + 512]
        zeros = con[:, C_LV:C_LV + 256].bitcast(BF16)

        def area(a, n, *shape):
            v = arena[:, a:a + n]
            if len(shape) == 2:
                return v.rearrange("p (a b) -> p a b", b=shape[1])
            if len(shape) == 3:
                return v.rearrange("p (a b c) -> p a b c", b=shape[1], c=shape[2])
            return v

        gates = area(0, 4096, 16, T)
        oh = nc.alloc_sbuf_tensor_at("oh", [P, KT, T], F32R, offset=arena_at + 4 * 4096)
        ol = nc.alloc_sbuf_tensor_at("ol", [P, KT, T], F32R, offset=arena_at + 4 * 6144)
        R0 = 8192
        pT = area(R0, 28 * T, 28, T)
        xin = area(R0 + 8192, 2048, NT, D)
        sq = area(R0 + 10240, 2048, KT, T)
        xn = area(R0 + 12288, 2048, KT, T)
        rstd = area(R0 + 14336, T)
        vtokA = area(R0 + 7168, 1024, NT, W)
        biasT = area(R0 + 8192, 3072, HEADS, 384)
        Sb = area(R0 + 11264, 3072, HEADS, 384)
        PTs = area(R0 + 14336, 3072, HEADS, 384)
        mix = area(R0 + 17408, 3840, NMIX, T)
        rowsb = area(R0 + 21248, 512)
        lwa = area(R0 + 21760, 512)
        lg0 = area(R0 + 22272, 512)
        lg1 = area(R0 + 22784, 512)
        bonehot = area(R0 + 23296, 512)
        relb = area(R0 + 23808, 8)

        def slot(n):
            return area(R0 + 1024 * n, 1024, CT, T)
        gB, bonus, bh, kh, vtok = slot(0), slot(1), slot(4), slot(5), area(R0 + 6144, 1024, NT, W)
        KR = area(R0 + 2048, 2048, CT, 2, T)
        tokk = area(R0 + 7168, 512)
        tokb = area(R0 + 7680, 512)
        lw, aB = slot(8), slot(9)
        Lz = area(R0 + 10240, CT * 257, CT, 257)
        E = area(R0 + 12288, CT * 2 * 129, CT, 2, 129)
        EI, kk, k2 = slot(14), slot(15), slot(16)
        rB, kB, vB = mix[:, 0:4], mix[:, 4:8], mix[:, 8:12]
        tmp = area(R0 + 23296, 1024, CT, T)
        mats = area(R0 + 8192, 8192, 16, 4, P)
        X = area(R0 + 16384, 2048, 16, P)
        XT = area(R0 + 18432, 2048, 16, P)
        P1 = area(R0 + 20480, 2048, 16, P)
        Gs = area(R0 + 22528, 512)
        nSK = area(R0 + 23040, 1024, 2, 512)
        ST = area(R0 + 24064, 256, CT, HD)
        osb, ocen, osq = area(R0 + 16384, 1024, CT, T), area(R0 + 17408, 1024, CT, T), area(R0 + 18432, 1024, CT, T)
        coef = area(0, P * T, P, T)
        qT = area(16384, 4096, 16, T)
        subk = area(20480, 2048, 16, P)
        S = area(22528, 4096, 2, 16, P)
        tv = area(26624, 512, 2, 256)
        ti = area(27136, 512, 2, 256).bitcast(U32)
        tif = area(27648, 512, 2, 256)
        cand = area(28160, 2048, HEADS, 256)
        eqt = area(30208, 2048, P, TOPK)
        bp = area(32256, 128).bitcast(U32)
        bpa = area(32384, 128).bitcast(U32)
        bpf = area(32512, 128)
        bvs = area(16384, 256, 2, P)
        i1s = area(16640, 256, 2, P)
        i2s = area(16896, 256, 2, P)

        landed = [sem(f"unit_landed{j}") for j in range(RAW)]
        hi_made = sem("hi_made")
        lo_dve = sem("lo_made_by_vector")
        lo_pool = sem("lo_made_by_gpsimd")
        unit_done = sem("unit_multiplied")
        act_evac = sem("act_evacuated")
        dve_evac = sem("dve_evacuated")
        dve_step = sem("dve_step")
        pe_step = sem("pe_step")
        act_step = sem("act_step")
        const_in = sem("const_in")
        x_in = sem("x_in")
        xt_ps, xt_sb = sem("xt_ps"), sem("xt_sb")
        sq_made, ss_made, xn_made = sem("sq_made"), sem("ss_made"), sem("xn_made")
        inv_made, root_made = sem("inverse_made"), sem("root_made")
        kk_root, gn_inv, gn_root = sem("kk_root"), sem("gn_inverse"), sem("gn_root")
        lora_in = sem("lora_in")
        rows_ps, rows_sb, rows_out, bias_in = sem("rows_ps"), sem("rows_sb"), sem("rows_out"), sem("bias_in")
        vA_ps, vA_sb = sem("vA_ps"), sem("vA_sb")
        sc_ps, sc_sb, sc_max, sc_exp, p_made = sem("sc_ps"), sem("sc_sb"), sem("sc_max"), sem("sc_exp"), sem("p_made")
        pt_ps, pt_sb, oa_ps, oa_made = sem("pt_ps"), sem("pt_sb"), sem("oa_ps"), sem("oa_made")
        mix_made, lor_act, lor_ps, lor_sb, lor_g = (sem("mix_made"), sem("lora_act"), sem("lora_ps"), sem("lora_sb"),
                                                    sem("lora_g_sb"))
        mid_made, e_made, kk_sq, kk_ss = sem("mid_made"), sem("e_made"), sem("kk_sq"), sem("kk_ss")
        rkv_made, bon_ps, tok_ps, tok_sb = sem("rkv_made"), sem("bonus_ps"), sem("tok_ps"), sem("tok_sb")
        bon_made = sem("bonus_made")
        mat_ps, mat_sb, m1_ps, m1_sb = sem("mat_ps"), sem("mat_sb"), sem("m1_ps"), sem("m1_sb")
        p1_ps, p1_sb, x_ps, x_sb = sem("p1_ps"), sem("p1_sb"), sem("x_ps"), sem("x_sb")
        g_ps, g_sb, sk_ps, sk_sb, st_ps, st_sb = (sem("g_ps"), sem("g_sb"), sem("sk_ps"), sem("sk_sb"), sem("st_ps"),
                                                  sem("st_sb"))
        o_ps, o_sb, mu_ps, cen_sb, var_ps, ob_made = (sem("o_ps"), sem("o_sb"), sem("mu_ps"), sem("cen_sb"),
                                                      sem("var_ps"), sem("ob_made"))
        y_made, h_made = sem("y_made"), sem("h_made")
        subk_in, score_ps, score_sb = sem("subk_in"), sem("score_ps"), sem("score_sb")
        shift_made, exp_made, picks_made, picks_ps, picks_sb = (sem("shift_made"), sem("exp_made"), sem("picks_made"),
                                                                sem("picks_ps"), sem("picks_sb"))
        hot_made, hot_ps, hot_dve, hot_act = sem("hot_made"), sem("hot_ps"), sem("hot_dve"), sem("hot_act")
        ge_made, coef_made, acc_open = sem("gelu_made"), sem("coef_made"), sem("acc_open")
        gh_made, gl_made, acc_done = sem("gh_made"), sem("gl_made"), sem("acc_done")
        zero_made = sem("zero_made")
        fin_ps, fin_sb, stored = sem("fin_ps"), sem("fin_sb"), sem("stored")

        U_IN, U_PROJ, U_OUT, U_Q, U_U, U_V = 0, 44, 52, 60, 76, 204
        U_END = 332

        block = ctx.enter_context(nc.Block())

        @block.sync
        def _(sp):
            def load(src, j, landed_after=None):
                sp.dma_start(raw[:, j, :], src).then_inc(landed[j], 16)

            sp.dma_start(xin, x.rearrange("(n p) d -> p n d", p=P)).then_inc(x_in, 16)
            sp.dma_start(con[:], consts).then_inc(const_in, 16)
            sp.dma_start(vec[:], vecs).then_inc(const_in, 16)
            for j in range(RAW):
                load(w_in[j], j)
            with sp.Fori(1, U_PROJ // 4) as i:
                for j in range(RAW):
                    sp.wait_ge(lo_dve, 4 * i + (j - 3))
                    load(w_in[4 * i + j], j)
                    if j == 0:
                        pass
            for dst, src in ((lwa, lora_wa), (lg0, lora_g[0:P]), (lg1[0:GLORA - P], lora_g[P:GLORA]),
                             (bonehot[0:33], bucket_onehot), (relb[0:32, 0:8], rel_bias_t)):
                sp.dma_start(dst, src).then_inc(lora_in, 16)
            for g in range(U_PROJ, U_OUT):
                sp.wait_ge(lo_dve, g - 3)
                load(w_proj[g - U_PROJ], g % 4)
                if g == U_PROJ + 1:
                    sp.wait_ge(rows_sb, 1)
                    sp.dma_start(bias_dram, rowsb[0:HEADS, :].unsqueeze(1).to_broadcast([HEADS, P, 512])
                                 ).then_inc(rows_out, 16)
                    sp.wait_ge(rows_out, 16)
                    for qt, k0, nk in ((0, 0, P), (1, P, T)):
                        src = bass.AP(bias_dram.tensor, T - 1 - qt * P, [[511, P], [512 * P, HEADS], [1, nk]])
                        sp.dma_start(biasT[:, :, k0:k0 + nk], src).then_inc(bias_in, 16)
            for g in range(U_OUT, U_Q):
                sp.wait_ge(lo_dve, g - 3)
                load(w_out[g - U_OUT], g % 4)
            with sp.Fori(0, 4) as i:
                for j in range(RAW):
                    sp.wait_ge(lo_dve, 4 * i + (U_Q + j - 3))
                    load(w_q[4 * i + j], j)
            for j in range(RAW):
                sp.wait_ge(lo_dve, U_U + j - 3)
                load(u_t[j], j)
            sp.wait_ge(h_made, 8)
            sp.dma_start(subk, subkeys_t).then_inc(subk_in, 16)
            with sp.Fori(1, 32) as i:
                for j in range(RAW):
                    sp.wait_ge(lo_pool, 4 * i + (j - 3))
                    load(u_t[4 * i + j], j)
            for j in range(RAW):
                sp.wait_ge(lo_pool, 128 + j - 3)
                load(v_t[j], j)
            with sp.Fori(1, 32) as i:
                for j in range(RAW):
                    sp.wait_ge(lo_dve, 4 * i + (U_U + j - 3))
                    load(v_t[4 * i + j], j)
            for n in range(4):
                sp.wait_ge(fin_sb, n + 1)
                sp.dma_start(out.rearrange("(n p) d -> n p d", p=P)[n // 2, :, 512 * (n % 2):512 * (n % 2) + 512],
                             xin[:, n // 2, 512 * (n % 2):512 * (n % 2) + 512]).then_inc(stored, 16)
            sp.wait_ge(stored, 64)

        @block.tensor
        def _(pe):
            mm = nc.tensor.matmul

            def splits_ready(g, lo_sem, lo_count):
                pe.wait_ge(hi_made, g + 1)
                pe.wait_ge(lo_sem, lo_count)

            def product(ps, s, mh, ml, k0=0, k1=KT):
                for k in range(k0, k1):
                    c = slice(P * k, P * k + P)
                    mm(ps, hi[:, s, c], mh[:, k, :], start=(k == k0), stop=False)
                    mm(ps, hi[:, s, c], ml[:, k, :], start=False, stop=False)
                    last = mm(ps, lo[:, s, c], mh[:, k, :], start=False, stop=(k == k1 - 1))
                return last

            def sum_of_squares(n):
                pe.wait_ge(sq_made, n + 1)
                for k in range(KT):
                    last = mm(PS[:, 2, 0:T], ones, sq[:, k, :], start=(k == 0), stop=(k == KT - 1))
                last.then_inc(ss_made, 1)

            pe.sem_inc(unit_done, SPLIT)
            pe.sem_inc(act_evac, 2)
            pe.sem_inc(hot_ps, 2)
            pe.wait_ge(x_in, 16)
            pe.wait_ge(const_in, 32)
            for b in range(4):
                for c in range(4):
                    k, n = 2 * b + c // 2, c % 2
                    last = nc.tensor.transpose(PS[:, 4 + b, P * c:P * c + P], xin[:, n, P * k:P * k + P], ident)
                last.then_inc(xt_ps, 1)
            sum_of_squares(0)
            pe.wait_ge(xn_made, 1)
            with pe.Fori(0, U_PROJ // 4) as i:
                for j in range(4):
                    splits_ready(4 * i + j, lo_dve, 4 * i + (j + 1))
                    pe.wait_ge(act_evac, 4 * i + (j + 1))
                    product(PS[:, j % 2, 0:T], j % 2, xh, xl).then_inc(unit_done, 1)
            evacs = U_PROJ
            pe.wait_ge(lora_in, 80)
            pe.wait_ge(dve_step, REL_ROW)
            mm(PS[0:8, 2, :], relb[0:33, 0:8], bonehot[0:33, :], start=True, stop=True).then_inc(rows_ps, 1)
            pe.wait_ge(act_evac, 2 + evacs)
            for n in range(NT):
                for c in range(CT):
                    last = nc.tensor.transpose(PS[:, 3 + n, P * c:P * c + P], pT[:, 8 + c, P * n:P * n + P], ident)
                last.then_inc(vA_ps, 1)
            for h in range(HEADS):
                b, c = HD * (h % 2), h // 2
                bank = [0, 1, 5, 6][h % 4]
                if h >= 4:
                    pe.wait_ge(sc_sb, h - 3)
                mm(PS[:, bank, 0:P], pT[b:b + HD, c, 0:P], pT[b:b + HD, 4 + c, 0:P], start=True, stop=True)
                mm(PS[:, bank, P:P + T], pT[b:b + HD, c, P:T], pT[b:b + HD, 4 + c, :], start=True,
                   stop=True).then_inc(sc_ps, 1)
            pe.wait_ge(p_made, 2)
            for h in range(HEADS):
                bank = [0, 1, 5, 6][h % 4]
                if h < 4:
                    pe.wait_ge(sc_sb, HEADS)
                else:
                    pe.wait_ge(pt_sb, h - 3)
                for n in range(3):
                    last = nc.tensor.transpose(PS[:, bank, P * n:P * n + P], Sb[:, h, P * n:P * n + P], ident)
                last.then_inc(pt_ps, 1)
            pe.wait_ge(vA_sb, 2)
            for h in range(HEADS):
                b, c = HD * (h % 2), h // 2
                pe.wait_ge(pt_sb, h + 1)
                o = PS[b:b + HD, 3 + c // 2, T * (c % 2):T * (c % 2) + T]
                mm(o, vtokA[:, 0, HD * h:HD * h + HD], PTs[:, h, 0:T], start=True, stop=False)
                last = mm(o[:, P:T], vtokA[:, 1, HD * h:HD * h + HD], PTs[:, h, T:T + P], start=False, stop=True)
                if h % 4 == 3:
                    last.then_inc(oa_ps, 1)
            pe.wait_ge(lor_act, 3)
            for c in range(CT):
                col = slice(P * c, P * c + P)
                if c:
                    pe.wait_ge(lor_sb, 2 * c)
                    pe.wait_ge(lor_g, c)
                else:
                    pe.wait_ge(pt_sb, HEADS)
                mm(PS[:, 0, 0:T], lwa[0:LORA, col], mix[0:LORA, 12, :], start=True, stop=True)
                mm(PS[:, 1, 0:T], lwa[LORA:P, col], mix[LORA:P, 12, :], start=True, stop=True)
                mm(PS[:, 5, 0:T], lg0[:, col], mix[:, 13, :], start=True, stop=False)
                mm(PS[:, 5, 0:T], lg1[0:32, col], mix[0:32, 14, :], start=False, stop=True).then_inc(lor_ps, 1)
            pe.wait_ge(kk_sq, 1)
            pe.wait_ge(oa_made, 2)
            for c in range(CT):
                last = mm(PS[:, 3 + c // 2, T * (c % 2):T * (c % 2) + T], blk, tmp[:, c, :], start=True, stop=True)
            last.then_inc(kk_ss, 1)
            pe.wait_ge(rkv_made, 1)
            for c in range(CT):
                last = mm(PS[:, 6 + c // 2, T * (c % 2):T * (c % 2) + T], blk, lw[:, c, :], start=True, stop=True)
            last.then_inc(bon_ps, 1)
            pe.wait_ge(rkv_made, 2)
            pe.wait_ge(lor_sb, 2 * CT)
            for bank, src, n in ((0, vB, 0), (1, vB, 1), (3, kh, 0), (4, bh, 0)):
                for c in range(CT):
                    last = nc.tensor.transpose(PS[:, bank, P * c:P * c + P], src[:, c, P * n:P * n + P], ident)
                last.then_inc(tok_ps, 1)
            pe.wait_ge(tok_sb, 4)
            pe.wait_ge(bon_made, 1)
            pe.wait_ge(lor_g, CT)
            for m in range(16):
                n, b, c = chunk_head(m)
                t = slice(P * n, P * n + P)
                if m >= 4:
                    pe.wait_ge(mat_sb, m - 3)
                mm(PS[:, m % 4, 0:T], kh[b:b + HD, c, t], KR[b:b + HD, c, :, t], start=True, stop=True)
                mm(PS[:, m % 4, T:2 * T], bh[b:b + HD, c, t], KR[b:b + HD, c, :, t], start=True,
                   stop=True).then_inc(mat_ps, 1)
            for m in range(16):
                n, b, c = chunk_head(m)
                t = slice(P * n, P * n + P)
                last = mm(PS[:, 4 + m // 4, P * (m % 4):P * (m % 4) + P], KR[b:b + HD, c, 0, t], bh[b:b + HD, c, t],
                          start=True, stop=True)
                if m % 4 == 3:
                    last.then_inc(m1_ps, 1)
            for lv in range(len(LEVELS)):
                for q in range(4):
                    if lv == 0:
                        pe.wait_ge(mat_sb, 16)
                        pe.wait_ge(m1_sb, 4)
                    else:
                        pe.wait_ge(x_sb, 4 * (lv - 1) + q + 1)
                    for m in range(4 * q, 4 * q + 4):
                        last = mm(PS[:, q, P * (m % 4):P * (m % 4) + P], mats[:, m, 2, :], X[:, m, :], start=True,
                                  stop=True)
                    last.then_inc(p1_ps, 1)
                for q in range(4):
                    pe.wait_ge(p1_sb, 4 * lv + q + 1)
                    if 4 * lv + q >= 2:
                        pe.wait_ge(x_sb, 4 * lv + q - 1)
                    for m in range(4 * q, 4 * q + 4):
                        last = mm(PS[:, 4 + 2 * (q % 2), P * (m % 4):P * (m % 4) + P], P1[:, m, :], XT[:, m, :],
                                  start=True, stop=True)
                    if lv < len(LEVELS) - 1:
                        for m in range(4 * q, 4 * q + 4):
                            last = mm(PS[:, 5 + 2 * (q % 2), P * (m % 4):P * (m % 4) + P], XT[:, m, :], P1[:, m, :],
                                      start=True, stop=True)
                    last.then_inc(x_ps, 1)
            pe.wait_ge(x_sb, 4 * len(LEVELS))
            for n in range(NT):
                if n:
                    pe.wait_ge(st_sb, 1)
                for m in range(8 * n, 8 * n + 8):
                    _, b, c = chunk_head(m)
                    o = PS[:, 2 * (b // HD), HD * c:HD * c + HD]
                    hs = slice(P * c + b, P * c + b + HD)
                    last = mm(o, mats[:, m, 0, :], vtok[:, n, hs], start=True, stop=(n == 0))
                    if n:
                        last = mm(o, KR[b:b + HD, c, 0, P:T], ST[b:b + HD, c, :], start=False, stop=True)
                last.then_inc(g_ps, 1)
                pe.wait_ge(g_sb, n + 1)
                for m in range(8):
                    last = mm(PS[:, 1, HD * m:HD * m + HD], XT[:, 8 * n + m, :], Gs[:, HD * m:HD * m + HD],
                              start=True, stop=True)
                last.then_inc(sk_ps, 1)
                pe.wait_ge(sk_sb, n + 1)
                if n == 0:
                    for m in range(8):
                        _, b, c = chunk_head(m)
                        hs = slice(P * c + b, P * c + b + HD)
                        o = PS[b:b + HD, 3, HD * c:HD * c + HD]
                        mm(o, tokk[:, hs], vtok[:, 0, hs], start=True, stop=False)
                        last = mm(o, tokb[:, hs], nSK[:, 0, HD * m:HD * m + HD], start=False, stop=True)
                    last.then_inc(st_ps, 1)
            for h in range(8):
                for n in range(NT):
                    m = 8 * n + h
                    _, b, c = chunk_head(m)
                    hs = slice(P * c + b, P * c + b + HD)
                    o = PS[b:b + HD, 3 + c // 2, T * (c % 2) + P * n:T * (c % 2) + P * n + P]
                    mm(o, vtok[:, n, hs], mats[:, m, 1, :], start=True, stop=False)
                    last = mm(o, nSK[:, n, HD * h:HD * h + HD], mats[:, m, 3, :], start=False, stop=(n == 0))
                    if n:
                        last = mm(o, ST[b:b + HD, c, :], KR[b:b + HD, c, 1, P:T], start=False, stop=True)
            last.then_inc(o_ps, 1)
            pe.wait_ge(o_sb, 1)
            for c in range(CT):
                last = mm(PS[:, 5 + c // 2, T * (c % 2):T * (c % 2) + T], blk, osb[:, c, :], start=True, stop=True)
            last.then_inc(mu_ps, 1)
            pe.wait_ge(cen_sb, 1)
            for c in range(CT):
                last = mm(PS[:, 3 + c // 2, T * (c % 2):T * (c % 2) + T], blk, osq[:, c, :], start=True, stop=True)
            last.then_inc(var_ps, 1)
            pe.wait_ge(ob_made, 1)
            for g in range(U_PROJ, U_OUT):
                splits_ready(g, lo_dve, g + 1)
                if g >= U_PROJ + 2:
                    pe.wait_ge(dve_evac, g - U_PROJ - 1)
                product(PS[:, g % 2, 0:T], g % 2, oh, ol, 0, 4)
                product(PS[:, g % 2, T:2 * T], g % 2, oh, ol, 4, 8).then_inc(unit_done, 1)
            pe.wait_ge(y_made, 8)
            for g in range(U_OUT, U_Q):
                splits_ready(g, lo_dve, g + 1)
                if g >= U_OUT + 2:
                    pe.wait_ge(h_made, g - U_OUT - 1)
                product(PS[:, g % 2, 0:T], g % 2, xh, xl).then_inc(unit_done, 1)
            sum_of_squares(1)
            pe.wait_ge(xn_made, 2)
            with pe.Fori(0, 4) as i:
                for j in range(4):
                    splits_ready(4 * i + (U_Q + j), lo_dve, 4 * i + (U_Q + j + 1))
                    pe.wait_ge(act_evac, 4 * i + (evacs + j + 1))
                    product(PS[:, j % 2, 0:T], j % 2, xh, xl).then_inc(unit_done, 1)
            evacs += 16
            pe.wait_ge(act_evac, evacs + 2)
            pe.wait_ge(subk_in, 16)
            for m in range(8):
                n, q = m // 4, m % 4
                if m >= 4:
                    pe.wait_ge(score_sb, m - 3)
                for u in range(4 * q, 4 * q + 4):
                    last = mm(PS[:, 4 + m % 4, P * (u % 4):P * (u % 4) + P], qT[:, u, P * n:P * n + P], subk[:, u, :],
                              start=True, stop=True)
                last.then_inc(score_ps, 1)
            with pe.Fori(0, HALF // 4) as i:
                for j in range(4):
                    splits_ready(4 * i + (U_U + j), lo_pool, 4 * i + (j + 1))
                    pe.wait_ge(act_evac, 4 * i + (evacs + j + 1))
                    product(PS[:, j % 2, 0:T], j % 2, xh, xl).then_inc(unit_done, 1)
            evacs += HALF
            pe.wait_ge(picks_made, 1)
            pe.wait_ge(score_sb, 8)
            for b, src in ((2, i1s), (3, i2s), (4, bvs)):
                for n in range(NT):
                    last = nc.tensor.transpose(PS[:, b, P * n:P * n + P], src[:, n, :], ident)
                last.then_inc(picks_ps, 1)
            pe.wait_ge(picks_sb, 3)
            with pe.Fori(0, T // 8) as i:
                for f in range(2):
                    pe.wait_ge(hot_made, 2 * i + (f + 1))
                    pe.wait_ge(hot_dve, 2 * i + (f + 1))
                    pe.wait_ge(hot_act, 2 * i + (f + 1))
                    for k in range(4):
                        mm(PS[:, 5 + f, HALF * k:HALF * k + HALF], oh1[:, f, k, :], oh2[:, f, k, 0:HALF], start=True,
                           stop=True)
                        last = mm(PS[:, 2 + f, HALF * k:HALF * k + HALF], oh1[:, f, k, :], oh2[:, f, k, HALF:],
                                  start=True, stop=True)
                    last.then_inc(hot_ps, 1)
            with pe.Fori(0, HALF // 4) as i:
                for j in range(4):
                    splits_ready(4 * i + (U_U + HALF + j), lo_pool, 4 * i + (HALF + j + 1))
                    pe.wait_ge(act_evac, 4 * i + (evacs + j + 1))
                    product(PS[:, j % 2, 0:T], j % 2, xh, xl).then_inc(unit_done, 1)
            evacs += HALF
            pe.wait_ge(act_evac, evacs + 2)
            pe.wait_ge(zero_made, 1)
            for b in range(4):
                mm(PS[:, b, :], zeros[:, 0:P], zeros, start=True, stop=False, skip_group_check=True)
            with pe.Fori(0, NKEYS // 4) as i:
                for j in range(4):
                    splits_ready(4 * i + (U_V + j), lo_dve, 4 * i + (U_U + j + 1))
                    pe.wait_ge(gh_made, 4 * i + (j + 1))
                    pe.wait_ge(gl_made, 4 * i + (j + 1))
                    s = j % 2
                    for k in range(KT):
                        o = PS[:, k // 2, T * (k % 2):T * (k % 2) + T]
                        c = slice(P * k, P * k + P)
                        mm(o, hi[:, s, c], gh[:, s, :], start=False, stop=False, skip_group_check=True)
                        mm(o, hi[:, s, c], gl[:, s, :], start=False, stop=False, skip_group_check=True)
                        last = mm(o, lo[:, s, c], gh[:, s, :], start=False, stop=False, skip_group_check=True)
                    last.then_inc(unit_done, 1)
            for b in range(4):
                mm(PS[:, b, :], zeros[:, 0:P], zeros, start=False, stop=True,
                   skip_group_check=True).then_inc(acc_done, 1)
            pe.wait_ge(h_made, 12)
            sum_of_squares(2)
            pe.wait_ge(xn_made, 3)
            for m in range(4):
                for k in range(4):
                    last = nc.tensor.transpose(PS[:, 4 + m, P * k:P * k + P],
                                               xn[:, 4 * (m % 2) + k, P * (m // 2):P * (m // 2) + P], ident)
                last.then_inc(fin_ps, 1)

        @block.scalar
        def _(act):
            def make_hi(G, j):
                act.wait_ge(landed[j], 16 * G + 16)
                act.wait_ge(unit_done, 4 * G + (j + 1))
                nc.scalar.activation(hi[:, j % 2, :], raw[:, j, :], ACT.Copy).then_inc(hi_made, 1)

            def next_hi(G, j):
                make_hi(G if j < 3 else G + 1, (j + 1) % 4)

            def squares(n):
                act.wait_ge([xt_sb, h_made, h_made][n], [4, 8, 12][n])
                nc.scalar.activation(sq, xT[:], ACT.Square).then_inc(sq_made, 1)
                act.wait_ge(inv_made, n + 1)
                nc.scalar.activation(rstd, rstd, ACT.Sqrt).then_inc(root_made, 1)

            make_hi(0, 0)
            squares(0)
            with act.Fori(0, NB_IN // 4) as i:
                for j in range(4):
                    next_hi(i, j)
                    act.wait_ge(unit_done, 4 * i + (j + 3))
                    nc.scalar.activation(pT[:, 4 * i + j, :], PS[:, j % 2, 0:T], ACT.Copy).then_inc(act_evac, 1)
            with act.Fori(0, NB_GATE // 4) as i:
                for j in range(4):
                    next_hi(i + NB_IN // 4, j)
                    act.wait_ge(unit_done, 4 * i + (NB_IN + j + 3))
                    nc.scalar.activation(gates[:, 4 * i + j, :], PS[:, j % 2, 0:T], ACT.Sigmoid).then_inc(act_evac, 1)
            act.wait_ge(rows_ps, 1)
            nc.scalar.copy(rowsb[0:HEADS, :], PS[0:HEADS, 2, :]).then_inc(rows_sb, 1)
            for n in range(NT):
                act.wait_ge(vA_ps, n + 1)
                nc.scalar.copy(vtokA[:, n, :], PS[:, 3 + n, :]).then_inc(vA_sb, 1)
            act.wait_ge(mix_made, 1)
            nc.scalar.activation(mix[0:LORA, 12, :], mix[0:LORA, 12, :], ACT.Tanh).then_inc(lor_act, 1)
            nc.scalar.activation(mix[:, 13, :], mix[:, 13, :], ACT.Sigmoid).then_inc(lor_act, 1)
            nc.scalar.activation(mix[0:32, 14, :], mix[0:32, 14, :], ACT.Sigmoid).then_inc(lor_act, 1)
            act.wait_ge(sc_max, 2)
            for h in range(HEADS):
                for n, a, b in ((0, 0, P), (1, P, P + T)):
                    nc.scalar.activation(Sb[:, h, a:b], Sb[:, h, a:b], ACT.Exp, bias=small[:, 8 * n + h:8 * n + h + 1],
                                         accum_out=small[:, 16 + 8 * n + h:17 + 8 * n + h]).then_inc(sc_exp, 1)
            for h in range(HEADS):
                act.wait_ge(pt_ps, h + 1)
                nc.scalar.copy(PTs[:, h, :], PS[:, [0, 1, 5, 6][h % 4], 0:384]).then_inc(pt_sb, 1)
            act.wait_ge(oa_made, 2)
            for c in range(CT):
                act.wait_ge(lor_ps, c + 1)
                nc.scalar.activation(lw[:, c, :], PS[:, 0, 0:T], ACT.Sigmoid,
                                     bias=vec[:, V_W0 + c:V_W0 + c + 1]).then_inc(lor_sb, 1)
                nc.scalar.activation(aB[:, c, :], PS[:, 1, 0:T], ACT.Sigmoid,
                                     bias=vec[:, V_A0 + c:V_A0 + c + 1]).then_inc(lor_sb, 1)
                nc.scalar.copy(gB[:, c, :], PS[:, 5, 0:T]).then_inc(lor_g, 1)
            act.wait_ge(kk_ss, 1)
            nc.scalar.activation(tmp.rearrange("p a b -> p (a b)"), PS[:, 3:5, :].rearrange("p a b -> p (a b)"),
                                 ACT.Sqrt).then_inc(kk_root, 1)
            act.wait_ge(mid_made, 1)
            for c in range(CT):
                for n in range(NT):
                    m = 32 + 2 * c + n
                    nc.scalar.activation(E[:, c, n, :], Lz[:, c, P * n:P * n + P + 1], ACT.Exp,
                                         bias=small[:, m:m + 1]).then_inc(e_made, 1)
                    nc.scalar.activation(EI[:, c, P * n:P * n + P], Lz[:, c, P * n + 1:P * n + P + 1], ACT.Exp,
                                         bias=small[:, m + 8:m + 9], scale=-1.0).then_inc(e_made, 1)
            nc.scalar.activation(small[:, 48:52], small[:, 52:56], ACT.Exp).then_inc(e_made, 1)
            for n, dst in enumerate((vtok[:, 0, :], vtok[:, 1, :], tokk, tokb)):
                act.wait_ge(tok_ps, n + 1)
                nc.scalar.copy(dst, PS[:, (0, 1, 3, 4)[n], :]).then_inc(tok_sb, 1)
            act.wait_ge(gn_inv, 1)
            nc.scalar.activation(osb, osb, ACT.Sqrt).then_inc(gn_root, 1)
            for g in range(U_PROJ, U_Q):
                next_hi(g // 4, g % 4)
            squares(1)
            with act.Fori(0, 4) as i:
                for j in range(4):
                    next_hi(i + U_Q // 4, j)
                    act.wait_ge(unit_done, 4 * i + (U_Q + j + 3))
                    nc.scalar.activation(qT[:, 4 * i + j, :], PS[:, j % 2, 0:T], ACT.Copy).then_inc(act_evac, 1)
            for m in range(8):
                act.wait_ge(score_ps, m + 1)
                nc.scalar.copy(S[:, m // 4, 4 * (m % 4):4 * (m % 4) + 4, :].rearrange("p a b -> p (a b)"),
                               PS[:, 4 + m % 4, :]).then_inc(score_sb, 1)
            with act.Fori(0, HALF // 4) as i:
                for j in range(4):
                    next_hi(i + U_U // 4, j)
                    act.wait_ge(unit_done, 4 * i + (U_U + j + 3))
                    nc.scalar.activation(coef[:, 4 * i + j, :], PS[:, j % 2, 0:T], ACT.Gelu).then_inc(act_evac, 1)
            act.wait_ge(shift_made, 2)
            nc.scalar.activation(bvs, bvs, ACT.Exp).then_inc(exp_made, 1)
            act.wait_ge(picks_ps, 3)
            act.sem_inc(hot_act, 2)
            with act.Fori(0, T // 8) as i:
                for f in range(2):
                    act.wait_ge(hot_ps, 2 * i + (f + 3))
                    nc.scalar.copy(coef[:, HALF:, bass.ds(8 * i + 4 * f, 4)],
                                   PS[:, 2 + f, 0:4 * HALF].rearrange("p (t k) -> p k t", t=4)).then_inc(hot_act, 1)
            with act.Fori(0, HALF // 4) as i:
                for j in range(4):
                    next_hi(i + (U_U + HALF) // 4, j)
                    act.wait_ge(unit_done, 4 * i + (U_U + HALF + j + 3))
                    act.wait_ge(coef_made, 4 * i + (j + 1))
                    nc.scalar.activation(oh1[:, j % 2, 0:2, :].rearrange("p a b -> p (a b)"), PS[:, j % 2, 0:T],
                                         ACT.Gelu).then_inc(act_evac, 1)

            def v_unit(i, j, last=False):
                act.wait_ge(unit_done, 4 * i + (U_V + j + 1))
                nc.scalar.activation(gh[:, j % 2, :], coef[:, 4 * i + j, :], ACT.Copy).then_inc(gh_made, 1)
                if not last:
                    next_hi(i + U_V // 4, j)

            act.wait_ge(coef_made, HALF + 2)
            with act.Fori(0, NKEYS // 4 - 1) as i:
                for j in range(4):
                    v_unit(i, j)
            for j in range(4):
                v_unit(NKEYS // 4 - 1, j, j == 3)
            squares(2)

        @block.gpsimd
        def _(pool):
            with pool.Fori(0, NKEYS // 4) as i:
                for j in range(4):
                    pool.wait_ge(hi_made, 4 * i + (U_U + j + 1))
                    nc.gpsimd.tensor_tensor(lo[:, j % 2, :], raw[:, j, :], hi[:, j % 2, :].bitcast(F32),
                                            ALU.subtract).then_inc(lo_pool, 1)

        @block.vector
        def _(dve):
            steps = [0]

            def link(ins):
                steps[0] += 1
                ins.then_inc(dve_step, 1)
                dve.wait_ge(dve_step, steps[0])

            V = nc.vector

            def make_lo(g, j):
                dve.wait_ge(hi_made, g)
                V.tensor_tensor(lo[:, j % 2, :], raw[:, j, :], hi[:, j % 2, :].bitcast(F32),
                                ALU.subtract).then_inc(lo_dve, 1)

            def per_channel(a):
                return vec[:, a:a + 1]

            def rms_scale(n, gain):
                dve.wait_ge(ss_made, n + 1)
                link(V.tensor_scalar(rstd, PS[:, 2, 0:T], 1.0 / D, RMS_EPS, ALU.mult, ALU.add))
                V.reciprocal(rstd, rstd).then_inc(inv_made, 1)
                dve.wait_ge(root_made, n + 1)
                for k in range(KT):
                    last = V.scalar_tensor_tensor(out=xn[:, k, :], in0=xT[:, k, :], scalar=per_channel(gain + k),
                                                  in1=rstd, op0=ALU.mult, op1=ALU.mult)
                if n == 2:
                    last.then_inc(xn_made, 1)
                    return
                link(last)
                link(V.tensor_copy(xh[:], xn))
                V.tensor_tensor(xl[:], xn, xh[:].bitcast(F32), ALU.subtract).then_inc(xn_made, 1)

            V.memset(relb[0:64, :], NEG).then_inc(dve_step, 1)
            steps[0] += 1
            for b in range(4):
                dve.wait_ge(xt_ps, b + 1)
                V.tensor_copy(xT[:, 2 * b:2 * b + 2, :], PS[:, 4 + b, :].rearrange("p (a b) -> p a b", a=2)
                              ).then_inc(xt_sb, 1)
            dve.wait_ge(xt_sb, 4)
            rms_scale(0, V_N1)
            with dve.Fori(0, U_PROJ // 4) as i:
                for j in range(4):
                    make_lo(4 * i + (j + 1), j)
            make_lo(U_PROJ + 1, 0)

            dve.wait_ge(act_evac, 2 + U_PROJ)
            dve.wait_ge(bias_in, 32)
            for h in range(HEADS):
                dve.wait_ge(sc_ps, h + 1)
                V.scalar_tensor_tensor(out=Sb[:, h, :], in0=PS[:, [0, 1, 5, 6][h % 4], 0:384], scalar=HD ** -0.5,
                                       in1=biasT[:, h, :], op0=ALU.mult, op1=ALU.add).then_inc(sc_sb, 1)
            dve.wait_ge(sc_sb, HEADS)
            V.tensor_reduce(small[:, 0:8], Sb[:, :, 0:P], AX_X, ALU.max, negate=True).then_inc(sc_max, 1)
            V.tensor_reduce(small[:, 8:16], Sb[:, :, P:P + T], AX_X, ALU.max, negate=True).then_inc(sc_max, 1)
            m15 = pT[:, 12:12 + NMIX, :]
            V.tensor_tensor(mix[:, :, 1:T], m15[:, :, 0:T - 1], m15[:, :, 1:T], ALU.subtract)
            link(V.tensor_scalar(mix[:, :, 0:1], m15[:, :, 0:1], -1.0, None, ALU.mult))
            for c in range(NMIX):
                last = V.scalar_tensor_tensor(out=mix[:, c, :], in0=mix[:, c, :], scalar=per_channel(V_MU + c),
                                              in1=m15[:, c, :], op0=ALU.mult, op1=ALU.add)
            last.then_inc(mix_made, 1)
            dve.wait_ge(sc_exp, 16)
            link(V.reciprocal(small[:, 16:32], small[:, 16:32]))
            V.tensor_tensor(Sb[:, :, 0:P], Sb[:, :, 0:P], small[:, 16:24].unsqueeze(2).to_broadcast([P, HEADS, P]),
                            ALU.mult).then_inc(p_made, 1)
            V.tensor_tensor(Sb[:, :, P:P + T], Sb[:, :, P:P + T],
                            small[:, 24:32].unsqueeze(2).to_broadcast([P, HEADS, T]), ALU.mult).then_inc(p_made, 1)

            def split_out(dst0, src):
                link(V.tensor_copy(oh[:, dst0[0]:dst0[1], :], src))
                return V.tensor_tensor(ol[:, dst0[0]:dst0[1], :], src, oh[:, dst0[0]:dst0[1], :].bitcast(F32),
                                       ALU.subtract)
            for b in range(2):
                dve.wait_ge(oa_ps, b + 1)
                split_out((2 * b, 2 * b + 2), PS[:, 3 + b, :].rearrange("p (a b) -> p a b", a=2)).then_inc(oa_made, 1)

            dve.wait_ge(mix_made, 1)
            dve.wait_ge(rows_sb, 1)
            for c in range(CT):
                last = V.tensor_scalar(kk[:, c, :], kB[:, c, :], per_channel(V_KK + c), None, ALU.mult)
            link(last)
            V.tensor_tensor(tmp, kk, kk, ALU.mult).then_inc(kk_sq, 1)
            dve.wait_ge(lor_sb, 2 * CT)
            link(V.tensor_scalar(lw, lw, -math.exp(-0.5), None, ALU.mult))
            V.memset(E[:, :, :, :], 1.0)
            link(V.memset(Lz[:, :, 0:1], 0.0))
            for c in range(CT):
                last = V.tensor_tensor_scan(Lz[:, c, 1:T + 1], E[:, 0, 0:2, :].rearrange("p a b -> p (a b)")[:, 0:T],
                                            lw[:, c, :], 0.0, ALU.mult, ALU.add)
            link(last)
            mids = Lz[:, :, HD:HD + P + 1:P]
            sm = small[:, 32:40].rearrange("p (c n) -> p c n", n=2)
            V.tensor_scalar(sm, mids, -1.0, None, ALU.mult)
            V.tensor_tensor(small[:, 52:56].unsqueeze(2), mids[:, :, 1:2], mids[:, :, 0:1], ALU.subtract)
            V.tensor_copy(small[:, 40:48].rearrange("p (c n) -> p c n", n=2), mids).then_inc(mid_made, 1)
            dve.wait_ge(kk_root, 1)
            link(V.tensor_scalar(tmp, tmp, 1e-12, None, ALU.max))
            link(V.reciprocal(tmp, tmp))
            link(V.tensor_tensor(kk, kk, tmp, ALU.mult))
            for c in range(CT):
                last = V.tensor_scalar(tmp[:, c, :], aB[:, c, :], 1.0, per_channel(V_KA + c), ALU.subtract, ALU.mult)
            link(last)
            link(V.scalar_tensor_tensor(out=k2, in0=tmp, scalar=1.0, in1=kB, op0=ALU.add, op1=ALU.mult))
            link(V.tensor_tensor(aB, kk, aB, ALU.mult))
            for c in range(CT):
                last = V.scalar_tensor_tensor(out=lw[:, c, :], in0=rB[:, c, :], scalar=per_channel(V_RK + c),
                                              in1=k2[:, c, :], op0=ALU.mult, op1=ALU.mult)
            last.then_inc(rkv_made, 1)
            dve.wait_ge(e_made, 4 * CT + 1)
            V.tensor_tensor(bh, aB, EI, ALU.mult)
            V.tensor_tensor(kh, k2, EI, ALU.mult)
            for n in range(NT):
                t = slice(P * n, P * n + P)
                V.tensor_tensor(KR[:, :, 0, t], kk[:, :, t], E[:, :, n, 0:P], ALU.mult)
                last = V.tensor_tensor(KR[:, :, 1, t], rB[:, :, t], E[:, :, n, 1:P + 1], ALU.mult)
            last.then_inc(rkv_made, 1)
            dve.wait_ge(bon_ps, 1)
            for b in range(2):
                last = V.tensor_tensor(bonus[:, 2 * b:2 * b + 2, :], PS[:, 6 + b, :].rearrange("p (a b) -> p a b", a=2),
                                       vB[:, 2 * b:2 * b + 2, :], ALU.mult)
            last.then_inc(bon_made, 1)
            dve.wait_ge(rkv_made, 2)
            dve.wait_ge(tok_ps, 4)
            for m in range(16):
                dve.wait_ge(mat_ps, m + 1)
                V.tensor_tensor(mats[:, m, :, :].rearrange("p a b -> p (a b)"), PS[:, m % 4, :], mask4,
                                ALU.mult).then_inc(mat_sb, 1)
            id4 = ident.unsqueeze(1).to_broadcast([P, 4, P])

            def bcast4(a):
                return con[:, a:a + P].unsqueeze(1).to_broadcast([P, 4, P])

            def bank4(b):
                return PS[:, b, :].rearrange("p (a b) -> p a b", a=4)
            dve.wait_ge(mat_sb, 16)
            for q in range(4):
                dve.wait_ge(m1_ps, q + 1)
                V.tensor_tensor(X[:, 4 * q:4 * q + 4, :], bank4(4 + q), bcast4(C_NM1), ALU.mult)
                link(V.tensor_tensor(XT[:, 4 * q:4 * q + 4, :], mats[:, 4 * q:4 * q + 4, 2, :], bcast4(C_NM1T), ALU.mult))
                V.tensor_tensor(X[:, 4 * q:4 * q + 4, :], X[:, 4 * q:4 * q + 4, :], id4, ALU.add)
                V.tensor_tensor(XT[:, 4 * q:4 * q + 4, :], XT[:, 4 * q:4 * q + 4, :], id4, ALU.add).then_inc(m1_sb, 1)
            for lv in range(len(LEVELS)):
                for q in range(4):
                    dve.wait_ge(p1_ps, 4 * lv + q + 1)
                    V.tensor_tensor(P1[:, 4 * q:4 * q + 4, :], bank4(q), bcast4(C_LV + P * lv),
                                    ALU.mult).then_inc(p1_sb, 1)
                for q in range(4):
                    dve.wait_ge(x_ps, 4 * lv + q + 1)
                    a = slice(4 * q, 4 * q + 4)
                    if lv < len(LEVELS) - 1:
                        V.tensor_tensor(X[:, a, :], X[:, a, :], bank4(5 + 2 * (q % 2)), ALU.subtract)
                    V.tensor_tensor(XT[:, a, :], XT[:, a, :], bank4(4 + 2 * (q % 2)), ALU.subtract).then_inc(x_sb, 1)
            for n in range(NT):
                dve.wait_ge(g_ps, n + 1)
                V.tensor_copy(Gs.rearrange("p (a b) -> p a b", a=2), PS[:, 0:3:2, 0:T]).then_inc(g_sb, 1)
                dve.wait_ge(sk_ps, n + 1)
                V.tensor_scalar(nSK[:, n, :], PS[:, 1, :], -1.0, None, ALU.mult).then_inc(sk_sb, 1)
                if n == 0:
                    dve.wait_ge(st_ps, 1)
                    V.tensor_tensor(ST, PS[:, 3, 0:CT * HD].rearrange("p (c i) -> p c i", i=HD),
                                    small[:, 48:52].unsqueeze(2).to_broadcast([P, CT, HD]), ALU.mult).then_inc(st_sb, 1)
            dve.wait_ge(x_sb, 4 * len(LEVELS))
            dve.wait_ge(o_ps, 1)
            for b in range(2):
                last = V.tensor_copy(osb[:, 2 * b:2 * b + 2, :], PS[:, 3 + b, :].rearrange("p (a b) -> p a b", a=2))
            last.then_inc(o_sb, 1)
            dve.wait_ge(o_sb, 1)
            dve.wait_ge(mu_ps, 1)
            for b in range(2):
                last = V.scalar_tensor_tensor(out=ocen[:, 2 * b:2 * b + 2, :],
                                              in0=PS[:, 5 + b, :].rearrange("p (a b) -> p a b", a=2), scalar=-1.0 / HD,
                                              in1=osb[:, 2 * b:2 * b + 2, :], op0=ALU.mult, op1=ALU.add)
            link(last)
            V.tensor_tensor(osq, ocen, ocen, ALU.mult).then_inc(cen_sb, 1)
            dve.wait_ge(var_ps, 1)
            for b in range(2):
                last = V.tensor_scalar(osb[:, 2 * b:2 * b + 2, :], PS[:, 3 + b, :].rearrange("p (a b) -> p a b", a=2),
                                       1.0 / HD, GN_EPS, ALU.mult, ALU.add)
            link(last)
            V.reciprocal(osb, osb).then_inc(gn_inv, 1)
            dve.wait_ge(gn_root, 1)
            link(V.tensor_tensor(ocen, ocen, osb, ALU.mult))
            for c in range(CT):
                last = V.tensor_scalar(ocen[:, c, :], ocen[:, c, :], per_channel(V_LG + c), per_channel(V_LB + c),
                                       ALU.mult, ALU.add)
            link(last)
            link(V.tensor_tensor(ocen, ocen, bonus, ALU.add))
            link(V.tensor_tensor(ocen, ocen, gB, ALU.mult))
            split_out((4, 8), ocen).then_inc(ob_made, 1)

            V.memset(zeros, 0.0).then_inc(zero_made, 1)

            ya, yb = xn[:, 0, :], xn[:, 1, :]
            for g in range(U_PROJ, U_OUT):
                make_lo(g + 2, (g + 1) % 4)
                k = g - U_PROJ
                dve.wait_ge(unit_done, g + 3)
                V.tensor_tensor(ya, PS[:, g % 2, 0:T], gates[:, k, :], ALU.mult)
                last = V.tensor_tensor(yb, PS[:, g % 2, T:2 * T], gates[:, KT + k, :], ALU.mult)
                last.then_inc(dve_evac, 1)
                dve.wait_ge(dve_evac, k + 1)
                link(V.tensor_tensor(ya, ya, yb, ALU.add))
                link(V.tensor_copy(xh[:, k, :], ya))
                V.tensor_tensor(xl[:, k, :], ya, xh[:, k, :].bitcast(F32), ALU.subtract).then_inc(y_made, 1)
                dve.wait_ge(y_made, k + 1)
            for g in range(U_OUT, U_Q):
                make_lo(g + 2, (g + 1) % 4)
                k = g - U_OUT
                dve.wait_ge(unit_done, g + 3)
                V.tensor_tensor(xT[:, k, :], xT[:, k, :], PS[:, g % 2, 0:T], ALU.add).then_inc(h_made, 1)
            dve.wait_ge(h_made, 8)
            rms_scale(1, V_N2)
            for j in range(1, 4):
                make_lo(U_Q + j + 1, j)
            with dve.Fori(1, 4) as i:
                for j in range(4):
                    make_lo(4 * i + (U_Q + j + 1), j)

            for n in range(NT):
                dve.wait_ge(score_sb, 8)

                def top16(values, vals, idx):
                    N = len(values)
                    for u in range(N):
                        last = V.max(vals[u][:, 0:8], values[u])
                    link(last)
                    for u in range(N):
                        last = V.max_index(idx[u][:, 0:8], vals[u][:, 0:8], values[u])
                    link(last)
                    for u in range(N):
                        last = V.match_replace(values[u], vals[u][:, 0:8], values[u], LOWEST)
                    link(last)
                    for u in range(N):
                        last = V.max(vals[u][:, 8:16], values[u])
                    link(last)
                    for u in range(N):
                        last = V.max_index(idx[u][:, 8:16], vals[u][:, 8:16], values[u])
                    link(last)

                top16([S[:, n, u, :] for u in range(16)], [tv[:, n, 16 * u:16 * u + 16] for u in range(16)],
                      [ti[:, n, 16 * u:16 * u + 16] for u in range(16)])
                V.tensor_copy(tif[:, n, :], ti[:, n, :])
                tv4 = tv[:, n, :].rearrange("p (h s k) -> p h s k", s=2, k=TOPK)
                ti4 = tif[:, n, :].rearrange("p (h s k) -> p h s k", s=2, k=TOPK)
                cand4 = cand.rearrange("p h (a b) -> p h a b", a=TOPK)
                link(V.tensor_tensor(cand4, tv4[:, :, 0, :].unsqueeze(3).to_broadcast([P, HEADS, TOPK, TOPK]),
                                     tv4[:, :, 1, :].unsqueeze(2).to_broadcast([P, HEADS, TOPK, TOPK]), ALU.add))
                top16([cand[:, h, :] for h in range(HEADS)], [bvs[:, n, 16 * h:16 * h + 16] for h in range(HEADS)],
                      [bp[:, 16 * h:16 * h + 16] for h in range(HEADS)])
                for side, dst in ((0, i1s), (1, i2s)):
                    if side == 0:
                        link(V.tensor_scalar(bpa, bp, 4, None, ALU.logical_shift_right))
                    else:
                        link(V.tensor_scalar(bpa, bp, 15, None, ALU.bitwise_and))
                    link(V.tensor_copy(bpf, bpa))
                    link(V.tensor_tensor(eqt, bpf.unsqueeze(2).to_broadcast([P, P, TOPK]),
                                         iota[:, 0:TOPK].unsqueeze(1).to_broadcast([P, P, TOPK]), ALU.is_equal))
                    e4 = eqt.rearrange("p (h k) j -> p h k j", h=HEADS)
                    link(V.tensor_tensor(e4, e4, ti4[:, :, side, :].unsqueeze(2).to_broadcast([P, HEADS, TOPK, TOPK]),
                                         ALU.mult))
                    link(V.tensor_reduce(dst[:, n, :], eqt, AX_X, ALU.add))
                b3 = bvs[:, n, :].rearrange("p (h k) -> p h k", k=TOPK)
                V.tensor_copy(small[:, 0:8].unsqueeze(2), b3[:, :, 0:1]).then_inc(dve_step, 1)
                steps[0] += 1
                dve.wait_ge(dve_step, steps[0])
                V.tensor_tensor(b3, b3, small[:, 0:8].unsqueeze(2).to_broadcast([P, HEADS, TOPK]),
                                ALU.subtract).then_inc(shift_made, 1)
            dve.wait_ge(exp_made, 1)
            b4 = bvs.rearrange("p n (h k) -> p (n h) k", k=TOPK)
            link(V.tensor_reduce(small[:, 0:16], b4, AX_X, ALU.add))
            link(V.reciprocal(small[:, 16:32], small[:, 0:16]))
            V.tensor_tensor(b4, b4, small[:, 16:32].unsqueeze(2).to_broadcast([P, 16, TOPK]),
                            ALU.mult).then_inc(picks_made, 1)
            for b, dst in ((2, i1T), (3, i2T), (4, gT)):
                dve.wait_ge(picks_ps, b - 1)
                V.tensor_copy(dst[:], PS[:, b, 0:T]).then_inc(picks_sb, 1)
            dve.wait_ge(picks_sb, 3)

            def one_hots(i, f):
                dve.wait_ge(hot_ps, 2 * i + (f + 1))
                for k in range(4):
                    t = 8 * i + (4 * f + k)
                    V.tensor_scalar(oh1[:, f, k, :], iota, i1T[:, bass.ds(t, 1)], gT[:, bass.ds(t, 1)], ALU.is_equal,
                                    ALU.mult)
                    last = V.tensor_scalar(oh2[:, f, k, :], iota, i2T[:, bass.ds(t, 1)], None, ALU.is_equal)
                last.then_inc(hot_made, 1)

            def apply_gates(i, f):
                dve.wait_ge(hot_ps, 2 * i + (f + 3))
                c = coef[:, 0:HALF, bass.ds(8 * i + 4 * f, 4)]
                V.tensor_tensor(c, PS[:, 5 + f, 0:4 * HALF].rearrange("p (t k) -> p k t", t=4), c,
                                ALU.mult).then_inc(hot_dve, 1)

            dve.sem_inc(hot_dve, 2)
            dve.wait_ge(act_evac, 2 + U_PROJ + 16 + HALF)
            one_hots(0, 0)
            one_hots(0, 1)
            with dve.Fori(0, T // 8 - 1) as i:
                for f in range(2):
                    apply_gates(i, f)
                    one_hots(i + 1, f)
            for f in range(2):
                apply_gates(T // 8 - 1, f)
            dve.wait_ge(hot_act, 2 + T // 4)
            dve.sem_inc(coef_made, 2)
            with dve.Fori(0, HALF // 4) as i:
                for j in range(4):
                    dve.wait_ge(act_evac, 4 * i + (U_PROJ + 16 + HALF + j + 3))
                    c = coef[:, 4 * i + (HALF + j), :]
                    V.tensor_tensor(c, c, oh1[:, j % 2, 0:2, :].rearrange("p a b -> p (a b)"), ALU.mult).then_inc(coef_made, 1)
            with dve.Fori(0, NKEYS // 4) as i:
                for j in range(4):
                    dve.wait_ge(gh_made, 4 * i + (j + 1))
                    V.tensor_tensor(gl[:, j % 2, :], coef[:, 4 * i + j, :], gh[:, j % 2, :].bitcast(F32),
                                    ALU.subtract).then_inc(gl_made, 1)
                    make_lo(4 * i + (U_V + j + 1), j)
            for b in range(4):
                dve.wait_ge(acc_done, b + 1)
                V.tensor_tensor(xT[:, 2 * b:2 * b + 2, :], xT[:, 2 * b:2 * b + 2, :],
                                PS[:, b, :].rearrange("p (a b) -> p a b", a=2), ALU.add).then_inc(h_made, 1)
            dve.wait_ge(h_made, 12)
            rms_scale(2, V_NF)
            for m in range(4):
                dve.wait_ge(fin_ps, m + 1)
                V.tensor_copy(xin[:, m // 2, 512 * (m % 2):512 * (m % 2) + 512], PS[:, 4 + m, :]).then_inc(fin_sb, 1)


REL_ROW = 1


def chunk_head(m):
    return m // 8, HD * (m % 8 // 4), m % 4


def shape_constants(np):
    r = np.arange(P)
    c = np.zeros((P, NCONST), np.float32)
    c[:, C_ID:C_ID + P] = np.eye(P)
    c[:, C_ONE:C_ONE + P] = 1
    c[:, C_BLK:C_BLK + P] = r[:, None] // HD == r[None, :] // HD
    c[:, C_IOTA:C_IOTA + P] = r[None, :]
    strict, incl = r[None, :] > r[:, None], r[None, :] >= r[:, None]
    for n, m in enumerate((strict, incl, strict, incl)):
        c[:, C_M4 + P * n:C_M4 + P * n + P] = m

    def lower_left(n):
        t, s = r[:, None], r[None, :]
        return (t // (2 * n) == s // (2 * n)) & (t // n % 2 == 1) & (s // n % 2 == 0)
    c[:, C_NM1:C_NM1 + P] = -1.0 * lower_left(1)
    c[:, C_NM1T:C_NM1T + P] = -1.0 * lower_left(1).T
    for k, n in enumerate(LEVELS):
        c[:, C_LV + P * k:C_LV + P * k + P] = lower_left(n)
    hot = np.zeros((33, 512), np.float32)
    for m in range(512):
        n = T - 1 - m
        if n < 0:
            b = 32
        elif n < 16:
            b = n
        else:
            f = np.float32(np.log(np.float32(n) / np.float32(16))) / np.float32(math.log(128 / 16))
            b = min(16 + int(np.float32(f) * np.float32(16)), 31)
        hot[b, m] = 1
    return c, hot


def kernel(**inputs):
    import numpy as _np
    import concourse.bacc as _bacc
    from concourse import mybir as _mybir
    from concourse.bass_utils import run_bass_kernel_spmd as _run

    i = {k: _np.asarray(v) for k, v in inputs.items()}

    def units(w):
        n = w.shape[1] // P
        return _np.ascontiguousarray(w.reshape(KT, P, n, P).transpose(2, 1, 0, 3)).reshape(n, P, D)

    def cols(a):
        return a.reshape(-1, P).T

    w = i['w_in'][0]
    n_in = 3 * W + 3 * W + 2 * LORA + GLORA
    w_all = _np.zeros((D, (NB_IN + NB_GATE) * P), w.dtype)
    w_all[:, :n_in] = w[:, :n_in]
    w_all[:, NB_IN * P:] = w[:, n_in:]
    mu = _np.zeros((NMIX * P,), w.dtype)
    mu[:n_in - 3 * W] = i['rwkv_mu'][0]
    vecs = _np.concatenate([cols(a) for a in (
        i['norm1_g'][0], i['norm2_g'][0], i['normf_g'], i['w0'][0], i['a0'][0], i['k_k'][0], i['k_a'][0],
        i['r_k'][0].reshape(-1), i['lnx_g'][0], i['lnx_b'][0], mu)], axis=1)
    consts, hot = shape_constants(_np)
    arrays = {
        'x': i['x'][0],
        'w_in_units': units(w_all),
        'w_proj_units': units(_np.concatenate([i['w_proj_a'][0], i['w_proj_b'][0]], axis=0)),
        'w_out_units': units(i['w_out'][0]),
        'w_q_units': units(i['peer_wq'][0]),
        'u_units': i['peer_u'][0].reshape(NKEYS, NKEYS, KT, P).transpose(1, 3, 2, 0).reshape(NKEYS, P, D),
        'v_units': i['peer_v'][0].reshape(NKEYS, NKEYS, D).transpose(1, 0, 2),
        'vecs': vecs,
        'lora_wa': _np.concatenate([i['w_lora_up'][0], i['a_lora_up'][0]], axis=0),
        'lora_g': i['g_lora_up'][0],
        'rel_bias_t': i['rel_bias'].T,
        'bucket_onehot': hot,
        'consts': consts,
        'subkeys_t': i['peer_subkeys'][0].reshape(2 * HEADS, NKEYS, P).transpose(2, 0, 1),
    }
    nc = _bacc.Bacc("TRN2", target_bir_lowering=False, num_devices=1)
    sent, args = {}, []
    for name, a in arrays.items():
        a = _np.ascontiguousarray(a)
        sent[f"in_{name}"] = a
        args.append(nc.dram_tensor(f"in_{name}", a.shape, _mybir.dt.from_np(a.dtype), kind="ExternalInput").ap())
    args.append(nc.dram_tensor("out_0", (T, D), F32, kind="ExternalOutput").ap())
    block_program(nc, *args)
    r = _run(nc, [sent], core_ids=[0])
    return r.results[0]["out_0"].reshape(1, T, D)
```

```python
import math
from contextlib import ExitStack

import concourse.bass as bass
from concourse import mybir

F32 = mybir.dt.float32
F32R = mybir.dt.float32r
BF16 = mybir.dt.bfloat16
U32 = mybir.dt.uint32
ALU = mybir.AluOpType
ACT = mybir.ActivationFunctionType
AX_X = mybir.AxisListType.X

P = 128
T = 256
NT = T // P
D = 1024
KT = D // P
HEADS = 8
HD = 64
W = HEADS * HD
CT = W // P
LORA = 64
GLORA = 160
NB_IN = 28
NB_GATE = 16
NKEYS = 128
TOPK = 16
RMS_EPS = 1e-6
GN_EPS = 64e-5
NEG = -1e30
LOWEST = -3.0e38
RAW = 4
HALF = NKEYS // 2
PICKS_AT = 12

V_N1, V_N2, V_NF = 0, 8, 16
V_W0, V_A0, V_KK, V_KA, V_RK, V_LG, V_LB = 24, 28, 32, 36, 40, 44, 48
V_MU = 52
NMIX = 15
NVEC = V_MU + NMIX

C_ID, C_ONE, C_BLK, C_IOTA, C_M4, C_NM1, C_NM1T, C_LV = 0, 128, 256, 384, 512, 1024, 1152, 1280
LEVELS = [2, 4, 8, 16, 32, 64]
NCONST = C_LV + 128 * len(LEVELS)


def block_program(nc, x, w_in, w_proj, w_out, w_q, u_t, v_t, vecs, lora_wa, lora_g, rel_bias_t, bucket_onehot,
                  consts, subkeys_t, out):
    with ExitStack() as ctx:
        def sb(name, shape, dt=F32):
            return ctx.enter_context(nc.sbuf_tensor(name, shape, dt))

        def sem(name):
            return ctx.enter_context(nc.semaphore(name))

        arena_at = -(-nc.sbuf_base // 32) * 32
        arena = sb("arena", [P, P * T])
        xT = sb("xT", [P, KT, T])
        xh = sb("xh", [P, KT, T], F32R)
        xl = sb("xl", [P, KT, T], F32R)
        raw_at = -(-nc.sbuf_base // 32) * 32
        raw = sb("raw", [P, RAW, D])
        lo = nc.alloc_sbuf_tensor_at("lo", [P, RAW, D], F32R, offset=raw_at)
        hi = sb("hi", [P, RAW, D], F32R)
        con = sb("con", [P, NCONST])
        vec = sb("vec", [P, NVEC])
        i1T = sb("i1T", [P, T])
        i2T = sb("i2T", [P, T])
        gT = sb("gT", [P, T])
        oh1 = sb("oh1", [P, 2, 4, P])
        oh2 = sb("oh2", [P, 2, 4, P])
        gt = sb("gt", [P, 2, T])
        small = sb("small", [P, 64])

        PS = ctx.enter_context(nc.psum_tensor("PS", [P, 8, 512], F32))
        bias_dram = nc.dram_tensor("bias_rows", [HEADS, P, 512], F32, kind="Internal").ap()

        ident = con[:, C_ID:C_ID + P]
        ones = con[:, C_ONE:C_ONE + P]
        blk = con[:, C_BLK:C_BLK + P]
        iota = con[:, C_IOTA:C_IOTA + P]
        mask4 = con[:, C_M4:C_M4 + 512]
        zeros = con[:, C_LV:C_LV + 256].bitcast(BF16)

        gh, gl = xh[:, 0:4, :], xl[:, 0:4, :]

        def area(a, n, *shape):
            v = arena[:, a:a + n]
            if len(shape) == 2:
                return v.rearrange("p (a b) -> p a b", b=shape[1])
            if len(shape) == 3:
                return v.rearrange("p (a b c) -> p a b c", b=shape[1], c=shape[2])
            return v

        gates = area(0, 4096, 16, T)
        oh = nc.alloc_sbuf_tensor_at("oh", [P, KT, T], F32R, offset=arena_at + 4 * 4096)
        ol = nc.alloc_sbuf_tensor_at("ol", [P, KT, T], F32R, offset=arena_at + 4 * 6144)
        R0 = 8192
        pT = area(R0, 28 * T, 28, T)
        xin = area(R0 + 8192, 2048, NT, D)
        sq = area(R0 + 10240, 2048, KT, T)
        xn = area(R0 + 12288, 2048, KT, T)
        rstd = area(R0 + 14336, T)
        vtokA = area(R0 + 7168, 1024, NT, W)
        biasT = area(R0 + 8192, 3072, HEADS, 384)
        Sb = area(R0 + 11264, 3072, HEADS, 384)
        PTs = area(R0 + 14336, 3072, HEADS, 384)
        mix = area(R0 + 17408, 3840, NMIX, T)
        rowsb = area(R0 + 21248, 512)
        lwa = area(R0 + 21760, 512)
        lg0 = area(R0 + 22272, 512)
        lg1 = area(R0 + 22784, 512)
        bonehot = area(R0 + 23296, 512)
        relb = area(R0 + 23808, 8)

        def slot(n):
            return area(R0 + 1024 * n, 1024, CT, T)
        gB, bonus, bh, kh, vtok = slot(0), slot(1), slot(4), slot(5), area(R0 + 6144, 1024, NT, W)
        KR = area(R0 + 2048, 2048, CT, 2, T)
        tokk = area(R0 + 7168, 512)
        tokb = area(R0 + 7680, 512)
        lw, aB = slot(8), slot(9)
        Lz = area(R0 + 10240, CT * 257, CT, 257)
        E = area(R0 + 12288, CT * 2 * 129, CT, 2, 129)
        EI, kk, k2 = slot(14), slot(15), slot(16)
        rB, kB, vB = mix[:, 0:4], mix[:, 4:8], mix[:, 8:12]
        tmp = area(R0 + 23296, 1024, CT, T)
        mats = area(R0 + 8192, 8192, 16, 4, P)
        X = area(R0 + 16384, 2048, 16, P)
        XT = area(R0 + 18432, 2048, 16, P)
        P1 = area(R0 + 20480, 2048, 16, P)
        Gs = area(R0 + 22528, 512)
        nSK = area(R0 + 23040, 1024, 2, 512)
        ST = area(R0 + 24064, 256, CT, HD)
        osb, ocen, osq = area(R0 + 16384, 1024, CT, T), area(R0 + 17408, 1024, CT, T), area(R0 + 18432, 1024, CT, T)
        coef = area(0, P * T, P, T)
        qT = area(16384, 4096, 16, T)
        subk = area(20480, 2048, 16, P)
        S = area(22528, 4096, 2, 16, P)
        tv = area(26624, 512, 2, 256)
        ti = area(27136, 512, 2, 256).bitcast(U32)
        tif = area(27648, 512, 2, 256)
        cand = area(28160, 2048, HEADS, 256)
        eqt = area(30208, 2048, P, TOPK)
        bp = area(32256, 128).bitcast(U32)
        bpa = area(32384, 128).bitcast(U32)
        bpf = area(32512, 128)
        bvs, i1s, i2s = (con[:, C_M4 + 256 * n:C_M4 + 256 * n + 256].rearrange("p (a b) -> p a b", b=P)
                         for n in range(3))

        landed = [sem(f"unit_landed{j}") for j in range(RAW)]
        hi_made = sem("hi_made")
        lo_dve = sem("lo_made_by_vector")
        lo_pool = sem("lo_made_by_gpsimd")
        unit_done = sem("unit_multiplied")
        act_evac = sem("act_evacuated")
        dve_evac = sem("dve_evacuated")
        dve_step = sem("dve_step")
        pe_step = sem("pe_step")
        act_step = sem("act_step")
        const_in = sem("const_in")
        x_in = sem("x_in")
        xt_ps, xt_sb = sem("xt_ps"), sem("xt_sb")
        sq_made, ss_made, xn_made = sem("sq_made"), sem("ss_made"), sem("xn_made")
        inv_made, root_made = sem("inverse_made"), sem("root_made")
        kk_root, gn_inv, gn_root = sem("kk_root"), sem("gn_inverse"), sem("gn_root")
        lora_in = sem("lora_in")
        rows_ps, rows_sb, rows_out, bias_in = sem("rows_ps"), sem("rows_sb"), sem("rows_out"), sem("bias_in")
        vA_ps, vA_sb = sem("vA_ps"), sem("vA_sb")
        sc_ps, sc_sb, sc_max, sc_exp, p_made = sem("sc_ps"), sem("sc_sb"), sem("sc_max"), sem("sc_exp"), sem("p_made")
        pt_ps, pt_sb, oa_ps, oa_made = sem("pt_ps"), sem("pt_sb"), sem("oa_ps"), sem("oa_made")
        mix_made, lor_act, lor_ps, lor_sb, lor_g = (sem("mix_made"), sem("lora_act"), sem("lora_ps"), sem("lora_sb"),
                                                    sem("lora_g_sb"))
        mid_made, e_made, kk_sq, kk_ss = sem("mid_made"), sem("e_made"), sem("kk_sq"), sem("kk_ss")
        rkv_made, bon_ps, tok_ps, tok_sb = sem("rkv_made"), sem("bonus_ps"), sem("tok_ps"), sem("tok_sb")
        bon_made = sem("bonus_made")
        mat_ps, mat_sb, m1_ps, m1_sb = sem("mat_ps"), sem("mat_sb"), sem("m1_ps"), sem("m1_sb")
        p1_ps, p1_sb, x_ps, x_sb = sem("p1_ps"), sem("p1_sb"), sem("x_ps"), sem("x_sb")
        g_ps, g_sb, sk_ps, sk_sb, st_ps, st_sb = (sem("g_ps"), sem("g_sb"), sem("sk_ps"), sem("sk_sb"), sem("st_ps"),
                                                  sem("st_sb"))
        o_ps, o_sb, mu_ps, cen_sb, var_ps, ob_made = (sem("o_ps"), sem("o_sb"), sem("mu_ps"), sem("cen_sb"),
                                                      sem("var_ps"), sem("ob_made"))
        y_made, h_made = sem("y_made"), sem("h_made")
        subk_in, score_ps, score_sb = sem("subk_in"), sem("score_ps"), sem("score_sb")
        shift_made, exp_made, picks_made, picks_ps, picks_sb = (sem("shift_made"), sem("exp_made"), sem("picks_made"),
                                                                sem("picks_ps"), sem("picks_sb"))
        hot_made = sem("hot_made")
        hot_ps = sem("gates_made")
        gates_used = sem("gates_used")
        coef_made = sem("coef_made")
        gh_made, gl_made, acc_done = sem("gh_made"), sem("gl_made"), sem("acc_done")
        zero_made = sem("zero_made")
        fin_ps, fin_sb, stored = sem("fin_ps"), sem("fin_sb"), sem("stored")

        U_IN, U_PROJ, U_OUT, U_Q, U_U, U_V = 0, 44, 52, 60, 76, 204

        block = ctx.enter_context(nc.Block())

        @block.sync
        def _(sp):
            def load(src, j):
                sp.dma_start(raw[:, j, :], src).then_inc(landed[j], 16)

            sp.dma_start(xin, x.rearrange("(n p) d -> p n d", p=P)).then_inc(x_in, 16)
            sp.dma_start(con[:], consts).then_inc(const_in, 16)
            sp.dma_start(vec[:], vecs).then_inc(const_in, 16)
            for j in range(RAW):
                load(w_in[j], j)
            with sp.Fori(1, U_PROJ // 4) as i:
                for j in range(RAW):
                    sp.wait_ge(unit_done, 4 * i + (j - 3))
                    load(w_in[4 * i + j], j)
            for dst, src in ((lwa, lora_wa), (lg0, lora_g[0:P]), (lg1[0:GLORA - P], lora_g[P:GLORA]),
                             (bonehot[0:33], bucket_onehot), (relb[0:32, 0:8], rel_bias_t)):
                sp.dma_start(dst, src).then_inc(lora_in, 16)
            for g in range(U_PROJ, U_OUT):
                sp.wait_ge(unit_done, g - 3)
                load(w_proj[g - U_PROJ], g % 4)
                if g == U_PROJ + 1:
                    sp.wait_ge(rows_sb, 1)
                    sp.dma_start(bias_dram, rowsb[0:HEADS, :].unsqueeze(1).to_broadcast([HEADS, P, 512])
                                 ).then_inc(rows_out, 16)
                    sp.wait_ge(rows_out, 16)
                    for qt, k0, nk in ((0, 0, P), (1, P, T)):
                        src = bass.AP(bias_dram.tensor, T - 1 - qt * P, [[511, P], [512 * P, HEADS], [1, nk]])
                        sp.dma_start(biasT[:, :, k0:k0 + nk], src).then_inc(bias_in, 16)
            for g in range(U_OUT, U_Q):
                sp.wait_ge(unit_done, g - 3)
                load(w_out[g - U_OUT], g % 4)
            with sp.Fori(0, 4) as i:
                for j in range(RAW):
                    sp.wait_ge(unit_done, 4 * i + (U_Q + j - 3))
                    load(w_q[4 * i + j], j)
            for j in range(RAW):
                sp.wait_ge(unit_done, U_U + j - 3)
                load(u_t[j], j)
            sp.wait_ge(h_made, 8)
            sp.dma_start(subk, subkeys_t).then_inc(subk_in, 16)
            with sp.Fori(1, 32) as i:
                for j in range(RAW):
                    sp.wait_ge(unit_done, 4 * i + (U_U + j - 3))
                    load(u_t[4 * i + j], j)
            for j in range(RAW):
                sp.wait_ge(unit_done, U_V + j - 3)
                load(v_t[j], j)
            with sp.Fori(1, 32) as i:
                for j in range(RAW):
                    sp.wait_ge(unit_done, 4 * i + (U_V + j - 3))
                    load(v_t[4 * i + j], j)
            for n in range(4):
                sp.wait_ge(fin_sb, n + 1)
                sp.dma_start(out.rearrange("(n p) d -> n p d", p=P)[n // 2, :, 512 * (n % 2):512 * (n % 2) + 512],
                             xin[:, n // 2, 512 * (n % 2):512 * (n % 2) + 512]).then_inc(stored, 16)
            sp.wait_ge(stored, 64)

        @block.tensor
        def _(pe):
            mm = nc.tensor.matmul

            def splits_ready(g, lo_sem, lo_count):
                pe.wait_ge(hi_made, g + 1)
                pe.wait_ge(lo_sem, lo_count)

            def product(ps, s, mh, ml, k0=0, k1=KT):
                for k in range(k0, k1):
                    c = slice(P * k, P * k + P)
                    mm(ps, hi[:, s, c], mh[:, k, :], start=(k == k0), stop=False)
                    mm(ps, hi[:, s, c], ml[:, k, :], start=False, stop=False)
                    last = mm(ps, lo[:, s, c], mh[:, k, :], start=False, stop=(k == k1 - 1))
                return last

            def sum_of_squares(n):
                pe.wait_ge(sq_made, n + 1)
                for k in range(KT):
                    last = mm(PS[:, 2, 0:T], ones, sq[:, k, :], start=(k == 0), stop=(k == KT - 1))
                last.then_inc(ss_made, 1)

            pe.sem_inc(act_evac, 2)
            pe.sem_inc(hot_ps, 2)
            pe.wait_ge(x_in, 16)
            pe.wait_ge(const_in, 32)
            for b in range(4):
                for c in range(4):
                    k, n = 2 * b + c // 2, c % 2
                    last = nc.tensor.transpose(PS[:, 4 + b, P * c:P * c + P], xin[:, n, P * k:P * k + P], ident)
                last.then_inc(xt_ps, 1)
            sum_of_squares(0)
            pe.wait_ge(xn_made, 1)
            with pe.Fori(0, U_PROJ // 4) as i:
                for j in range(4):
                    splits_ready(4 * i + j, lo_dve, 4 * i + (j + 1))
                    pe.wait_ge(act_evac, 4 * i + (j + 1))
                    product(PS[:, j % 2, 0:T], j, xh, xl).then_inc(unit_done, 1)
            evacs = U_PROJ
            pe.wait_ge(lora_in, 80)
            pe.wait_ge(dve_step, REL_ROW)
            mm(PS[0:8, 2, :], relb[0:33, 0:8], bonehot[0:33, :], start=True, stop=True).then_inc(rows_ps, 1)
            pe.wait_ge(act_evac, 2 + evacs)
            for n in range(NT):
                for c in range(CT):
                    last = nc.tensor.transpose(PS[:, 3 + n, P * c:P * c + P], pT[:, 8 + c, P * n:P * n + P], ident)
                last.then_inc(vA_ps, 1)
            for h in range(HEADS):
                b, c = HD * (h % 2), h // 2
                bank = [0, 1, 5, 6][h % 4]
                if h >= 4:
                    pe.wait_ge(sc_sb, h - 3)
                mm(PS[:, bank, 0:P], pT[b:b + HD, c, 0:P], pT[b:b + HD, 4 + c, 0:P], start=True, stop=True)
                mm(PS[:, bank, P:P + T], pT[b:b + HD, c, P:T], pT[b:b + HD, 4 + c, :], start=True,
                   stop=True).then_inc(sc_ps, 1)
            pe.wait_ge(p_made, 2)
            for h in range(HEADS):
                bank = [0, 1, 5, 6][h % 4]
                if h < 4:
                    pe.wait_ge(sc_sb, HEADS)
                else:
                    pe.wait_ge(pt_sb, h - 3)
                for n in range(3):
                    last = nc.tensor.transpose(PS[:, bank, P * n:P * n + P], Sb[:, h, P * n:P * n + P], ident)
                last.then_inc(pt_ps, 1)
            pe.wait_ge(vA_sb, 2)
            for h in range(HEADS):
                b, c = HD * (h % 2), h // 2
                pe.wait_ge(pt_sb, h + 1)
                o = PS[b:b + HD, 3 + c // 2, T * (c % 2):T * (c % 2) + T]
                mm(o, vtokA[:, 0, HD * h:HD * h + HD], PTs[:, h, 0:T], start=True, stop=False)
                last = mm(o[:, P:T], vtokA[:, 1, HD * h:HD * h + HD], PTs[:, h, T:T + P], start=False, stop=True)
                if h % 4 == 3:
                    last.then_inc(oa_ps, 1)
            pe.wait_ge(lor_act, 3)
            for c in range(CT):
                col = slice(P * c, P * c + P)
                if c:
                    pe.wait_ge(lor_sb, 2 * c)
                    pe.wait_ge(lor_g, c)
                else:
                    pe.wait_ge(pt_sb, HEADS)
                mm(PS[:, 0, 0:T], lwa[0:LORA, col], mix[0:LORA, 12, :], start=True, stop=True)
                mm(PS[:, 1, 0:T], lwa[LORA:P, col], mix[LORA:P, 12, :], start=True, stop=True)
                mm(PS[:, 5, 0:T], lg0[:, col], mix[:, 13, :], start=True, stop=False)
                mm(PS[:, 5, 0:T], lg1[0:32, col], mix[0:32, 14, :], start=False, stop=True).then_inc(lor_ps, 1)
            pe.wait_ge(kk_sq, 1)
            pe.wait_ge(oa_made, 2)
            for c in range(CT):
                last = mm(PS[:, 3 + c // 2, T * (c % 2):T * (c % 2) + T], blk, tmp[:, c, :], start=True, stop=True)
            last.then_inc(kk_ss, 1)
            pe.wait_ge(rkv_made, 1)
            for c in range(CT):
                last = mm(PS[:, 6 + c // 2, T * (c % 2):T * (c % 2) + T], blk, lw[:, c, :], start=True, stop=True)
            last.then_inc(bon_ps, 1)
            pe.wait_ge(rkv_made, 2)
            pe.wait_ge(lor_sb, 2 * CT)
            for bank, src, n in ((0, vB, 0), (1, vB, 1), (3, kh, 0), (4, bh, 0)):
                for c in range(CT):
                    last = nc.tensor.transpose(PS[:, bank, P * c:P * c + P], src[:, c, P * n:P * n + P], ident)
                last.then_inc(tok_ps, 1)
            pe.wait_ge(tok_sb, 4)
            pe.wait_ge(bon_made, 1)
            pe.wait_ge(lor_g, CT)
            for m in range(16):
                n, b, c = chunk_head(m)
                t = slice(P * n, P * n + P)
                if m >= 4:
                    pe.wait_ge(mat_sb, m - 3)
                mm(PS[:, m % 4, 0:T], kh[b:b + HD, c, t], KR[b:b + HD, c, :, t], start=True, stop=True)
                mm(PS[:, m % 4, T:2 * T], bh[b:b + HD, c, t], KR[b:b + HD, c, :, t], start=True,
                   stop=True).then_inc(mat_ps, 1)
            for m in range(16):
                n, b, c = chunk_head(m)
                t = slice(P * n, P * n + P)
                last = mm(PS[:, 4 + m // 4, P * (m % 4):P * (m % 4) + P], KR[b:b + HD, c, 0, t], bh[b:b + HD, c, t],
                          start=True, stop=True)
                if m % 4 == 3:
                    last.then_inc(m1_ps, 1)
            for lv in range(len(LEVELS)):
                for q in range(4):
                    if lv == 0:
                        pe.wait_ge(mat_sb, 16)
                        pe.wait_ge(m1_sb, 4)
                    else:
                        pe.wait_ge(x_sb, 4 * (lv - 1) + q + 1)
                    for m in range(4 * q, 4 * q + 4):
                        last = mm(PS[:, q, P * (m % 4):P * (m % 4) + P], mats[:, m, 2, :], X[:, m, :], start=True,
                                  stop=True)
                    last.then_inc(p1_ps, 1)
                for q in range(4):
                    pe.wait_ge(p1_sb, 4 * lv + q + 1)
                    if 4 * lv + q >= 2:
                        pe.wait_ge(x_sb, 4 * lv + q - 1)
                    for m in range(4 * q, 4 * q + 4):
                        last = mm(PS[:, 4 + 2 * (q % 2), P * (m % 4):P * (m % 4) + P], P1[:, m, :], XT[:, m, :],
                                  start=True, stop=True)
                    if lv < len(LEVELS) - 1:
                        for m in range(4 * q, 4 * q + 4):
                            last = mm(PS[:, 5 + 2 * (q % 2), P * (m % 4):P * (m % 4) + P], XT[:, m, :], P1[:, m, :],
                                      start=True, stop=True)
                    last.then_inc(x_ps, 1)
            pe.wait_ge(x_sb, 4 * len(LEVELS))
            for n in range(NT):
                if n:
                    pe.wait_ge(st_sb, 1)
                for m in range(8 * n, 8 * n + 8):
                    _, b, c = chunk_head(m)
                    o = PS[:, 2 * (b // HD), HD * c:HD * c + HD]
                    hs = slice(P * c + b, P * c + b + HD)
                    last = mm(o, mats[:, m, 0, :], vtok[:, n, hs], start=True, stop=(n == 0))
                    if n:
                        last = mm(o, KR[b:b + HD, c, 0, P:T], ST[b:b + HD, c, :], start=False, stop=True)
                last.then_inc(g_ps, 1)
                pe.wait_ge(g_sb, n + 1)
                for m in range(8):
                    last = mm(PS[:, 1, HD * m:HD * m + HD], XT[:, 8 * n + m, :], Gs[:, HD * m:HD * m + HD],
                              start=True, stop=True)
                last.then_inc(sk_ps, 1)
                pe.wait_ge(sk_sb, n + 1)
                if n == 0:
                    for m in range(8):
                        _, b, c = chunk_head(m)
                        hs = slice(P * c + b, P * c + b + HD)
                        o = PS[b:b + HD, 3, HD * c:HD * c + HD]
                        mm(o, tokk[:, hs], vtok[:, 0, hs], start=True, stop=False)
                        last = mm(o, tokb[:, hs], nSK[:, 0, HD * m:HD * m + HD], start=False, stop=True)
                    last.then_inc(st_ps, 1)
            for h in range(8):
                for n in range(NT):
                    m = 8 * n + h
                    _, b, c = chunk_head(m)
                    hs = slice(P * c + b, P * c + b + HD)
                    o = PS[b:b + HD, 3 + c // 2, T * (c % 2) + P * n:T * (c % 2) + P * n + P]
                    mm(o, vtok[:, n, hs], mats[:, m, 1, :], start=True, stop=False)
                    last = mm(o, nSK[:, n, HD * h:HD * h + HD], mats[:, m, 3, :], start=False, stop=(n == 0))
                    if n:
                        last = mm(o, ST[b:b + HD, c, :], KR[b:b + HD, c, 1, P:T], start=False, stop=True)
            last.then_inc(o_ps, 1)
            pe.wait_ge(o_sb, 1)
            for c in range(CT):
                last = mm(PS[:, 5 + c // 2, T * (c % 2):T * (c % 2) + T], blk, osb[:, c, :], start=True, stop=True)
            last.then_inc(mu_ps, 1)
            pe.wait_ge(cen_sb, 1)
            for c in range(CT):
                last = mm(PS[:, 3 + c // 2, T * (c % 2):T * (c % 2) + T], blk, osq[:, c, :], start=True, stop=True)
            last.then_inc(var_ps, 1)
            pe.wait_ge(ob_made, 1)
            for g in range(U_PROJ, U_OUT):
                splits_ready(g, lo_pool, g - U_PROJ + 1)
                if g >= U_PROJ + 2:
                    pe.wait_ge(dve_evac, g - U_PROJ - 1)
                product(PS[:, g % 2, 0:T], g % 4, oh, ol, 0, 4)
                product(PS[:, g % 2, T:2 * T], g % 4, oh, ol, 4, 8).then_inc(unit_done, 1)
            pe.wait_ge(y_made, 8)
            for g in range(U_OUT, U_Q):
                splits_ready(g, lo_dve, g - 7)
                if g >= U_OUT + 2:
                    pe.wait_ge(h_made, g - U_OUT - 1)
                product(PS[:, g % 2, 0:T], g % 4, xh, xl).then_inc(unit_done, 1)
            sum_of_squares(1)
            pe.wait_ge(xn_made, 2)
            with pe.Fori(0, 4) as i:
                for j in range(4):
                    splits_ready(4 * i + (U_Q + j), lo_dve, 4 * i + (U_Q + j - 7))
                    pe.wait_ge(act_evac, 4 * i + (evacs + j + 1))
                    product(PS[:, j % 2, 0:T], j, xh, xl).then_inc(unit_done, 1)
            evacs += 16
            pe.wait_ge(act_evac, evacs + 2)
            pe.wait_ge(subk_in, 16)
            for m in range(8):
                n, q = m // 4, m % 4
                if m >= 4:
                    pe.wait_ge(score_sb, m - 3)
                for u in range(4 * q, 4 * q + 4):
                    last = mm(PS[:, 4 + m % 4, P * (u % 4):P * (u % 4) + P], qT[:, u, P * n:P * n + P], subk[:, u, :],
                              start=True, stop=True)
                last.then_inc(score_ps, 1)
            def expert_unit(i, j):
                splits_ready(4 * i + (U_U + j), lo_pool, 4 * i + (8 + j + 1))
                pe.wait_ge(act_evac, 4 * i + (evacs + j + 1))
                product(PS[:, j % 2, 0:T], j, xh, xl).then_inc(unit_done, 1)

            with pe.Fori(0, PICKS_AT) as i:
                for j in range(4):
                    expert_unit(i, j)
            pe.wait_ge(picks_made, 1)
            pe.wait_ge(score_sb, 8)
            for b, src in ((2, i1s), (3, i2s), (4, bvs)):
                for n in range(NT):
                    last = nc.tensor.transpose(PS[:, b, P * n:P * n + P], src[:, n, :], ident)
                last.then_inc(picks_ps, 1)
            with pe.Fori(PICKS_AT, HALF // 4) as i:
                for j in range(4):
                    expert_unit(i, j)
            pe.wait_ge(picks_sb, 3)
            with pe.Fori(HALF // 4, NKEYS // 4) as i:
                for j in range(4):
                    expert_unit(i, j)
                    n = 4 * i + (j - HALF)
                    pe.wait_ge(hot_made, n + 1)
                    pe.wait_ge(gates_used, n + 1)
                    for k in range(4):
                        last = mm(PS[:, 2 + j % 2, P * k:P * k + P], oh1[:, j % 2, k, :], oh2[:, j % 2, k, :],
                                  start=True, stop=True)
                    last.then_inc(hot_ps, 1)
            evacs += NKEYS
            pe.wait_ge(act_evac, evacs + 2)
            pe.wait_ge(gates_used, HALF + 2)
            pe.wait_ge(zero_made, 1)
            for b in range(4):
                mm(PS[:, b, :], zeros[:, 0:P], zeros, start=True, stop=False, skip_group_check=True)
            with pe.Fori(0, NKEYS // 4) as i:
                for j in range(4):
                    splits_ready(4 * i + (U_V + j), lo_dve, 4 * i + (U_U + j - 7))
                    pe.wait_ge(gh_made, 4 * i + (j + 1))
                    pe.wait_ge(gl_made, 4 * i + (j + 1))
                    for k in range(KT):
                        o = PS[:, k // 2, T * (k % 2):T * (k % 2) + T]
                        c = slice(P * k, P * k + P)
                        mm(o, hi[:, j, c], gh[:, j, :], start=False, stop=False, skip_group_check=True)
                        mm(o, hi[:, j, c], gl[:, j, :], start=False, stop=False, skip_group_check=True)
                        last = mm(o, lo[:, j, c], gh[:, j, :], start=False, stop=False, skip_group_check=True)
                    last.then_inc(unit_done, 1)
            for b in range(4):
                mm(PS[:, b, :], zeros[:, 0:P], zeros, start=False, stop=True,
                   skip_group_check=True).then_inc(acc_done, 1)
            pe.wait_ge(h_made, 12)
            sum_of_squares(2)
            pe.wait_ge(xn_made, 3)
            for m in range(4):
                for k in range(4):
                    last = nc.tensor.transpose(PS[:, 4 + m, P * k:P * k + P],
                                               xn[:, 4 * (m % 2) + k, P * (m // 2):P * (m // 2) + P], ident)
                last.then_inc(fin_ps, 1)

        @block.scalar
        def _(act):
            def make_hi(G, j):
                act.wait_ge(landed[j], 16 * G + 16)
                nc.scalar.copy(hi[:, j, :], raw[:, j, :]).then_inc(hi_made, 1)

            def next_hi(G, j):
                make_hi(G if j < 2 else G + 1, (j + 2) % 4)

            def squares(n):
                act.wait_ge([xt_sb, h_made, h_made][n], [4, 8, 12][n])
                nc.scalar.activation(sq, xT[:], ACT.Square).then_inc(sq_made, 1)
                act.wait_ge(inv_made, n + 1)
                nc.scalar.activation(rstd, rstd, ACT.Sqrt).then_inc(root_made, 1)

            make_hi(0, 0)
            make_hi(0, 1)
            squares(0)
            with act.Fori(0, NB_IN // 4) as i:
                for j in range(4):
                    next_hi(i, j)
                    act.wait_ge(unit_done, 4 * i + (j + 1))
                    nc.scalar.copy(pT[:, 4 * i + j, :], PS[:, j % 2, 0:T]).then_inc(act_evac, 1)
            nc.scalar.preload_act_table(ACT.Sigmoid)
            with act.Fori(0, NB_GATE // 4) as i:
                for j in range(4):
                    next_hi(i + NB_IN // 4, j)
                    act.wait_ge(unit_done, 4 * i + (NB_IN + j + 1))
                    nc.scalar.activation(gates[:, 4 * i + j, :], PS[:, j % 2, 0:T], ACT.Sigmoid).then_inc(act_evac, 1)
            act.wait_ge(rows_ps, 1)
            nc.scalar.copy(rowsb[0:HEADS, :], PS[0:HEADS, 2, :]).then_inc(rows_sb, 1)
            for n in range(NT):
                act.wait_ge(vA_ps, n + 1)
                nc.scalar.copy(vtokA[:, n, :], PS[:, 3 + n, :]).then_inc(vA_sb, 1)
            act.wait_ge(mix_made, 1)
            nc.scalar.activation(mix[0:LORA, 12, :], mix[0:LORA, 12, :], ACT.Tanh).then_inc(lor_act, 1)
            nc.scalar.activation(mix[:, 13, :], mix[:, 13, :], ACT.Sigmoid).then_inc(lor_act, 1)
            nc.scalar.activation(mix[0:32, 14, :], mix[0:32, 14, :], ACT.Sigmoid).then_inc(lor_act, 1)
            act.wait_ge(sc_max, 2)
            for h in range(HEADS):
                for n, a, b in ((0, 0, P), (1, P, P + T)):
                    nc.scalar.activation(Sb[:, h, a:b], Sb[:, h, a:b], ACT.Exp, bias=small[:, 8 * n + h:8 * n + h + 1],
                                         accum_out=small[:, 16 + 8 * n + h:17 + 8 * n + h]).then_inc(sc_exp, 1)
            for h in range(HEADS):
                act.wait_ge(pt_ps, h + 1)
                nc.scalar.copy(PTs[:, h, :], PS[:, [0, 1, 5, 6][h % 4], 0:384]).then_inc(pt_sb, 1)
            act.wait_ge(oa_made, 2)
            for c in range(CT):
                act.wait_ge(lor_ps, c + 1)
                nc.scalar.activation(lw[:, c, :], PS[:, 0, 0:T], ACT.Sigmoid,
                                     bias=vec[:, V_W0 + c:V_W0 + c + 1]).then_inc(lor_sb, 1)
                nc.scalar.activation(aB[:, c, :], PS[:, 1, 0:T], ACT.Sigmoid,
                                     bias=vec[:, V_A0 + c:V_A0 + c + 1]).then_inc(lor_sb, 1)
                nc.scalar.copy(gB[:, c, :], PS[:, 5, 0:T]).then_inc(lor_g, 1)
            act.wait_ge(kk_ss, 1)
            nc.scalar.activation(tmp.rearrange("p a b -> p (a b)"), PS[:, 3:5, :].rearrange("p a b -> p (a b)"),
                                 ACT.Sqrt).then_inc(kk_root, 1)
            act.wait_ge(mid_made, 1)
            for c in range(CT):
                for n in range(NT):
                    m = 32 + 2 * c + n
                    nc.scalar.activation(E[:, c, n, :], Lz[:, c, P * n:P * n + P + 1], ACT.Exp,
                                         bias=small[:, m:m + 1]).then_inc(e_made, 1)
                    nc.scalar.activation(EI[:, c, P * n:P * n + P], Lz[:, c, P * n + 1:P * n + P + 1], ACT.Exp,
                                         bias=small[:, m + 8:m + 9], scale=-1.0).then_inc(e_made, 1)
            nc.scalar.activation(small[:, 48:52], small[:, 52:56], ACT.Exp).then_inc(e_made, 1)
            for n, dst in enumerate((vtok[:, 0, :], vtok[:, 1, :], tokk, tokb)):
                act.wait_ge(tok_ps, n + 1)
                nc.scalar.copy(dst, PS[:, (0, 1, 3, 4)[n], :]).then_inc(tok_sb, 1)
            act.wait_ge(gn_inv, 1)
            nc.scalar.activation(osb, osb, ACT.Sqrt).then_inc(gn_root, 1)
            for g in range(U_PROJ, U_Q):
                next_hi(g // 4, g % 4)
            squares(1)
            with act.Fori(0, 4) as i:
                for j in range(4):
                    next_hi(i + U_Q // 4, j)
                    act.wait_ge(unit_done, 4 * i + (U_Q + j + 1))
                    nc.scalar.copy(qT[:, 4 * i + j, :], PS[:, j % 2, 0:T]).then_inc(act_evac, 1)
            for m in range(8):
                act.wait_ge(score_ps, m + 1)
                nc.scalar.copy(S[:, m // 4, 4 * (m % 4):4 * (m % 4) + 4, :].rearrange("p a b -> p (a b)"),
                               PS[:, 4 + m % 4, :]).then_inc(score_sb, 1)
            nc.scalar.preload_act_table(ACT.Gelu)
            with act.Fori(0, PICKS_AT) as i:
                for j in range(4):
                    next_hi(i + U_U // 4, j)
                    act.wait_ge(unit_done, 4 * i + (U_U + j + 1))
                    nc.scalar.activation(coef[:, 4 * i + j, :], PS[:, j % 2, 0:T], ACT.Gelu).then_inc(act_evac, 1)
            act.wait_ge(shift_made, 2)
            nc.scalar.activation(bvs, bvs, ACT.Exp).then_inc(exp_made, 1)
            nc.scalar.preload_act_table(ACT.Gelu)
            with act.Fori(PICKS_AT, HALF // 4) as i:
                for j in range(4):
                    next_hi(i + U_U // 4, j)
                    act.wait_ge(unit_done, 4 * i + (U_U + j + 1))
                    nc.scalar.activation(coef[:, 4 * i + j, :], PS[:, j % 2, 0:T], ACT.Gelu).then_inc(act_evac, 1)
            with act.Fori(HALF // 4, NKEYS // 4) as i:
                for j in range(4):
                    next_hi(i + U_U // 4, j)
                    act.wait_ge(unit_done, 4 * i + (U_U + j + 1))
                    act.wait_ge(coef_made, 4 * i + (j + 1 - HALF))
                    nc.scalar.activation(gt[:, j % 2, :], PS[:, j % 2, 0:T], ACT.Gelu).then_inc(act_evac, 1)

            def make_gh(i, j):
                act.wait_ge(unit_done, 4 * i + (U_V + j - 3))
                nc.scalar.copy(gh[:, j % 4, :], coef[:, 4 * i + j, :]).then_inc(gh_made, 1)

            act.wait_ge(coef_made, HALF + 2)
            make_gh(0, 0)
            make_gh(0, 1)
            with act.Fori(0, NKEYS // 4 - 1) as i:
                for j in range(4):
                    make_gh(i, j + 2)
                    next_hi(i + U_V // 4, j)
            for j in range(2):
                make_gh(NKEYS // 4 - 1, j + 2)
                next_hi(U_V // 4 + NKEYS // 4 - 1, j)
            squares(2)

        @block.gpsimd
        def _(pool):
            for g in range(U_PROJ, U_OUT):
                pool.wait_ge(hi_made, g + 1)
                nc.gpsimd.tensor_tensor(lo[:, g % 4, :], raw[:, g % 4, :], hi[:, g % 4, :].bitcast(F32),
                                        ALU.subtract).then_inc(lo_pool, 1)
            with pool.Fori(0, NKEYS // 4) as i:
                for j in range(4):
                    pool.wait_ge(hi_made, 4 * i + (U_U + j + 1))
                    nc.gpsimd.tensor_tensor(lo[:, j, :], raw[:, j, :], hi[:, j, :].bitcast(F32),
                                            ALU.subtract).then_inc(lo_pool, 1)

        @block.vector
        def _(dve):
            steps = [0]

            def link(ins):
                steps[0] += 1
                ins.then_inc(dve_step, 1)
                dve.wait_ge(dve_step, steps[0])

            V = nc.vector

            def make_lo(g, j):
                dve.wait_ge(hi_made, g)
                V.tensor_tensor(lo[:, j, :], raw[:, j, :], hi[:, j, :].bitcast(F32),
                                ALU.subtract).then_inc(lo_dve, 1)

            def per_channel(a):
                return vec[:, a:a + 1]

            def rms_scale(n, gain):
                dve.wait_ge(ss_made, n + 1)
                link(V.tensor_scalar(rstd, PS[:, 2, 0:T], 1.0 / D, RMS_EPS, ALU.mult, ALU.add))
                V.reciprocal(rstd, rstd).then_inc(inv_made, 1)
                dve.wait_ge(root_made, n + 1)
                for k in range(KT):
                    last = V.scalar_tensor_tensor(out=xn[:, k, :], in0=xT[:, k, :], scalar=per_channel(gain + k),
                                                  in1=rstd, op0=ALU.mult, op1=ALU.mult)
                if n == 2:
                    last.then_inc(xn_made, 1)
                    return
                link(last)
                link(V.tensor_copy(xh[:], xn))
                V.tensor_tensor(xl[:], xn, xh[:].bitcast(F32), ALU.subtract).then_inc(xn_made, 1)

            V.memset(relb[0:64, :], NEG).then_inc(dve_step, 1)
            steps[0] += 1
            for b in range(4):
                dve.wait_ge(xt_ps, b + 1)
                V.tensor_copy(xT[:, 2 * b:2 * b + 2, :], PS[:, 4 + b, :].rearrange("p (a b) -> p a b", a=2)
                              ).then_inc(xt_sb, 1)
            dve.wait_ge(xt_sb, 4)
            rms_scale(0, V_N1)
            with dve.Fori(0, U_PROJ // 4) as i:
                for j in range(4):
                    make_lo(4 * i + (j + 1), j)

            dve.wait_ge(act_evac, 2 + U_PROJ)
            dve.wait_ge(bias_in, 32)
            for h in range(HEADS):
                dve.wait_ge(sc_ps, h + 1)
                V.scalar_tensor_tensor(out=Sb[:, h, :], in0=PS[:, [0, 1, 5, 6][h % 4], 0:384], scalar=HD ** -0.5,
                                       in1=biasT[:, h, :], op0=ALU.mult, op1=ALU.add).then_inc(sc_sb, 1)
            dve.wait_ge(sc_sb, HEADS)
            V.tensor_reduce(small[:, 0:8], Sb[:, :, 0:P], AX_X, ALU.max, negate=True).then_inc(sc_max, 1)
            V.tensor_reduce(small[:, 8:16], Sb[:, :, P:P + T], AX_X, ALU.max, negate=True).then_inc(sc_max, 1)
            m15 = pT[:, 12:12 + NMIX, :]
            V.tensor_tensor(mix[:, :, 1:T], m15[:, :, 0:T - 1], m15[:, :, 1:T], ALU.subtract)
            link(V.tensor_scalar(mix[:, :, 0:1], m15[:, :, 0:1], -1.0, None, ALU.mult))
            for c in range(NMIX):
                last = V.scalar_tensor_tensor(out=mix[:, c, :], in0=mix[:, c, :], scalar=per_channel(V_MU + c),
                                              in1=m15[:, c, :], op0=ALU.mult, op1=ALU.add)
            last.then_inc(mix_made, 1)
            dve.wait_ge(sc_exp, 16)
            link(V.reciprocal(small[:, 16:32], small[:, 16:32]))
            V.tensor_tensor(Sb[:, :, 0:P], Sb[:, :, 0:P], small[:, 16:24].unsqueeze(2).to_broadcast([P, HEADS, P]),
                            ALU.mult).then_inc(p_made, 1)
            V.tensor_tensor(Sb[:, :, P:P + T], Sb[:, :, P:P + T],
                            small[:, 24:32].unsqueeze(2).to_broadcast([P, HEADS, T]), ALU.mult).then_inc(p_made, 1)

            def split_out(dst0, src):
                link(V.tensor_copy(oh[:, dst0[0]:dst0[1], :], src))
                return V.tensor_tensor(ol[:, dst0[0]:dst0[1], :], src, oh[:, dst0[0]:dst0[1], :].bitcast(F32),
                                       ALU.subtract)
            for b in range(2):
                dve.wait_ge(oa_ps, b + 1)
                split_out((2 * b, 2 * b + 2), PS[:, 3 + b, :].rearrange("p (a b) -> p a b", a=2)).then_inc(oa_made, 1)

            dve.wait_ge(mix_made, 1)
            dve.wait_ge(rows_sb, 1)
            for c in range(CT):
                last = V.tensor_scalar(kk[:, c, :], kB[:, c, :], per_channel(V_KK + c), None, ALU.mult)
            link(last)
            V.tensor_tensor(tmp, kk, kk, ALU.mult).then_inc(kk_sq, 1)
            dve.wait_ge(lor_sb, 2 * CT)
            link(V.tensor_scalar(lw, lw, -math.exp(-0.5), None, ALU.mult))
            V.memset(E[:, :, :, :], 1.0)
            link(V.memset(Lz[:, :, 0:1], 0.0))
            for c in range(CT):
                last = V.tensor_tensor_scan(Lz[:, c, 1:T + 1], E[:, 0, 0:2, :].rearrange("p a b -> p (a b)")[:, 0:T],
                                            lw[:, c, :], 0.0, ALU.mult, ALU.add)
            link(last)
            mids = Lz[:, :, HD:HD + P + 1:P]
            sm = small[:, 32:40].rearrange("p (c n) -> p c n", n=2)
            V.tensor_scalar(sm, mids, -1.0, None, ALU.mult)
            V.tensor_tensor(small[:, 52:56].unsqueeze(2), mids[:, :, 1:2], mids[:, :, 0:1], ALU.subtract)
            V.tensor_copy(small[:, 40:48].rearrange("p (c n) -> p c n", n=2), mids).then_inc(mid_made, 1)
            dve.wait_ge(kk_root, 1)
            link(V.tensor_scalar(tmp, tmp, 1e-12, None, ALU.max))
            link(V.reciprocal(tmp, tmp))
            link(V.tensor_tensor(kk, kk, tmp, ALU.mult))
            for c in range(CT):
                last = V.tensor_scalar(tmp[:, c, :], aB[:, c, :], 1.0, per_channel(V_KA + c), ALU.subtract, ALU.mult)
            link(last)
            link(V.scalar_tensor_tensor(out=k2, in0=tmp, scalar=1.0, in1=kB, op0=ALU.add, op1=ALU.mult))
            link(V.tensor_tensor(aB, kk, aB, ALU.mult))
            for c in range(CT):
                last = V.scalar_tensor_tensor(out=lw[:, c, :], in0=rB[:, c, :], scalar=per_channel(V_RK + c),
                                              in1=k2[:, c, :], op0=ALU.mult, op1=ALU.mult)
            last.then_inc(rkv_made, 1)
            dve.wait_ge(e_made, 4 * CT + 1)
            V.tensor_tensor(bh, aB, EI, ALU.mult)
            V.tensor_tensor(kh, k2, EI, ALU.mult)
            for n in range(NT):
                t = slice(P * n, P * n + P)
                V.tensor_tensor(KR[:, :, 0, t], kk[:, :, t], E[:, :, n, 0:P], ALU.mult)
                last = V.tensor_tensor(KR[:, :, 1, t], rB[:, :, t], E[:, :, n, 1:P + 1], ALU.mult)
            last.then_inc(rkv_made, 1)
            dve.wait_ge(bon_ps, 1)
            for b in range(2):
                last = V.tensor_tensor(bonus[:, 2 * b:2 * b + 2, :], PS[:, 6 + b, :].rearrange("p (a b) -> p a b", a=2),
                                       vB[:, 2 * b:2 * b + 2, :], ALU.mult)
            last.then_inc(bon_made, 1)
            dve.wait_ge(rkv_made, 2)
            dve.wait_ge(tok_ps, 4)
            for m in range(16):
                dve.wait_ge(mat_ps, m + 1)
                V.tensor_tensor(mats[:, m, :, :].rearrange("p a b -> p (a b)"), PS[:, m % 4, :], mask4,
                                ALU.mult).then_inc(mat_sb, 1)
            id4 = ident.unsqueeze(1).to_broadcast([P, 4, P])

            def bcast4(a):
                return con[:, a:a + P].unsqueeze(1).to_broadcast([P, 4, P])

            def bank4(b):
                return PS[:, b, :].rearrange("p (a b) -> p a b", a=4)
            dve.wait_ge(mat_sb, 16)
            for q in range(4):
                dve.wait_ge(m1_ps, q + 1)
                V.tensor_tensor(X[:, 4 * q:4 * q + 4, :], bank4(4 + q), bcast4(C_NM1), ALU.mult)
                link(V.tensor_tensor(XT[:, 4 * q:4 * q + 4, :], mats[:, 4 * q:4 * q + 4, 2, :], bcast4(C_NM1T), ALU.mult))
                V.tensor_tensor(X[:, 4 * q:4 * q + 4, :], X[:, 4 * q:4 * q + 4, :], id4, ALU.add)
                V.tensor_tensor(XT[:, 4 * q:4 * q + 4, :], XT[:, 4 * q:4 * q + 4, :], id4, ALU.add).then_inc(m1_sb, 1)
            for lv in range(len(LEVELS)):
                for q in range(4):
                    dve.wait_ge(p1_ps, 4 * lv + q + 1)
                    V.tensor_tensor(P1[:, 4 * q:4 * q + 4, :], bank4(q), bcast4(C_LV + P * lv),
                                    ALU.mult).then_inc(p1_sb, 1)
                for q in range(4):
                    dve.wait_ge(x_ps, 4 * lv + q + 1)
                    a = slice(4 * q, 4 * q + 4)
                    if lv < len(LEVELS) - 1:
                        V.tensor_tensor(X[:, a, :], X[:, a, :], bank4(5 + 2 * (q % 2)), ALU.subtract)
                    V.tensor_tensor(XT[:, a, :], XT[:, a, :], bank4(4 + 2 * (q % 2)), ALU.subtract).then_inc(x_sb, 1)
            for n in range(NT):
                dve.wait_ge(g_ps, n + 1)
                V.tensor_copy(Gs.rearrange("p (a b) -> p a b", a=2), PS[:, 0:3:2, 0:T]).then_inc(g_sb, 1)
                dve.wait_ge(sk_ps, n + 1)
                V.tensor_scalar(nSK[:, n, :], PS[:, 1, :], -1.0, None, ALU.mult).then_inc(sk_sb, 1)
                if n == 0:
                    dve.wait_ge(st_ps, 1)
                    V.tensor_tensor(ST, PS[:, 3, 0:CT * HD].rearrange("p (c i) -> p c i", i=HD),
                                    small[:, 48:52].unsqueeze(2).to_broadcast([P, CT, HD]), ALU.mult).then_inc(st_sb, 1)
            dve.wait_ge(x_sb, 4 * len(LEVELS))
            dve.wait_ge(o_ps, 1)
            for b in range(2):
                last = V.tensor_copy(osb[:, 2 * b:2 * b + 2, :], PS[:, 3 + b, :].rearrange("p (a b) -> p a b", a=2))
            last.then_inc(o_sb, 1)
            dve.wait_ge(o_sb, 1)
            dve.wait_ge(mu_ps, 1)
            for b in range(2):
                last = V.scalar_tensor_tensor(out=ocen[:, 2 * b:2 * b + 2, :],
                                              in0=PS[:, 5 + b, :].rearrange("p (a b) -> p a b", a=2), scalar=-1.0 / HD,
                                              in1=osb[:, 2 * b:2 * b + 2, :], op0=ALU.mult, op1=ALU.add)
            link(last)
            V.tensor_tensor(osq, ocen, ocen, ALU.mult).then_inc(cen_sb, 1)
            dve.wait_ge(var_ps, 1)
            for b in range(2):
                last = V.tensor_scalar(osb[:, 2 * b:2 * b + 2, :], PS[:, 3 + b, :].rearrange("p (a b) -> p a b", a=2),
                                       1.0 / HD, GN_EPS, ALU.mult, ALU.add)
            link(last)
            V.reciprocal(osb, osb).then_inc(gn_inv, 1)
            dve.wait_ge(gn_root, 1)
            link(V.tensor_tensor(ocen, ocen, osb, ALU.mult))
            for c in range(CT):
                last = V.tensor_scalar(ocen[:, c, :], ocen[:, c, :], per_channel(V_LG + c), per_channel(V_LB + c),
                                       ALU.mult, ALU.add)
            link(last)
            link(V.tensor_tensor(ocen, ocen, bonus, ALU.add))
            link(V.tensor_tensor(ocen, ocen, gB, ALU.mult))
            split_out((4, 8), ocen).then_inc(ob_made, 1)

            V.memset(zeros, 0.0).then_inc(zero_made, 1)

            ya, yb = xn[:, 0, :], xn[:, 1, :]
            for g in range(U_PROJ, U_OUT):
                k = g - U_PROJ
                dve.wait_ge(unit_done, g + 1)
                V.tensor_tensor(ya, PS[:, g % 2, 0:T], gates[:, k, :], ALU.mult)
                last = V.tensor_tensor(yb, PS[:, g % 2, T:2 * T], gates[:, KT + k, :], ALU.mult)
                last.then_inc(dve_evac, 1)
                dve.wait_ge(dve_evac, k + 1)
                link(V.tensor_tensor(ya, ya, yb, ALU.add))
                link(V.tensor_copy(xh[:, k, :], ya))
                V.tensor_tensor(xl[:, k, :], ya, xh[:, k, :].bitcast(F32), ALU.subtract).then_inc(y_made, 1)
                dve.wait_ge(y_made, k + 1)
            make_lo(U_OUT + 1, 0)
            make_lo(U_OUT + 2, 1)
            for g in range(U_OUT, U_Q):
                if g < U_Q - 2:
                    make_lo(g + 3, (g + 2) % 4)
                k = g - U_OUT
                dve.wait_ge(unit_done, g + 1)
                V.tensor_tensor(xT[:, k, :], xT[:, k, :], PS[:, g % 2, 0:T], ALU.add).then_inc(h_made, 1)
            dve.wait_ge(h_made, 8)
            rms_scale(1, V_N2)
            with dve.Fori(0, 4) as i:
                for j in range(4):
                    make_lo(4 * i + (U_Q + j + 1), j)

            for n in range(NT):
                dve.wait_ge(score_sb, 8)

                def top16(values, vals, idx):
                    N = len(values)
                    for u in range(N):
                        last = V.max(vals[u][:, 0:8], values[u])
                    link(last)
                    for u in range(N):
                        last = V.max_index(idx[u][:, 0:8], vals[u][:, 0:8], values[u])
                    link(last)
                    for u in range(N):
                        last = V.match_replace(values[u], vals[u][:, 0:8], values[u], LOWEST)
                    link(last)
                    for u in range(N):
                        last = V.max(vals[u][:, 8:16], values[u])
                    link(last)
                    for u in range(N):
                        last = V.max_index(idx[u][:, 8:16], vals[u][:, 8:16], values[u])
                    link(last)

                top16([S[:, n, u, :] for u in range(16)], [tv[:, n, 16 * u:16 * u + 16] for u in range(16)],
                      [ti[:, n, 16 * u:16 * u + 16] for u in range(16)])
                V.tensor_copy(tif[:, n, :], ti[:, n, :])
                tv4 = tv[:, n, :].rearrange("p (h s k) -> p h s k", s=2, k=TOPK)
                ti4 = tif[:, n, :].rearrange("p (h s k) -> p h s k", s=2, k=TOPK)
                cand4 = cand.rearrange("p h (a b) -> p h a b", a=TOPK)
                link(V.tensor_tensor(cand4, tv4[:, :, 0, :].unsqueeze(3).to_broadcast([P, HEADS, TOPK, TOPK]),
                                     tv4[:, :, 1, :].unsqueeze(2).to_broadcast([P, HEADS, TOPK, TOPK]), ALU.add))
                top16([cand[:, h, :] for h in range(HEADS)], [bvs[:, n, 16 * h:16 * h + 16] for h in range(HEADS)],
                      [bp[:, 16 * h:16 * h + 16] for h in range(HEADS)])
                for side, dst in ((0, i1s), (1, i2s)):
                    if side == 0:
                        link(V.tensor_scalar(bpa, bp, 4, None, ALU.logical_shift_right))
                    else:
                        link(V.tensor_scalar(bpa, bp, 15, None, ALU.bitwise_and))
                    link(V.tensor_copy(bpf, bpa))
                    link(V.tensor_tensor(eqt, bpf.unsqueeze(2).to_broadcast([P, P, TOPK]),
                                         iota[:, 0:TOPK].unsqueeze(1).to_broadcast([P, P, TOPK]), ALU.is_equal))
                    e4 = eqt.rearrange("p (h k) j -> p h k j", h=HEADS)
                    link(V.tensor_tensor(e4, e4, ti4[:, :, side, :].unsqueeze(2).to_broadcast([P, HEADS, TOPK, TOPK]),
                                         ALU.mult))
                    link(V.tensor_reduce(dst[:, n, :], eqt, AX_X, ALU.add))
                b3 = bvs[:, n, :].rearrange("p (h k) -> p h k", k=TOPK)
                V.tensor_copy(small[:, 0:8].unsqueeze(2), b3[:, :, 0:1]).then_inc(dve_step, 1)
                steps[0] += 1
                dve.wait_ge(dve_step, steps[0])
                V.tensor_tensor(b3, b3, small[:, 0:8].unsqueeze(2).to_broadcast([P, HEADS, TOPK]),
                                ALU.subtract).then_inc(shift_made, 1)
            dve.wait_ge(exp_made, 1)
            b4 = bvs.rearrange("p n (h k) -> p (n h) k", k=TOPK)
            link(V.tensor_reduce(small[:, 0:16], b4, AX_X, ALU.add))
            link(V.reciprocal(small[:, 16:32], small[:, 0:16]))
            V.tensor_tensor(b4, b4, small[:, 16:32].unsqueeze(2).to_broadcast([P, 16, TOPK]),
                            ALU.mult).then_inc(picks_made, 1)
            for b, dst in ((2, i1T), (3, i2T), (4, gT)):
                dve.wait_ge(picks_ps, b - 1)
                V.tensor_copy(dst[:], PS[:, b, 0:T]).then_inc(picks_sb, 1)
            dve.wait_ge(picks_sb, 3)

            V.memset(coef[:, HALF:, :], 1.0).then_inc(coef_made, 2)

            def one_hots(i, j):
                dve.wait_ge(hot_ps, 4 * i + (j + 1))
                for k in range(4):
                    t = 16 * i + (4 * j + k)
                    V.tensor_scalar(oh1[:, j % 2, k, :], iota, i1T[:, bass.ds(t, 1)], gT[:, bass.ds(t, 1)],
                                    ALU.is_equal, ALU.mult)
                    last = V.tensor_scalar(oh2[:, j % 2, k, :], iota, i2T[:, bass.ds(t, 1)], None, ALU.is_equal)
                last.then_inc(hot_made, 1)

            def coefficients(i, j):
                n = 4 * i + j
                dve.wait_ge(hot_ps, n + 3)
                dve.wait_ge(coef_made, n + 2)
                c = coef[:, :, bass.ds(4 * n, 4)]
                V.tensor_tensor(c, PS[:, 2 + j % 2, :].rearrange("p (t k) -> p k t", t=4), c,
                                ALU.mult).then_inc(gates_used, 1)
                dve.wait_ge(act_evac, n + (2 + U_PROJ + 16 + HALF + 1))
                dve.wait_ge(gates_used, n + 3)
                c = coef[:, n + HALF, :]
                V.tensor_tensor(c, c, gt[:, j % 2, :], ALU.mult).then_inc(coef_made, 1)

            dve.sem_inc(gates_used, 2)
            one_hots(0, 0)
            one_hots(0, 1)
            dve.wait_ge(act_evac, 2 + U_PROJ + 16 + HALF)
            with dve.Fori(0, T // 16 - 1) as i:
                for j in range(4):
                    coefficients(i, j)
                    one_hots(i, j + 2)
            for j in range(4):
                coefficients(T // 16 - 1, j)
                if j < 2:
                    one_hots(T // 16 - 1, j + 2)
            with dve.Fori(0, NKEYS // 4) as i:
                for j in range(4):
                    dve.wait_ge(gh_made, 4 * i + (j + 1))
                    V.tensor_tensor(gl[:, j, :], coef[:, 4 * i + j, :], gh[:, j, :].bitcast(F32),
                                    ALU.subtract).then_inc(gl_made, 1)
                    make_lo(4 * i + (U_V + j + 1), j)
            for b in range(4):
                dve.wait_ge(acc_done, b + 1)
                V.tensor_tensor(xT[:, 2 * b:2 * b + 2, :], xT[:, 2 * b:2 * b + 2, :],
                                PS[:, b, :].rearrange("p (a b) -> p a b", a=2), ALU.add).then_inc(h_made, 1)
            dve.wait_ge(h_made, 12)
            rms_scale(2, V_NF)
            for m in range(4):
                dve.wait_ge(fin_ps, m + 1)
                V.tensor_copy(xin[:, m // 2, 512 * (m % 2):512 * (m % 2) + 512], PS[:, 4 + m, :]).then_inc(fin_sb, 1)


REL_ROW = 1


def chunk_head(m):
    return m // 8, HD * (m % 8 // 4), m % 4


def shape_constants(np):
    r = np.arange(P)
    c = np.zeros((P, NCONST), np.float32)
    c[:, C_ID:C_ID + P] = np.eye(P)
    c[:, C_ONE:C_ONE + P] = 1
    c[:, C_BLK:C_BLK + P] = r[:, None] // HD == r[None, :] // HD
    c[:, C_IOTA:C_IOTA + P] = r[None, :]
    strict, incl = r[None, :] > r[:, None], r[None, :] >= r[:, None]
    for n, m in enumerate((strict, incl, strict, incl)):
        c[:, C_M4 + P * n:C_M4 + P * n + P] = m

    def lower_left(n):
        t, s = r[:, None], r[None, :]
        return (t // (2 * n) == s // (2 * n)) & (t // n % 2 == 1) & (s // n % 2 == 0)
    c[:, C_NM1:C_NM1 + P] = -1.0 * lower_left(1)
    c[:, C_NM1T:C_NM1T + P] = -1.0 * lower_left(1).T
    for k, n in enumerate(LEVELS):
        c[:, C_LV + P * k:C_LV + P * k + P] = lower_left(n)
    hot = np.zeros((33, 512), np.float32)
    for m in range(512):
        n = T - 1 - m
        if n < 0:
            b = 32
        elif n < 16:
            b = n
        else:
            f = np.float32(np.log(np.float32(n) / np.float32(16))) / np.float32(math.log(128 / 16))
            b = min(16 + int(np.float32(f) * np.float32(16)), 31)
        hot[b, m] = 1
    return c, hot


def kernel(**inputs):
    import numpy as _np
    import concourse.bacc as _bacc
    from concourse import mybir as _mybir
    from concourse.bass_utils import run_bass_kernel_spmd as _run

    i = {k: _np.asarray(v) for k, v in inputs.items()}

    def units(w):
        n = w.shape[1] // P
        return _np.ascontiguousarray(w.reshape(KT, P, n, P).transpose(2, 1, 0, 3)).reshape(n, P, D)

    def cols(a):
        return a.reshape(-1, P).T

    w = i['w_in'][0]
    n_in = 3 * W + 3 * W + 2 * LORA + GLORA
    w_all = _np.zeros((D, (NB_IN + NB_GATE) * P), w.dtype)
    w_all[:, :n_in] = w[:, :n_in]
    w_all[:, NB_IN * P:] = w[:, n_in:]
    mu = _np.zeros((NMIX * P,), w.dtype)
    mu[:n_in - 3 * W] = i['rwkv_mu'][0]
    vecs = _np.concatenate([cols(a) for a in (
        i['norm1_g'][0], i['norm2_g'][0], i['normf_g'], i['w0'][0], i['a0'][0], i['k_k'][0], i['k_a'][0],
        i['r_k'][0].reshape(-1), i['lnx_g'][0], i['lnx_b'][0], mu)], axis=1)
    consts, hot = shape_constants(_np)
    arrays = {
        'x': i['x'][0],
        'w_in_units': units(w_all),
        'w_proj_units': units(_np.concatenate([i['w_proj_a'][0], i['w_proj_b'][0]], axis=0)),
        'w_out_units': units(i['w_out'][0]),
        'w_q_units': units(i['peer_wq'][0]),
        'u_units': i['peer_u'][0].reshape(NKEYS, NKEYS, KT, P).transpose(1, 3, 2, 0).reshape(NKEYS, P, D),
        'v_units': i['peer_v'][0].reshape(NKEYS, NKEYS, D).transpose(1, 0, 2),
        'vecs': vecs,
        'lora_wa': _np.concatenate([i['w_lora_up'][0], i['a_lora_up'][0]], axis=0),
        'lora_g': i['g_lora_up'][0],
        'rel_bias_t': i['rel_bias'].T,
        'bucket_onehot': hot,
        'consts': consts,
        'subkeys_t': i['peer_subkeys'][0].reshape(2 * HEADS, NKEYS, P).transpose(2, 0, 1),
    }
    nc = _bacc.Bacc("TRN2", target_bir_lowering=False, num_devices=1)
    sent, args = {}, []
    for name, a in arrays.items():
        a = _np.ascontiguousarray(a)
        sent[f"in_{name}"] = a
        args.append(nc.dram_tensor(f"in_{name}", a.shape, _mybir.dt.from_np(a.dtype), kind="ExternalInput").ap())
    args.append(nc.dram_tensor("out_0", (T, D), F32, kind="ExternalOutput").ap())
    block_program(nc, *args)
    r = _run(nc, [sent], core_ids=[0])
    return r.results[0]["out_0"].reshape(1, T, D)
```

```python
import math
from contextlib import ExitStack

import concourse.bass as bass
from concourse import mybir

F32 = mybir.dt.float32
F32R = mybir.dt.float32r
BF16 = mybir.dt.bfloat16
U32 = mybir.dt.uint32
ALU = mybir.AluOpType
ACT = mybir.ActivationFunctionType
AX_X = mybir.AxisListType.X

P = 128
T = 256
NT = T // P
D = 1024
KT = D // P
HEADS = 8
HD = 64
W = HEADS * HD
CT = W // P
LORA = 64
GLORA = 160
NB_R = 16
NB_IN = 28
NB_GATE = 16
NKEYS = 128
TOPK = 16
RMS_EPS = 1e-6
GN_EPS = 64e-5
NEG = -1e30
LOWEST = -3.0e38
RAW = 4
HALF = NKEYS // 2
PICKS_AT = 12

V_N1, V_N2 = 0, 8
V_W0, V_A0, V_KK, V_KA, V_RK, V_LG, V_LB = 16, 20, 24, 28, 32, 36, 40
V_MU = 44
NMIX = 15
NVEC = V_MU + NMIX

C_ID, C_ONE, C_BLK, C_IOTA, C_M4, C_NM1, C_NM1T, C_LV = 0, 128, 256, 384, 512, 1024, 1152, 1280
LEVELS = [2, 4, 8, 16, 32, 64]
NCONST = C_LV + 128 * len(LEVELS)


def block_program(nc, x, w_in, w_proj, w_out, w_q, u_t, v_t, vecs, gain_row, lora_wa, lora_g, rel_bias_t, bucket_onehot,
                  consts, subkeys_t, out):
    with ExitStack() as ctx:
        def sb(name, shape, dt=F32):
            return ctx.enter_context(nc.sbuf_tensor(name, shape, dt))

        def sem(name):
            return ctx.enter_context(nc.semaphore(name))

        arena_at = -(-nc.sbuf_base // 32) * 32
        arena = sb("arena", [P, P * T])
        xT = sb("xT", [P, KT, T])
        xh = sb("xh", [P, KT, T], F32R)
        xl = sb("xl", [P, KT, T], F32R)
        raw_at = -(-nc.sbuf_base // 32) * 32
        raw = sb("raw", [P, RAW, D])
        lo = nc.alloc_sbuf_tensor_at("lo", [P, RAW, D], F32R, offset=raw_at)
        hi = sb("hi", [P, RAW, D], F32R)
        con = sb("con", [P, NCONST])
        vec = sb("vec", [P, NVEC])
        i1T = sb("i1T", [P, T])
        i2T = sb("i2T", [P, T])
        gT = sb("gT", [P, T])
        hot = sb("hot", [P, 2, 2, 4, P])
        oh1, oh2 = hot[:, 0], hot[:, 1]
        gt = sb("gt", [P, 2, T])
        small = sb("small", [P, 96])
        rms = small[:, 56:60]
        kk_scale, gn_scale = small[:, 64:80], small[:, 80:96]

        PS = ctx.enter_context(nc.psum_tensor("PS", [P, 8, 512], F32))
        bias_dram = nc.dram_tensor("bias_rows", [HEADS, P, 512], F32, kind="Internal").ap()

        ident = con[:, C_ID:C_ID + P]
        ones = con[:, C_ONE:C_ONE + P]
        blk = con[:, C_BLK:C_BLK + P]
        iota = con[:, C_IOTA:C_IOTA + P]
        mask4 = con[:, C_M4:C_M4 + 512]
        zeros = gt[:, 0, :].bitcast(BF16)
        head_cols = con[:, C_BLK:C_BLK + P:HD]

        gh, gl = xh[:, 0:4, :], xl[:, 0:4, :]

        def area(a, n, *shape):
            v = arena[:, a:a + n]
            if len(shape) == 2:
                return v.rearrange("p (a b) -> p a b", b=shape[1])
            if len(shape) == 3:
                return v.rearrange("p (a b c) -> p a b c", b=shape[1], c=shape[2])
            return v

        gates = area(0, 4096, 16, T)
        oh = nc.alloc_sbuf_tensor_at("oh", [P, KT, T], F32R, offset=arena_at + 4 * 4096)
        ol = nc.alloc_sbuf_tensor_at("ol", [P, KT, T], F32R, offset=arena_at + 4 * 6144)
        R0 = 8192
        pT = area(R0, 28 * T, 28, T)
        xin = area(R0 + 8192, 2048, NT, D)
        sq = area(R0 + 10240, 2048, KT, T)
        xn = area(R0 + 15360, 2048, KT, T)
        q0, k0, v0 = NB_R, NB_R + CT, NB_R + 2 * CT
        Sb = area(0, 3072, HEADS, 384)
        vtokA = area(5120, 1024, NT, W)
        PT2 = area(7168, 1024, HEADS, P)
        PT01 = hot[:].rearrange("p a b c d -> p (a b c d)").rearrange("p (h k) -> p h k", h=HEADS)
        mix = area(R0 + 17408, 3840, NMIX, T)
        rowsb = area(R0 + 21248, 512)
        lwa = area(R0 + 21760, 512)
        lg0 = area(R0 + 22272, 512)
        lg1 = area(R0 + 22784, 512)
        bonehot = area(R0 + 23296, 512)
        relb = area(R0 + 23808, 8)

        def slot(n):
            return area(R0 + 1024 * n, 1024, CT, T)
        gB, bonus, bh, kh, vtok = slot(0), slot(1), slot(4), slot(5), area(R0 + 6144, 1024, NT, W)
        KR = area(R0 + 2048, 2048, CT, 2, T)
        tokk = area(R0 + 7168, 512)
        tokb = area(R0 + 7680, 512)
        lw, aB = slot(8), slot(9)
        Lz = area(R0 + 10240, CT * 257, CT, 257)
        E = area(R0 + 12288, CT * 2 * 129, CT, 2, 129)
        EI, kk, k2 = slot(14), slot(15), slot(16)
        rB, kB, vB = mix[:, 0:4], mix[:, 4:8], mix[:, 8:12]
        tmp = area(R0 + 23296, 1024, CT, T)
        mats = area(R0 + 8192, 8192, 16, 4, P)
        X = area(R0 + 16384, 2048, 16, P)
        XT = area(R0 + 18432, 2048, 16, P)
        P1 = area(R0 + 20480, 2048, 16, P)
        Gs = area(R0 + 22528, 512)
        nSK = area(R0 + 23040, 1024, 2, 512)
        ST = area(R0 + 24064, 256, CT, HD)
        tmp_flat, osb_flat = area(R0 + 23296, 1024), area(R0 + 16384, 1024)
        osb, ocen, osq = area(R0 + 16384, 1024, CT, T), area(R0 + 17408, 1024, CT, T), area(R0 + 18432, 1024, CT, T)
        coef = area(0, P * T, P, T)
        qT = area(16384, 4096, 16, T)
        subk = area(20480, 2048, 16, P)
        S = area(22528, 4096, 2, 16, P)
        tv = area(26624, 512, 2, 256)
        ti = area(27136, 512, 2, 256).bitcast(U32)
        tif = area(27648, 512, 2, 256)
        cand = area(28160, 2048, HEADS, 256)
        eqt = area(30208, 2048, P, TOPK)
        bp = area(32256, 128).bitcast(U32)
        bpa = area(32384, 128).bitcast(U32)
        bpf = area(32512, 128)
        gain_all = hot[:].rearrange("p a b c d -> p (a b c d)")[:, 0:D]
        result = area(16384, 2048, NT, D)
        bvs, i1s, i2s = (con[:, C_M4 + 256 * n:C_M4 + 256 * n + 256].rearrange("p (a b) -> p a b", b=P)
                         for n in range(3))

        def bcast4(a):
            return con[:, a:a + P].unsqueeze(1).to_broadcast([P, 4, P])

        landed = [sem(f"unit_landed{j}") for j in range(RAW)]
        hi_made = sem("hi_made")
        lo_dve = sem("lo_made_by_vector")
        lo_pool = sem("lo_made_by_gpsimd")
        unit_done = sem("unit_multiplied")
        act_evac = sem("act_evacuated")
        dve_evac = sem("dve_evacuated")
        dve_step = sem("dve_step")
        pe_step = sem("pe_step")
        act_step = sem("act_step")
        const_in, mask_in = sem("const_in"), sem("mask_in")
        x_in = sem("x_in")
        xt_ps, xt_sb = sem("xt_ps"), sem("xt_sb")
        sq_made, ss_made, rms_ps, scaled = sem("sq_made"), sem("ss_made"), sem("rms_spread"), sem("scaled")
        xh_made, xl_dve, xl_pool = sem("xh_made"), sem("xl_made_by_vector"), sem("xl_made_by_gpsimd")
        inv_made, root_made = sem("inverse_made"), sem("root_made")
        kk_root, gn_inv, gn_root = sem("kk_root"), sem("gn_inverse"), sem("gn_root")
        kk_inv, kk_ps, kk_used, gn_ps = sem("kk_inverse"), sem("kk_spread"), sem("kk_used"), sem("gn_spread")
        gn_wide = sem("gn_wide")
        lora_in = sem("lora_in")
        rows_ps, rows_sb, rows_out, bias_in = sem("rows_ps"), sem("rows_sb"), sem("rows_out"), sem("bias_in")
        vA_ps, vA_sb = sem("vA_ps"), sem("vA_sb")
        sc_ps, sc_sb, sc_max, sc_exp, p_made = sem("sc_ps"), sem("sc_sb"), sem("sc_max"), sem("sc_exp"), sem("p_made")
        pt_ps, pt_sb, oa_ps, oa_made = sem("pt_ps"), sem("pt_sb"), sem("oa_ps"), sem("oa_made")
        mix_made, lor_act, lor_ps, lor_sb, lor_g = (sem("mix_made"), sem("lora_act"), sem("lora_ps"), sem("lora_sb"),
                                                    sem("lora_g_sb"))
        mid_made, e_made, kk_sq, kk_ss = sem("mid_made"), sem("e_made"), sem("kk_sq"), sem("kk_ss")
        rkv_made, bon_ps, tok_ps, tok_sb = sem("rkv_made"), sem("bonus_ps"), sem("tok_ps"), sem("tok_sb")
        bon_made = sem("bonus_made")
        mat_ps, mat_sb, m1_ps, m1_sb = sem("mat_ps"), sem("mat_sb"), sem("m1_ps"), sem("m1_sb")
        flip_ps, flip_sb = sem("flip_ps"), sem("flip_sb")
        xt_masked, xt_made = sem("xt_masked"), sem("xt_made")
        p1_ps, p1_sb, x_ps, x_sb = sem("p1_ps"), sem("p1_sb"), sem("x_ps"), sem("x_sb")
        g_ps, g_sb, sk_ps, sk_sb, st_ps, st_sb = (sem("g_ps"), sem("g_sb"), sem("sk_ps"), sem("sk_sb"), sem("st_ps"),
                                                  sem("st_sb"))
        o_ps, o_sb, mu_ps, cen_sb, var_ps, ob_made = (sem("o_ps"), sem("o_sb"), sem("mu_ps"), sem("cen_sb"),
                                                      sem("var_ps"), sem("ob_made"))
        y_made, h_made = sem("y_made"), sem("h_made")
        subk_in, score_ps, score_sb = sem("subk_in"), sem("score_ps"), sem("score_sb")
        shift_made, exp_made, picks_made, picks_ps, picks_sb = (sem("shift_made"), sem("exp_made"), sem("picks_made"),
                                                                sem("picks_ps"), sem("picks_sb"))
        hot_made = sem("hot_made")
        hot_ps = sem("gates_made")
        gates_used = sem("gates_used")
        coef_made = sem("coef_made")
        gh_made, gl_made, acc_done = sem("gh_made"), sem("gl_made"), sem("acc_done")
        zero_made, gain_in = sem("zero_made"), sem("gain_in")
        fin_sq, fin_inv, fin_root, fin_sb, stored = (sem("fin_sq"), sem("fin_inverse"), sem("fin_root"),
                                                     sem("fin_sb"), sem("stored"))

        U_PROJ = NB_IN + NB_GATE
        U_OUT = U_PROJ + KT
        U_Q = U_OUT + KT
        U_U = U_Q + 2 * HEADS
        U_V = U_U + NKEYS

        block = ctx.enter_context(nc.Block())

        @block.sync
        def _(sp):
            def load(src, j):
                sp.dma_start(raw[:, j, :], src).then_inc(landed[j], 16)

            sp.dma_start(con[:, 0:C_M4], consts[:, 0:C_M4]).then_inc(const_in, 16)
            for n in range(NT):
                sp.dma_start(xin[:, n, :], x[P * n:P * n + P, :]).then_inc(x_in, 16)
            sp.dma_start(vec[:], vecs).then_inc(const_in, 16)
            for j in range(RAW):
                load(w_in[j], j)
            sp.dma_start(con[:, C_M4:NCONST], consts[:, C_M4:NCONST]).then_inc(mask_in, 16)
            sp.wait_ge(dve_step, REL_ROW)
            for dst, src in ((bonehot[0:33], bucket_onehot), (relb[0:32, 0:8], rel_bias_t), (lwa, lora_wa),
                             (lg0, lora_g[0:P]), (lg1[0:GLORA - P], lora_g[P:GLORA])):
                sp.dma_start(dst, src).then_inc(lora_in, 16)
            for g in range(RAW, 5 * RAW):
                sp.wait_ge(unit_done, g - 3)
                load(w_in[g], g % 4)
                h = g - 5
                if h == 0:
                    sp.wait_ge(rows_sb, 1)
                if 0 <= h < HEADS:
                    sp.dma_start(bias_dram[h:h + 1], rowsb[h:h + 1, :].unsqueeze(1).to_broadcast([1, P, 512])
                                 ).then_inc(rows_out, 16)
                q = g - 14
                if q == 0:
                    sp.wait_ge(rows_out, 16 * HEADS)
                if 0 <= q < 4:
                    h0, qt = 4 * (q // 2), q % 2
                    src = bass.AP(bias_dram.tensor, 512 * P * h0 + T - 1 - qt * P, [[511, P], [512 * P, 4],
                                                                                   [1, P + P * qt]])
                    sp.dma_start(Sb[:, h0:h0 + 4, P * qt:P * qt + P + P * qt], src).then_inc(bias_in, 16)
            with sp.Fori(5, U_PROJ // 4) as i:
                for j in range(RAW):
                    sp.wait_ge(unit_done, 4 * i + (j - 3))
                    load(w_in[4 * i + j], j)
            for g in range(U_PROJ, U_OUT):
                sp.wait_ge(unit_done, g - 3)
                load(w_proj[g - U_PROJ], g % 4)
            for g in range(U_OUT, U_Q):
                sp.wait_ge(unit_done, g - 3)
                load(w_out[g - U_OUT], g % 4)
            for j in range(RAW):
                sp.wait_ge(unit_done, U_Q + j - 3)
                load(w_q[j], j)
            sp.wait_ge(h_made, 8)
            sp.dma_start(subk, subkeys_t).then_inc(subk_in, 16)
            with sp.Fori(1, 4) as i:
                for j in range(RAW):
                    sp.wait_ge(unit_done, 4 * i + (U_Q + j - 3))
                    load(w_q[4 * i + j], j)
            for j in range(RAW):
                sp.wait_ge(unit_done, U_U + j - 3)
                load(u_t[j], j)
            with sp.Fori(1, 32) as i:
                for j in range(RAW):
                    sp.wait_ge(unit_done, 4 * i + (U_U + j - 3))
                    load(u_t[4 * i + j], j)
            for j in range(RAW):
                sp.wait_ge(unit_done, U_V + j - 3)
                load(v_t[j], j)
            sp.wait_ge(coef_made, HALF + 2)
            sp.dma_start(gain_all, gain_row.to_broadcast([P, D])).then_inc(gain_in, 16)
            with sp.Fori(1, 32) as i:
                for j in range(RAW):
                    sp.wait_ge(unit_done, 4 * i + (U_V + j - 3))
                    load(v_t[4 * i + j], j)
            for n in range(4):
                sp.wait_ge(fin_sb, n + 1)
                sp.dma_start(out.rearrange("(n p) d -> n p d", p=P)[n // 2, :, 512 * (n % 2):512 * (n % 2) + 512],
                             result[:, n // 2, 512 * (n % 2):512 * (n % 2) + 512]).then_inc(stored, 16)
            sp.wait_ge(stored, 64)

        @block.tensor
        def _(pe):
            mm = nc.tensor.matmul

            LO_DVE_SKIP = U_OUT + 4 - NB_R

            def splits_ready(g, lo_sem, lo_count):
                pe.wait_ge(hi_made, g + 1)
                pe.wait_ge(lo_sem, lo_count)

            def product(ps, s, mh, ml, k0=0, k1=KT, tile_ready=None):
                for k in range(k0, k1):
                    if tile_ready:
                        tile_ready(k)
                    c = slice(P * k, P * k + P)
                    mm(ps, hi[:, s, c], mh[:, k, :], start=(k == k0), stop=False)
                    mm(ps, hi[:, s, c], ml[:, k, :], start=False, stop=False)
                    last = mm(ps, lo[:, s, c], mh[:, k, :], start=False, stop=(k == k1 - 1))
                return last

            def spread_rms(n):
                pe.wait_ge(root_made, n + 1)
                for t in range(NT):
                    last = mm(PS[:, 2, P * t:P * t + P], rms[:, t:t + 1].to_broadcast([P, P]), ident, start=True,
                              stop=True)
                last.then_inc(rms_ps, 1)

            def low_part_made(n):
                def wait(k):
                    if k < XL_POOL:
                        pe.wait_ge(xl_pool, XL_POOL * n + k + 1)
                    else:
                        pe.wait_ge(xl_dve, (KT - XL_POOL) * n + k - XL_POOL + 1)
                return wait

            pe.sem_inc(act_evac, 2)
            pe.sem_inc(hot_ps, 2)
            pe.wait_ge(x_in, 32)
            pe.wait_ge(const_in, 32)
            for b in range(4):
                for c in range(4):
                    k, n = 2 * b + c // 2, c % 2
                    last = nc.tensor.transpose(PS[:, 4 + b, P * c:P * c + P], xin[:, n, P * k:P * k + P], ident)
                last.then_inc(xt_ps, 1)
            spread_rms(0)
            def first_unit(i, j, tile_ready=None):
                splits_ready(4 * i + j, lo_dve, 4 * i + (j + 1))
                pe.wait_ge(act_evac, 4 * i + (j + 1))
                product(PS[:, j % 2, 0:T], j, xh, xl, tile_ready=tile_ready).then_inc(unit_done, 1)

            first_unit(0, 0, low_part_made(0))
            pe.wait_ge(lora_in, 80)
            pe.wait_ge(dve_step, REL_ROW)
            mm(PS[0:8, 3, :], relb[0:33, 0:8], bonehot[0:33, :], start=True, stop=True).then_inc(rows_ps, 1)
            for j in range(1, 4):
                first_unit(0, j)
            with pe.Fori(1, NB_R // 4) as i:
                for j in range(4):
                    first_unit(i, j)

            def in_unit(i, j):
                splits_ready(4 * i + j, lo_pool, 4 * i + (j + 1 - NB_R))
                pe.wait_ge(act_evac, 4 * i + (j + 1))
                product(PS[:, j % 2, 0:T], j, xh, xl).then_inc(unit_done, 1)

            def units(*gs):
                for g in gs:
                    in_unit(g // 4, g % 4)

            units(16, 17, 18, 19, 20, 21)
            pe.wait_ge(lor_act, 3)
            pe.wait_ge(rows_sb, 1)
            for c in range(CT):
                col = slice(P * c, P * c + P)
                b = 2 + 3 * (c % 2)
                if c >= 2:
                    pe.wait_ge(lor_sb, 2 * c - 2)
                    pe.wait_ge(lor_g, c - 1)
                mm(PS[:, b, 0:T], lwa[0:LORA, col], mix[0:LORA, 12, :], start=True, stop=True)
                mm(PS[:, b + 1, 0:T], lwa[LORA:P, col], mix[LORA:P, 12, :], start=True, stop=True)
                mm(PS[:, b + 2, 0:T], lg0[:, col], mix[:, 13, :], start=True, stop=False)
                mm(PS[:, b + 2, 0:T], lg1[0:32, col], mix[0:32, 14, :], start=False, stop=True).then_inc(lor_ps, 1)
            units(22, 23)

            def head_sums(bank, src):
                for n in range(NT):
                    for c in range(CT):
                        a = 8 * n + 2 * c
                        last = mm(PS[:, bank, a:a + 2], src[:, c, P * n:P * n + P], head_cols, start=True, stop=True)
                return last

            def spread_heads(bank, scale):
                for c in range(CT):
                    for n in range(NT):
                        a = 8 * n + 2 * c
                        b = T * (c % 2) + P * n
                        last = mm(PS[:, bank + c // 2, b:b + P], scale[:, HD * a:HD * a + P], ident, start=True,
                                  stop=True)
                return last

            pe.wait_ge(kk_sq, 1)
            pe.wait_ge(lor_sb, 2 * CT)
            pe.wait_ge(lor_g, CT)
            head_sums(2, tmp).then_inc(kk_ss, 1)
            units(24, 25)
            pe.wait_ge(kk_inv, 1)
            spread_heads(2, tmp_flat).then_inc(kk_ps, 1)
            units(26, 27)
            pe.wait_ge(act_evac, 2 + NB_IN)
            for n in range(NT):
                for c in range(CT):
                    last = nc.tensor.transpose(PS[:, 4 + n, P * c:P * c + P], pT[:, v0 + c, P * n:P * n + P], ident)
                last.then_inc(vA_ps, 1)
            for h in range(HEADS):
                b, c = HD * (h % 2), h // 2
                bank = S_BANKS[h % 4]
                if h == 2:
                    pe.wait_ge(kk_used, 1)
                if h >= 4:
                    pe.wait_ge(sc_sb, h - 3)
                mm(PS[:, bank, 0:P], pT[b:b + HD, q0 + c, 0:P], pT[b:b + HD, k0 + c, 0:P], start=True, stop=True)
                mm(PS[:, bank, P:P + T], pT[b:b + HD, q0 + c, P:T], pT[b:b + HD, k0 + c, :], start=True,
                   stop=True).then_inc(sc_ps, 1)
            units(28, 29, 30, 31)
            pe.wait_ge(rkv_made, 1)
            pe.wait_ge(vA_sb, 2)
            for c in range(CT):
                last = mm(PS[:, 4 + c // 2, T * (c % 2):T * (c % 2) + T], blk, lw[:, c, :], start=True, stop=True)
            last.then_inc(bon_ps, 1)
            pe.wait_ge(rkv_made, 2)
            pe.wait_ge(sc_sb, HEADS)
            for bank, src, n in ((6, vB, 0), (7, vB, 1), (2, kh, 0), (3, bh, 0)):
                for c in range(CT):
                    last = nc.tensor.transpose(PS[:, bank, P * c:P * c + P], src[:, c, P * n:P * n + P], ident)
                last.then_inc(tok_ps, 1)
            pe.wait_ge(tok_sb, 4)
            pe.wait_ge(bon_made, 1)
            for m in range(16):
                n, b, c = chunk_head(m)
                t = slice(P * n, P * n + P)
                if m >= 4:
                    pe.wait_ge(mat_sb, m - 3)
                mm(PS[:, 4 + m % 4, 0:T], kh[b:b + HD, c, t], KR[b:b + HD, c, :, t], start=True, stop=True)
                mm(PS[:, 4 + m % 4, T:2 * T], bh[b:b + HD, c, t], KR[b:b + HD, c, :, t], start=True,
                   stop=True).then_inc(mat_ps, 1)
            pe.wait_ge(mat_sb, 16)
            for m in range(16):
                n, b, c = chunk_head(m)
                t = slice(P * n, P * n + P)
                last = mm(PS[:, 4 + m // 4, P * (m % 4):P * (m % 4) + P], KR[b:b + HD, c, 0, t], bh[b:b + HD, c, t],
                          start=True, stop=True)
                if m % 4 == 3:
                    last.then_inc(m1_ps, 1)
            pe.wait_ge(p_made, 2)
            pe.wait_ge(act_evac, 2 + NB_IN + 4)
            for h in range(HEADS):
                if h >= 4:
                    pe.wait_ge(pt_sb, 2 * (h - 3))
                for n in range(3):
                    last = nc.tensor.transpose(PS[:, h % 4, P * n:P * n + P], Sb[:, h, P * n:P * n + P], ident)
                last.then_inc(pt_ps, 1)
            pe.wait_ge(pt_sb, 2 * HEADS)
            for h in range(HEADS):
                b, c = HD * (h % 2), h // 2
                o = PS[b:b + HD, 2 + c // 2, T * (c % 2):T * (c % 2) + T]
                mm(o, vtokA[:, 0, HD * h:HD * h + HD], PT01[:, h, :], start=True, stop=False)
                last = mm(o[:, P:T], vtokA[:, 1, HD * h:HD * h + HD], PT2[:, h, :], start=False, stop=True)
                if h % 4 == 3:
                    last.then_inc(oa_ps, 1)
            units(32, 33, 34)
            pe.wait_ge(act_evac, 2 + 35)
            pe.wait_ge(oa_made, 2)
            for lv in range(len(LEVELS)):
                for q in range(4):
                    if lv == 0:
                        pe.wait_ge(m1_sb, 4)
                        pe.wait_ge(xt_made, 4)
                    else:
                        pe.wait_ge(flip_sb, 4 * (lv - 1) + q + 1)
                    for m in range(4 * q, 4 * q + 4):
                        last = mm(PS[:, q, P * (m % 4):P * (m % 4) + P], mats[:, m, 2, :], X[:, m, :], start=True,
                                  stop=True)
                    last.then_inc(p1_ps, 1)
                for q in range(4):
                    pe.wait_ge(p1_sb, 4 * lv + q + 1)
                    final = lv == len(LEVELS) - 1
                    for m in range(4):
                        a = 4 * q + m
                        stationary, moving = (P1[:, a, :], XT[:, a, :]) if final else (XT[:, a, :], P1[:, a, :])
                        last = mm(PS[:, 4 + q, P * m:P * m + P], stationary, moving, start=True, stop=True)
                    last.then_inc(x_ps, 1)
                for q in range(4):
                    if not final:
                        pe.wait_ge(x_sb, 4 * lv + q + 1)
                        for m in range(4):
                            last = nc.tensor.transpose(PS[:, q, P * m:P * m + P], X[:, 4 * q + m, :], ident)
                        last.then_inc(flip_ps, 1)
            pe.wait_ge(x_sb, 4 * len(LEVELS))
            for n in range(NT):
                if n:
                    pe.wait_ge(st_sb, 1)
                for m in range(8 * n, 8 * n + 8):
                    _, b, c = chunk_head(m)
                    o = PS[:, 2 + b // HD, HD * c:HD * c + HD]
                    hs = slice(P * c + b, P * c + b + HD)
                    last = mm(o, mats[:, m, 0, :], vtok[:, n, hs], start=True, stop=(n == 0))
                    if n:
                        last = mm(o, KR[b:b + HD, c, 0, P:T], ST[b:b + HD, c, :], start=False, stop=True)
                last.then_inc(g_ps, 1)
                units(35 + 3 * n)
                pe.wait_ge(g_sb, n + 1)
                for m in range(8):
                    last = mm(PS[:, 4, HD * m:HD * m + HD], XT[:, 8 * n + m, :], Gs[:, HD * m:HD * m + HD],
                              start=True, stop=True)
                last.then_inc(sk_ps, 1)
                units(36 + 3 * n)
                pe.wait_ge(sk_sb, n + 1)
                if n == 0:
                    for m in range(8):
                        _, b, c = chunk_head(m)
                        hs = slice(P * c + b, P * c + b + HD)
                        o = PS[b:b + HD, 5, HD * c:HD * c + HD]
                        mm(o, tokk[:, hs], vtok[:, 0, hs], start=True, stop=False)
                        last = mm(o, tokb[:, hs], nSK[:, 0, HD * m:HD * m + HD], start=False, stop=True)
                    last.then_inc(st_ps, 1)
                    units(37)
            for h in range(8):
                for n in range(NT):
                    m = 8 * n + h
                    _, b, c = chunk_head(m)
                    hs = slice(P * c + b, P * c + b + HD)
                    o = PS[b:b + HD, 6 + c // 2, T * (c % 2) + P * n:T * (c % 2) + P * n + P]
                    mm(o, vtok[:, n, hs], mats[:, m, 1, :], start=True, stop=False)
                    last = mm(o, nSK[:, n, HD * h:HD * h + HD], mats[:, m, 3, :], start=False, stop=(n == 0))
                    if n:
                        last = mm(o, ST[b:b + HD, c, :], KR[b:b + HD, c, 1, P:T], start=False, stop=True)
            last.then_inc(o_ps, 1)
            units(40)
            pe.wait_ge(o_sb, 1)
            for c in range(CT):
                last = mm(PS[:, 2 + c // 2, T * (c % 2):T * (c % 2) + T], blk, osb[:, c, :], start=True, stop=True)
            last.then_inc(mu_ps, 1)
            units(41)
            pe.wait_ge(cen_sb, 1)
            head_sums(4, osq).then_inc(var_ps, 1)
            units(42)
            pe.wait_ge(gn_wide, 1)
            spread_heads(5, osb_flat).then_inc(gn_ps, 1)
            units(43)
            evacs = U_PROJ
            pe.wait_ge(act_evac, 2 + evacs)
            for g in range(U_PROJ, U_OUT):
                splits_ready(g, lo_pool, g + 1 - NB_R)
                if g >= U_PROJ + 2:
                    pe.wait_ge(dve_evac, g - U_PROJ - 1)
                product(PS[:, g % 2, 0:T], g % 4, oh, ol, 0, 4)
                pe.wait_ge(ob_made, 1)
                product(PS[:, g % 2, T:2 * T], g % 4, oh, ol, 4, 8).then_inc(unit_done, 1)
            def sum_squares(k):
                pe.wait_ge(sq_made, k + 1)
                for t in range(NT):
                    last = mm(PS[:, 2 + t, 0:1], sq[:, k, P * t:P * t + P], ones[:, 0:1], start=(k == 0),
                              stop=(k == KT - 1))
                return last

            for g in range(U_OUT, U_Q):
                splits_ready(g, *((lo_pool, g + 1 - NB_R) if g < U_OUT + 4 else (lo_dve, g + 1 - LO_DVE_SKIP)))
                if g >= U_OUT + 2:
                    pe.wait_ge(h_made, g - U_OUT - 1)
                else:
                    pe.wait_ge(dve_evac, g - U_PROJ - 1)
                product(PS[:, g % 2, 0:T], g % 4, xh, xl,
                        tile_ready=(lambda k: pe.wait_ge(y_made, k + 1)) if g == U_OUT else None
                        ).then_inc(unit_done, 1)
                if g >= U_OUT + 2:
                    sum_squares(g - U_OUT - 2)
            sum_squares(KT - 2)
            sum_squares(KT - 1).then_inc(ss_made, 1)
            spread_rms(1)

            def query_unit(i, j, tile_ready=None):
                splits_ready(4 * i + (U_Q + j), lo_dve, 4 * i + (U_Q + j + 1 - LO_DVE_SKIP))
                pe.wait_ge(act_evac, 4 * i + (U_PROJ + j + 1))
                product(PS[:, j % 2, 0:T], j, xh, xl, tile_ready=tile_ready).then_inc(unit_done, 1)

            for j in range(4):
                query_unit(0, j, None if j else low_part_made(1))
            with pe.Fori(1, 4) as i:
                for j in range(4):
                    query_unit(i, j)
            evacs += U_U - U_Q
            pe.wait_ge(act_evac, evacs + 2)
            pe.wait_ge(subk_in, 16)
            for m in range(8):
                n, q = m // 4, m % 4
                if m >= 4:
                    pe.wait_ge(score_sb, m - 3)
                for u in range(4 * q, 4 * q + 4):
                    last = mm(PS[:, 4 + m % 4, P * (u % 4):P * (u % 4) + P], qT[:, u, P * n:P * n + P], subk[:, u, :],
                              start=True, stop=True)
                last.then_inc(score_ps, 1)
            def expert_unit(i, j):
                splits_ready(4 * i + (U_U + j), lo_pool, 4 * i + (U_OUT + 4 - NB_R + j + 1))
                pe.wait_ge(act_evac, 4 * i + (evacs + j + 1))
                product(PS[:, j % 2, 0:T], j, xh, xl).then_inc(unit_done, 1)

            with pe.Fori(0, PICKS_AT + 1) as i:
                for j in range(4):
                    expert_unit(i, j)
            pe.wait_ge(picks_made, 1)
            pe.wait_ge(score_sb, 8)
            for b, src in ((2, i1s), (3, i2s), (4, bvs)):
                for n in range(NT):
                    last = nc.tensor.transpose(PS[:, b, P * n:P * n + P], src[:, n, :], ident)
                last.then_inc(picks_ps, 1)
            with pe.Fori(PICKS_AT + 1, HALF // 4) as i:
                for j in range(4):
                    expert_unit(i, j)
            pe.wait_ge(picks_sb, 3)
            with pe.Fori(HALF // 4, NKEYS // 4) as i:
                for j in range(4):
                    expert_unit(i, j)
                    n = 4 * i + (j - HALF)
                    pe.wait_ge(hot_made, n + 1)
                    pe.wait_ge(gates_used, n + 1)
                    for k in range(4):
                        last = mm(PS[:, 2 + j % 2, P * k:P * k + P], oh1[:, j % 2, k, :], oh2[:, j % 2, k, :],
                                  start=True, stop=True)
                    last.then_inc(hot_ps, 1)
            evacs += NKEYS
            pe.wait_ge(act_evac, evacs + 2)
            pe.wait_ge(gates_used, HALF + 2)
            pe.wait_ge(zero_made, 1)
            for b in range(4):
                mm(PS[:, b, :], zeros[:, 0:P], zeros, start=True, stop=False, skip_group_check=True)
                for k in range(4 * (b % 2), 4 * (b % 2) + 4):
                    c = P * (k % 4)
                    mm(PS[:, b, c:c + P], xT[:, k, P * (b // 2):P * (b // 2) + P], ident, start=False, stop=False,
                       skip_group_check=True)
            with pe.Fori(0, NKEYS // 4) as i:
                for j in range(4):
                    splits_ready(4 * i + (U_V + j), lo_dve, 4 * i + (U_V + j + 1 - LO_DVE_SKIP - NKEYS))
                    pe.wait_ge(gh_made, 4 * i + (j + 1))
                    pe.wait_ge(gl_made, 4 * i + (j + 1))
                    for b in range(4):
                        o = PS[:, b, :]
                        t = slice(P * (b // 2), P * (b // 2) + P)
                        c = slice(512 * (b % 2), 512 * (b % 2) + 512)
                        mm(o, gh[:, j, t], hi[:, j, c], start=False, stop=False, skip_group_check=True)
                        mm(o, gl[:, j, t], hi[:, j, c], start=False, stop=False, skip_group_check=True)
                        last = mm(o, gh[:, j, t], lo[:, j, c], start=False, stop=False, skip_group_check=True)
                    last.then_inc(unit_done, 1)
            for b in range(4):
                mm(PS[:, b, :], zeros[:, 0:P], zeros, start=False, stop=True,
                   skip_group_check=True).then_inc(acc_done, 1)

        @block.scalar
        def _(act):
            def make_hi(G, j):
                act.wait_ge(landed[j], 16 * G + 16)
                nc.scalar.copy(hi[:, j, :], raw[:, j, :]).then_inc(hi_made, 1)

            def next_hi(G, j):
                make_hi(G if j < 2 else G + 1, (j + 2) % 4)

            def rms_root(n):
                act.wait_ge(inv_made, n + 1)
                nc.scalar.activation(rms[:, 0:2], rms[:, 0:2], ACT.Sqrt).then_inc(root_made, 1)

            def operand_high(n):
                for k in range(KT):
                    act.wait_ge(scaled, KT * n + k + 1)
                    nc.scalar.copy(xh[:, k, :], xn[:, k, :]).then_inc(xh_made, 1)

            nc.scalar.preload_act_table(ACT.Sqrt)
            act.wait_ge(x_in, 32)
            for n in range(NT):
                nc.scalar.activation(sq.rearrange("p a b -> p (a b)")[:, D * n:D * n + D], xin[:, n, :], ACT.Square,
                                     accum_out=rms[:, n:n + 1]).then_inc(ss_made, 1)
            make_hi(0, 0)
            rms_root(0)
            operand_high(0)
            make_hi(0, 1)
            def in_evac(i, j):
                next_hi(i, j)
                act.wait_ge(unit_done, 4 * i + (j + 1))
                nc.scalar.copy(pT[:, 4 * i + j, :], PS[:, j % 2, 0:T]).then_inc(act_evac, 1)

            def gate_evac(*gs):
                for g in gs:
                    next_hi(g // 4, g % 4)
                    act.wait_ge(unit_done, g + 1)
                    nc.scalar.activation(gates[:, (g - NB_IN - 4) % NB_GATE, :], PS[:, g % 2, 0:T],
                                         ACT.Sigmoid).then_inc(act_evac, 1)

            in_evac(0, 0)
            act.wait_ge(rows_ps, 1)
            nc.scalar.copy(rowsb[0:HEADS, :], PS[0:HEADS, 3, :]).then_inc(rows_sb, 1)
            for j in range(1, 4):
                in_evac(0, j)
            with act.Fori(1, NB_R // 4 + 1) as i:
                for j in range(4):
                    in_evac(i, j)
            act.wait_ge(mix_made, 1)
            nc.scalar.activation(mix[0:LORA, 12, :], mix[0:LORA, 12, :], ACT.Tanh).then_inc(lor_act, 1)
            nc.scalar.activation(mix[:, 13, :], mix[:, 13, :], ACT.Sigmoid).then_inc(lor_act, 1)
            nc.scalar.activation(mix[0:32, 14, :], mix[0:32, 14, :], ACT.Sigmoid).then_inc(lor_act, 1)
            for j in range(2):
                in_evac(NB_R // 4 + 1, j)
            for c in range(CT):
                b = 2 + 3 * (c % 2)
                act.wait_ge(lor_ps, c + 1)
                nc.scalar.activation(lw[:, c, :], PS[:, b, 0:T], ACT.Sigmoid,
                                     bias=vec[:, V_W0 + c:V_W0 + c + 1]).then_inc(lor_sb, 1)
                nc.scalar.activation(aB[:, c, :], PS[:, b + 1, 0:T], ACT.Sigmoid,
                                     bias=vec[:, V_A0 + c:V_A0 + c + 1]).then_inc(lor_sb, 1)
                nc.scalar.copy(gB[:, c, :], PS[:, b + 2, 0:T]).then_inc(lor_g, 1)
            in_evac(5, 2)
            in_evac(5, 3)
            act.wait_ge(kk_ss, 1)
            nc.scalar.activation(kk_scale, PS[:, 2, 0:16], ACT.Sqrt).then_inc(kk_root, 1)
            for j in range(4):
                in_evac(6, j)
            act.wait_ge(mid_made, 1)
            for c in range(CT):
                for n in range(NT):
                    m = 32 + 2 * c + n
                    nc.scalar.activation(E[:, c, n, :], Lz[:, c, P * n:P * n + P + 1], ACT.Exp,
                                         bias=small[:, m:m + 1]).then_inc(e_made, 1)
                    nc.scalar.activation(EI[:, c, P * n:P * n + P], Lz[:, c, P * n + 1:P * n + P + 1], ACT.Exp,
                                         bias=small[:, m + 8:m + 9], scale=-1.0).then_inc(e_made, 1)
            nc.scalar.activation(small[:, 48:52], small[:, 52:56], ACT.Exp).then_inc(e_made, 1)
            for n in range(NT):
                act.wait_ge(vA_ps, n + 1)
                nc.scalar.copy(vtokA[:, n, :], PS[:, 4 + n, :]).then_inc(vA_sb, 1)
            gate_evac(28, 29, 30, 31)
            for n, dst in enumerate((vtok[:, 0, :], vtok[:, 1, :], tokk, tokb)):
                act.wait_ge(tok_ps, n + 1)
                nc.scalar.copy(dst, PS[:, (6, 7, 2, 3)[n], :]).then_inc(tok_sb, 1)
            act.wait_ge(sc_max, 2)
            for h in range(HEADS):
                for n, a, b in ((0, 0, P), (1, P, P + T)):
                    nc.scalar.activation(Sb[:, h, a:b], Sb[:, h, a:b], ACT.Exp, bias=small[:, 8 * n + h:8 * n + h + 1],
                                         accum_out=small[:, 16 + 8 * n + h:17 + 8 * n + h]).then_inc(sc_exp, 1)
            for h in range(HEADS):
                act.wait_ge(pt_ps, h + 1)
                nc.scalar.copy(PT01[:, h, :], PS[:, h % 4, 0:T]).then_inc(pt_sb, 1)
                nc.scalar.copy(PT2[:, h, :], PS[:, h % 4, T:T + P]).then_inc(pt_sb, 1)
            gate_evac(32, 33, 34)
            for n in range(4 * len(LEVELS) - 4):
                act.wait_ge(flip_ps, n + 1)
                q = n % 4
                nc.scalar.copy(XT[:, 4 * q:4 * q + 4, :].rearrange("p a b -> p (a b)"), PS[:, q, :]).then_inc(flip_sb, 1)
            gate_evac(*range(35, 42))
            act.wait_ge(gn_inv, 1)
            nc.scalar.activation(gn_scale, gn_scale, ACT.Sqrt).then_inc(gn_root, 1)
            gate_evac(42, 43)
            for g in range(U_PROJ, U_Q):
                next_hi(g // 4, g % 4)
            nc.scalar.preload_act_table(ACT.Sqrt)
            rms_root(1)
            operand_high(1)
            with act.Fori(0, 4) as i:
                for j in range(4):
                    next_hi(i + U_Q // 4, j)
                    act.wait_ge(unit_done, 4 * i + (U_Q + j + 1))
                    nc.scalar.copy(qT[:, 4 * i + j, :], PS[:, j % 2, 0:T]).then_inc(act_evac, 1)
            for m in range(8):
                act.wait_ge(score_ps, m + 1)
                nc.scalar.copy(S[:, m // 4, 4 * (m % 4):4 * (m % 4) + 4, :].rearrange("p a b -> p (a b)"),
                               PS[:, 4 + m % 4, :]).then_inc(score_sb, 1)
            nc.scalar.preload_act_table(ACT.Gelu)
            with act.Fori(0, PICKS_AT) as i:
                for j in range(4):
                    next_hi(i + U_U // 4, j)
                    act.wait_ge(unit_done, 4 * i + (U_U + j + 1))
                    nc.scalar.activation(coef[:, 4 * i + j, :], PS[:, j % 2, 0:T], ACT.Gelu).then_inc(act_evac, 1)
            act.wait_ge(shift_made, 2)
            nc.scalar.activation(bvs, bvs, ACT.Exp).then_inc(exp_made, 1)
            nc.scalar.preload_act_table(ACT.Gelu)
            with act.Fori(PICKS_AT, HALF // 4) as i:
                for j in range(4):
                    next_hi(i + U_U // 4, j)
                    act.wait_ge(unit_done, 4 * i + (U_U + j + 1))
                    nc.scalar.activation(coef[:, 4 * i + j, :], PS[:, j % 2, 0:T], ACT.Gelu).then_inc(act_evac, 1)
            with act.Fori(HALF // 4, NKEYS // 4) as i:
                for j in range(4):
                    next_hi(i + U_U // 4, j)
                    act.wait_ge(unit_done, 4 * i + (U_U + j + 1))
                    act.wait_ge(coef_made, 4 * i + (j + 1 - HALF))
                    nc.scalar.activation(gt[:, j % 2, :], PS[:, j % 2, 0:T], ACT.Gelu).then_inc(act_evac, 1)

            def make_gh(i, j):
                act.wait_ge(unit_done, 4 * i + (U_V + j - 3))
                nc.scalar.copy(gh[:, j % 4, :], coef[:, 4 * i + j, :]).then_inc(gh_made, 1)

            act.wait_ge(coef_made, HALF + 2)
            make_gh(0, 0)
            make_gh(0, 1)
            with act.Fori(0, NKEYS // 4 - 1) as i:
                for j in range(4):
                    make_gh(i, j + 2)
                    next_hi(i + U_V // 4, j)
            for j in range(2):
                make_gh(NKEYS // 4 - 1, j + 2)
                next_hi(U_V // 4 + NKEYS // 4 - 1, j)
            nc.scalar.preload_act_table(ACT.Sqrt)
            for b in range(4):
                act.wait_ge(acc_done, b + 1)
                nc.scalar.activation(sq.rearrange("p a b -> p (a b)")[:, 512 * b:512 * b + 512], PS[:, b, :], ACT.Square,
                                     accum_out=rms[:, b:b + 1]).then_inc(fin_sq, 1)
                if b >= 2:
                    act.wait_ge(fin_inv, b - 1)
                    n = b - 2
                    nc.scalar.activation(rms[:, 2 * n:2 * n + 1], rms[:, 2 * n:2 * n + 1], ACT.Sqrt
                                         ).then_inc(fin_root, 1)

        @block.gpsimd
        def _(pool):
            def make_lo(i, j):
                pool.wait_ge(hi_made, 4 * i + (j + 1))
                nc.gpsimd.tensor_tensor(lo[:, j, :], raw[:, j, :], hi[:, j, :].bitcast(F32),
                                        ALU.subtract).then_inc(lo_pool, 1)

            def operand_low(n):
                for k in range(XL_POOL):
                    pool.wait_ge(xh_made, KT * n + k + 1)
                    nc.gpsimd.tensor_tensor(xl[:, k, :], xn[:, k, :], xh[:, k, :].bitcast(F32),
                                            ALU.subtract).then_inc(xl_pool, 1)

            operand_low(0)
            with pool.Fori(NB_R // 4, NB_IN // 4 + 1) as i:
                for j in range(4):
                    make_lo(i, j)
            pool.wait_ge(mask_in, 16)
            for q in range(2):
                pool.wait_ge(mat_sb, 4 * q + 4)
                nc.gpsimd.tensor_tensor(XT[:, 4 * q:4 * q + 4, :], mats[:, 4 * q:4 * q + 4, 2, :], bcast4(C_NM1T),
                                        ALU.mult).then_inc(xt_masked, 1)
                pool.wait_ge(xt_masked, q + 1)
                nc.gpsimd.tensor_tensor(XT[:, 4 * q:4 * q + 4, :], XT[:, 4 * q:4 * q + 4, :], bcast4(C_ID),
                                        ALU.add).then_inc(xt_made, 1)
            with pool.Fori(NB_IN // 4 + 1, U_OUT // 4 + 1) as i:
                for j in range(4):
                    make_lo(i, j)
            operand_low(1)
            with pool.Fori(0, NKEYS // 4) as i:
                for j in range(4):
                    make_lo(i + U_U // 4, j)

        @block.vector
        def _(dve):
            steps = [0]

            def link(ins):
                steps[0] += 1
                ins.then_inc(dve_step, 1)
                dve.wait_ge(dve_step, steps[0])

            V = nc.vector

            def make_lo(g, j):
                dve.wait_ge(hi_made, g)
                V.tensor_tensor(lo[:, j, :], raw[:, j, :], hi[:, j, :].bitcast(F32),
                                ALU.subtract).then_inc(lo_dve, 1)

            def per_channel(a):
                return vec[:, a:a + 1]

            def rms_inverse(dst, src, inv):
                link(V.tensor_scalar(dst, src, 1.0 / D, RMS_EPS, ALU.mult, ALU.add))
                V.reciprocal(dst, dst).then_inc(inv, 1)

            def rms_scale(n, gain):
                dve.wait_ge(rms_ps, n + 1)
                for k in range(KT):
                    V.scalar_tensor_tensor(out=xn[:, k, :], in0=xT[:, k, :], scalar=per_channel(gain + k),
                                           in1=PS[:, 2, 0:T], op0=ALU.mult, op1=ALU.mult).then_inc(scaled, 1)
                for k in range(XL_POOL, KT):
                    dve.wait_ge(xh_made, KT * n + k + 1)
                    V.tensor_tensor(xl[:, k, :], xn[:, k, :], xh[:, k, :].bitcast(F32), ALU.subtract).then_inc(xl_dve, 1)

            V.memset(relb[0:64, :], NEG).then_inc(dve_step, 1)
            steps[0] += 1
            for b in range(4):
                dve.wait_ge(xt_ps, b + 1)
                V.tensor_copy(xT[:, 2 * b:2 * b + 2, :], PS[:, 4 + b, :].rearrange("p (a b) -> p a b", a=2)
                              ).then_inc(xt_sb, 1)
            dve.wait_ge(ss_made, NT)
            rms_inverse(rms[:, 0:2], rms[:, 0:2], inv_made)
            make_lo(1, 0)
            dve.wait_ge(xt_sb, 4)
            rms_scale(0, V_N1)
            for j in range(1, 4):
                make_lo(j + 1, j)
            with dve.Fori(1, NB_R // 4) as i:
                for j in range(4):
                    make_lo(4 * i + (j + 1), j)

            dve.wait_ge(act_evac, 2 + NB_R)
            m15 = pT[:, 0:NMIX, :]
            V.tensor_tensor(mix[:, :, 1:T], m15[:, :, 0:T - 1], m15[:, :, 1:T], ALU.subtract)
            link(V.tensor_scalar(mix[:, :, 0:1], m15[:, :, 0:1], -1.0, None, ALU.mult))
            for c in range(NMIX):
                last = V.scalar_tensor_tensor(out=mix[:, c, :], in0=mix[:, c, :], scalar=per_channel(V_MU + c),
                                              in1=m15[:, c, :], op0=ALU.mult, op1=ALU.add)
            last.then_inc(mix_made, 1)
            def split_out(dst0, src):
                link(V.tensor_copy(oh[:, dst0[0]:dst0[1], :], src))
                return V.tensor_tensor(ol[:, dst0[0]:dst0[1], :], src, oh[:, dst0[0]:dst0[1], :].bitcast(F32),
                                       ALU.subtract)
            dve.wait_ge(mix_made, 1)
            dve.wait_ge(rows_sb, 1)
            for c in range(CT):
                last = V.tensor_scalar(kk[:, c, :], kB[:, c, :], per_channel(V_KK + c), None, ALU.mult)
            link(last)
            V.tensor_tensor(tmp, kk, kk, ALU.mult).then_inc(kk_sq, 1)
            V.memset(E[:, :, :, :], 1.0)
            link(V.memset(Lz[:, :, 0:1], 0.0))
            dve.wait_ge(lor_sb, 2 * CT)
            link(V.tensor_scalar(lw, lw, -math.exp(-0.5), None, ALU.mult))
            for c in range(CT):
                last = V.tensor_tensor_scan(Lz[:, c, 1:T + 1], E[:, 0, 0:2, :].rearrange("p a b -> p (a b)")[:, 0:T],
                                            lw[:, c, :], 0.0, ALU.mult, ALU.add)
            link(last)
            mids = Lz[:, :, HD:HD + P + 1:P]
            sm = small[:, 32:40].rearrange("p (c n) -> p c n", n=2)
            V.tensor_scalar(sm, mids, -1.0, None, ALU.mult)
            V.tensor_tensor(small[:, 52:56].unsqueeze(2), mids[:, :, 1:2], mids[:, :, 0:1], ALU.subtract)
            V.tensor_copy(small[:, 40:48].rearrange("p (c n) -> p c n", n=2), mids).then_inc(mid_made, 1)
            for c in range(CT):
                last = V.tensor_scalar(k2[:, c, :], aB[:, c, :], 1.0, per_channel(V_KA + c), ALU.subtract, ALU.mult)
            link(last)
            link(V.scalar_tensor_tensor(out=k2, in0=k2, scalar=1.0, in1=kB, op0=ALU.add, op1=ALU.mult))
            for c in range(CT):
                last = V.scalar_tensor_tensor(out=lw[:, c, :], in0=rB[:, c, :], scalar=per_channel(V_RK + c),
                                              in1=k2[:, c, :], op0=ALU.mult, op1=ALU.mult)
            last.then_inc(rkv_made, 1)
            dve.wait_ge(kk_root, 1)
            link(V.tensor_scalar(kk_scale, kk_scale, 1e-12, None, ALU.max))
            link(V.reciprocal(kk_scale, kk_scale))
            V.tensor_copy(tmp_flat.rearrange("p (a b) -> p a b", b=HD),
                          kk_scale.unsqueeze(2).to_broadcast([P, 16, HD])).then_inc(kk_inv, 1)
            dve.wait_ge(kk_ps, 1)
            for b in range(2):
                last = V.tensor_tensor(kk[:, 2 * b:2 * b + 2, :], kk[:, 2 * b:2 * b + 2, :],
                                       PS[:, 2 + b, :].rearrange("p (a b) -> p a b", a=2), ALU.mult)
            last.then_inc(kk_used, 1)
            dve.wait_ge(kk_used, 1)
            link(V.tensor_tensor(aB, kk, aB, ALU.mult))
            dve.wait_ge(bias_in, 64)
            for h in range(HEADS):
                dve.wait_ge(sc_ps, h + 1)
                V.scalar_tensor_tensor(out=Sb[:, h, :], in0=PS[:, S_BANKS[h % 4], 0:384], scalar=HD ** -0.5,
                                       in1=Sb[:, h, :], op0=ALU.mult, op1=ALU.add).then_inc(sc_sb, 1)
            dve.wait_ge(sc_sb, HEADS)
            V.tensor_reduce(small[:, 0:8], Sb[:, :, 0:P], AX_X, ALU.max, negate=True).then_inc(sc_max, 1)
            V.tensor_reduce(small[:, 8:16], Sb[:, :, P:P + T], AX_X, ALU.max, negate=True).then_inc(sc_max, 1)
            dve.wait_ge(vA_sb, 2)
            dve.wait_ge(e_made, 4 * CT + 1)
            V.tensor_tensor(bh, aB, EI, ALU.mult)
            V.tensor_tensor(kh, k2, EI, ALU.mult)
            for n in range(NT):
                t = slice(P * n, P * n + P)
                V.tensor_tensor(KR[:, :, 0, t], kk[:, :, t], E[:, :, n, 0:P], ALU.mult)
                last = V.tensor_tensor(KR[:, :, 1, t], rB[:, :, t], E[:, :, n, 1:P + 1], ALU.mult)
            last.then_inc(rkv_made, 1)
            dve.wait_ge(bon_ps, 1)
            for b in range(2):
                last = V.tensor_tensor(bonus[:, 2 * b:2 * b + 2, :], PS[:, 4 + b, :].rearrange("p (a b) -> p a b", a=2),
                                       vB[:, 2 * b:2 * b + 2, :], ALU.mult)
            last.then_inc(bon_made, 1)
            dve.wait_ge(mask_in, 16)
            dve.wait_ge(rkv_made, 2)
            dve.wait_ge(tok_ps, 4)
            for m in range(16):
                dve.wait_ge(mat_ps, m + 1)
                V.tensor_tensor(mats[:, m, :, :].rearrange("p a b -> p (a b)"), PS[:, 4 + m % 4, :], mask4,
                                ALU.mult).then_inc(mat_sb, 1)
            id4 = ident.unsqueeze(1).to_broadcast([P, 4, P])

            def bank4(b):
                return PS[:, b, :].rearrange("p (a b) -> p a b", a=4)
            dve.wait_ge(sc_exp, 16)
            link(V.reciprocal(small[:, 16:32], small[:, 16:32]))
            V.tensor_tensor(Sb[:, :, 0:P], Sb[:, :, 0:P], small[:, 16:24].unsqueeze(2).to_broadcast([P, HEADS, P]),
                            ALU.mult).then_inc(p_made, 1)
            V.tensor_tensor(Sb[:, :, P:P + T], Sb[:, :, P:P + T],
                            small[:, 24:32].unsqueeze(2).to_broadcast([P, HEADS, T]), ALU.mult).then_inc(p_made, 1)

            for q in range(4):
                dve.wait_ge(m1_ps, q + 1)
                link(V.tensor_tensor(X[:, 4 * q:4 * q + 4, :], bank4(4 + q), bcast4(C_NM1), ALU.mult))
                V.tensor_tensor(X[:, 4 * q:4 * q + 4, :], X[:, 4 * q:4 * q + 4, :], id4, ALU.add).then_inc(m1_sb, 1)
            for q in range(2, 4):
                a = slice(4 * q, 4 * q + 4)
                link(V.tensor_tensor(XT[:, a, :], mats[:, a, 2, :], bcast4(C_NM1T), ALU.mult))
                V.tensor_tensor(XT[:, a, :], XT[:, a, :], id4, ALU.add).then_inc(xt_made, 1)
            for b in range(2):
                dve.wait_ge(oa_ps, b + 1)
                split_out((2 * b, 2 * b + 2), PS[:, 2 + b, :].rearrange("p (a b) -> p a b", a=2)).then_inc(oa_made, 1)

            for c in range(CT):
                V.scalar_tensor_tensor(out=bonus[:, c, :], in0=bonus[:, c, :], scalar=per_channel(V_LB + c),
                                       in1=gB[:, c, :], op0=ALU.add, op1=ALU.mult)
            for c in range(CT):
                last = V.tensor_scalar(gB[:, c, :], gB[:, c, :], per_channel(V_LG + c), None, ALU.mult)
            link(last)
            for lv in range(len(LEVELS)):
                for q in range(4):
                    dve.wait_ge(p1_ps, 4 * lv + q + 1)
                    V.tensor_tensor(P1[:, 4 * q:4 * q + 4, :], bank4(q), bcast4(C_LV + P * lv),
                                    ALU.mult).then_inc(p1_sb, 1)
                for q in range(4):
                    dve.wait_ge(x_ps, 4 * lv + q + 1)
                    a = slice(4 * q, 4 * q + 4)
                    updated = X if lv < len(LEVELS) - 1 else XT
                    V.tensor_tensor(updated[:, a, :], updated[:, a, :], bank4(4 + q), ALU.subtract).then_inc(x_sb, 1)
            for n in range(NT):
                dve.wait_ge(g_ps, n + 1)
                V.tensor_copy(Gs.rearrange("p (a b) -> p a b", a=2), PS[:, 2:4, 0:T]).then_inc(g_sb, 1)
                dve.wait_ge(sk_ps, n + 1)
                V.tensor_scalar(nSK[:, n, :], PS[:, 4, :], -1.0, None, ALU.mult).then_inc(sk_sb, 1)
                if n == 0:
                    dve.wait_ge(st_ps, 1)
                    V.tensor_tensor(ST, PS[:, 5, 0:CT * HD].rearrange("p (c i) -> p c i", i=HD),
                                    small[:, 48:52].unsqueeze(2).to_broadcast([P, CT, HD]), ALU.mult).then_inc(st_sb, 1)
            dve.wait_ge(x_sb, 4 * len(LEVELS))
            dve.wait_ge(o_ps, 1)
            for b in range(2):
                last = V.tensor_copy(osb[:, 2 * b:2 * b + 2, :], PS[:, 6 + b, :].rearrange("p (a b) -> p a b", a=2))
            last.then_inc(o_sb, 1)
            dve.wait_ge(o_sb, 1)
            dve.wait_ge(mu_ps, 1)
            for b in range(2):
                last = V.scalar_tensor_tensor(out=ocen[:, 2 * b:2 * b + 2, :],
                                              in0=PS[:, 2 + b, :].rearrange("p (a b) -> p a b", a=2), scalar=-1.0 / HD,
                                              in1=osb[:, 2 * b:2 * b + 2, :], op0=ALU.mult, op1=ALU.add)
            link(last)
            V.tensor_tensor(osq, ocen, ocen, ALU.mult).then_inc(cen_sb, 1)
            link(V.tensor_tensor(ocen, ocen, gB, ALU.mult))
            dve.wait_ge(var_ps, 1)
            link(V.tensor_scalar(gn_scale, PS[:, 4, 0:16], 1.0 / HD, GN_EPS, ALU.mult, ALU.add))
            V.reciprocal(gn_scale, gn_scale).then_inc(gn_inv, 1)
            dve.wait_ge(gn_root, 1)
            V.tensor_copy(osb_flat.rearrange("p (a b) -> p a b", b=HD),
                          gn_scale.unsqueeze(2).to_broadcast([P, 16, HD])).then_inc(gn_wide, 1)
            dve.wait_ge(gn_ps, 1)
            for b in range(2):
                last = V.tensor_tensor(ocen[:, 2 * b:2 * b + 2, :], ocen[:, 2 * b:2 * b + 2, :],
                                       PS[:, 5 + b, :].rearrange("p (a b) -> p a b", a=2), ALU.mult)
            link(last)
            link(V.tensor_tensor(ocen, ocen, bonus, ALU.add))
            split_out((4, 8), ocen).then_inc(ob_made, 1)

            ya, yb = xn[:, 0, :], xn[:, 1, :]
            dve.wait_ge(act_evac, 2 + U_PROJ)
            for g in range(U_PROJ, U_OUT):
                k = g - U_PROJ
                dve.wait_ge(unit_done, g + 1)
                V.tensor_tensor(ya, PS[:, g % 2, 0:T], gates[:, k, :], ALU.mult)
                last = V.tensor_tensor(yb, PS[:, g % 2, T:2 * T], gates[:, KT + k, :], ALU.mult)
                last.then_inc(dve_evac, 1)
                dve.wait_ge(dve_evac, k + 1)
                link(V.tensor_tensor(ya, ya, yb, ALU.add))
                link(V.tensor_copy(xh[:, k, :], ya))
                V.tensor_tensor(xl[:, k, :], ya, xh[:, k, :].bitcast(F32), ALU.subtract).then_inc(y_made, 1)
                dve.wait_ge(y_made, k + 1)
            for g in range(U_OUT, U_Q):
                if g >= U_OUT + 2:
                    make_lo(g + 3, (g + 2) % 4)
                k = g - U_OUT
                dve.wait_ge(unit_done, g + 1)
                V.tensor_tensor(xT[:, k, :], xT[:, k, :], PS[:, g % 2, 0:T], ALU.add).then_inc(h_made, 1)
                dve.wait_ge(h_made, k + 1)
                V.tensor_tensor(sq[:, k, :], xT[:, k, :], xT[:, k, :], ALU.mult).then_inc(sq_made, 1)
            dve.wait_ge(ss_made, NT + 1)
            rms_inverse(rms[:, 0:2].unsqueeze(2), PS[:, 2:4, 0:1], inv_made)
            rms_scale(1, V_N2)
            for j in (2, 3):
                make_lo(U_Q + j + 1, j)
            with dve.Fori(1, 4) as i:
                for j in range(4):
                    make_lo(4 * i + (U_Q + j + 1), j)

            for n in range(NT):
                dve.wait_ge(score_sb, 8)

                def top16(values, vals, idx):
                    N = len(values)
                    for u in range(N):
                        last = V.max(vals[u][:, 0:8], values[u])
                    link(last)
                    for u in range(N):
                        last = V.max_index(idx[u][:, 0:8], vals[u][:, 0:8], values[u])
                    link(last)
                    for u in range(N):
                        last = V.match_replace(values[u], vals[u][:, 0:8], values[u], LOWEST)
                    link(last)
                    for u in range(N):
                        last = V.max(vals[u][:, 8:16], values[u])
                    link(last)
                    for u in range(N):
                        last = V.max_index(idx[u][:, 8:16], vals[u][:, 8:16], values[u])
                    link(last)

                top16([S[:, n, u, :] for u in range(16)], [tv[:, n, 16 * u:16 * u + 16] for u in range(16)],
                      [ti[:, n, 16 * u:16 * u + 16] for u in range(16)])
                V.tensor_copy(tif[:, n, :], ti[:, n, :])
                tv4 = tv[:, n, :].rearrange("p (h s k) -> p h s k", s=2, k=TOPK)
                ti4 = tif[:, n, :].rearrange("p (h s k) -> p h s k", s=2, k=TOPK)
                cand4 = cand.rearrange("p h (a b) -> p h a b", a=TOPK)
                link(V.tensor_tensor(cand4, tv4[:, :, 0, :].unsqueeze(3).to_broadcast([P, HEADS, TOPK, TOPK]),
                                     tv4[:, :, 1, :].unsqueeze(2).to_broadcast([P, HEADS, TOPK, TOPK]), ALU.add))
                top16([cand[:, h, :] for h in range(HEADS)], [bvs[:, n, 16 * h:16 * h + 16] for h in range(HEADS)],
                      [bp[:, 16 * h:16 * h + 16] for h in range(HEADS)])
                for side, dst in ((0, i1s), (1, i2s)):
                    if side == 0:
                        link(V.tensor_scalar(bpa, bp, 4, None, ALU.logical_shift_right))
                    else:
                        link(V.tensor_scalar(bpa, bp, 15, None, ALU.bitwise_and))
                    link(V.tensor_copy(bpf, bpa))
                    link(V.tensor_tensor(eqt, bpf.unsqueeze(2).to_broadcast([P, P, TOPK]),
                                         iota[:, 0:TOPK].unsqueeze(1).to_broadcast([P, P, TOPK]), ALU.is_equal))
                    e4 = eqt.rearrange("p (h k) j -> p h k j", h=HEADS)
                    link(V.tensor_tensor(e4, e4, ti4[:, :, side, :].unsqueeze(2).to_broadcast([P, HEADS, TOPK, TOPK]),
                                         ALU.mult))
                    link(V.tensor_reduce(dst[:, n, :], eqt, AX_X, ALU.add))
                b3 = bvs[:, n, :].rearrange("p (h k) -> p h k", k=TOPK)
                V.tensor_copy(small[:, 0:8].unsqueeze(2), b3[:, :, 0:1]).then_inc(dve_step, 1)
                steps[0] += 1
                dve.wait_ge(dve_step, steps[0])
                V.tensor_tensor(b3, b3, small[:, 0:8].unsqueeze(2).to_broadcast([P, HEADS, TOPK]),
                                ALU.subtract).then_inc(shift_made, 1)
            dve.wait_ge(exp_made, 1)
            b4 = bvs.rearrange("p n (h k) -> p (n h) k", k=TOPK)
            link(V.tensor_reduce(small[:, 0:16], b4, AX_X, ALU.add))
            link(V.reciprocal(small[:, 16:32], small[:, 0:16]))
            V.tensor_tensor(b4, b4, small[:, 16:32].unsqueeze(2).to_broadcast([P, 16, TOPK]),
                            ALU.mult).then_inc(picks_made, 1)
            for b, dst in ((2, i1T), (3, i2T), (4, gT)):
                dve.wait_ge(picks_ps, b - 1)
                V.tensor_copy(dst[:], PS[:, b, 0:T]).then_inc(picks_sb, 1)
            dve.wait_ge(picks_sb, 3)

            V.memset(coef[:, HALF:, :], 1.0).then_inc(coef_made, 2)

            def one_hots(i, j):
                dve.wait_ge(hot_ps, 4 * i + (j + 1))
                for k in range(4):
                    t = 16 * i + (4 * j + k)
                    V.tensor_scalar(oh1[:, j % 2, k, :], iota, i1T[:, bass.ds(t, 1)], gT[:, bass.ds(t, 1)],
                                    ALU.is_equal, ALU.mult)
                    last = V.tensor_scalar(oh2[:, j % 2, k, :], iota, i2T[:, bass.ds(t, 1)], None, ALU.is_equal)
                last.then_inc(hot_made, 1)

            def coefficients(i, j):
                n = 4 * i + j
                dve.wait_ge(hot_ps, n + 3)
                dve.wait_ge(coef_made, n + 2)
                c = coef[:, :, bass.ds(4 * n, 4)]
                V.tensor_tensor(c, PS[:, 2 + j % 2, :].rearrange("p (t k) -> p k t", t=4), c,
                                ALU.mult).then_inc(gates_used, 1)
                dve.wait_ge(act_evac, n + (2 + U_PROJ + 16 + HALF + 1))
                dve.wait_ge(gates_used, n + 3)
                c = coef[:, n + HALF, :]
                V.tensor_tensor(c, c, gt[:, j % 2, :], ALU.mult).then_inc(coef_made, 1)

            dve.sem_inc(gates_used, 2)
            one_hots(0, 0)
            one_hots(0, 1)
            dve.wait_ge(act_evac, 2 + U_PROJ + 16 + HALF)
            with dve.Fori(0, T // 16 - 1) as i:
                for j in range(4):
                    coefficients(i, j)
                    one_hots(i, j + 2)
            for j in range(4):
                coefficients(T // 16 - 1, j)
                if j < 2:
                    one_hots(T // 16 - 1, j + 2)
            dve.wait_ge(coef_made, HALF + 2)
            V.memset(zeros, 0.0).then_inc(zero_made, 1)
            with dve.Fori(0, NKEYS // 4) as i:
                for j in range(4):
                    dve.wait_ge(gh_made, 4 * i + (j + 1))
                    V.tensor_tensor(gl[:, j, :], coef[:, 4 * i + j, :], gh[:, j, :].bitcast(F32),
                                    ALU.subtract).then_inc(gl_made, 1)
                    make_lo(4 * i + (U_V + j + 1), j)
            dve.wait_ge(gain_in, 16)
            for n in range(NT):
                dve.wait_ge(fin_sq, 2 * n + 2)
                r0 = rms[:, 2 * n:2 * n + 1]
                link(V.tensor_tensor(r0, r0, rms[:, 2 * n + 1:2 * n + 2], ALU.add))
                rms_inverse(r0, r0, fin_inv)
            for b in range(4):
                if b % 2 == 0:
                    dve.wait_ge(fin_root, b // 2 + 1)
                h = slice(512 * (b % 2), 512 * (b % 2) + 512)
                V.scalar_tensor_tensor(out=result[:, b // 2, h], in0=PS[:, b, :], scalar=rms[:, b // 2 * 2:b // 2 * 2 + 1],
                                       in1=gain_all[:, h], op0=ALU.mult, op1=ALU.mult).then_inc(fin_sb, 1)


XL_POOL = 5
S_BANKS = [6, 7, 2, 3]
REL_ROW = 1


def chunk_head(m):
    return m // 8, HD * (m % 8 // 4), m % 4


def shape_constants(np):
    r = np.arange(P)
    c = np.zeros((P, NCONST), np.float32)
    c[:, C_ID:C_ID + P] = np.eye(P)
    c[:, C_ONE:C_ONE + P] = 1
    c[:, C_BLK:C_BLK + P] = r[:, None] // HD == r[None, :] // HD
    c[:, C_IOTA:C_IOTA + P] = r[None, :]
    strict, incl = r[None, :] > r[:, None], r[None, :] >= r[:, None]
    for n, m in enumerate((strict, incl, strict, incl)):
        c[:, C_M4 + P * n:C_M4 + P * n + P] = m

    def lower_left(n):
        t, s = r[:, None], r[None, :]
        return (t // (2 * n) == s // (2 * n)) & (t // n % 2 == 1) & (s // n % 2 == 0)
    c[:, C_NM1:C_NM1 + P] = -1.0 * lower_left(1)
    c[:, C_NM1T:C_NM1T + P] = -1.0 * lower_left(1).T
    for k, n in enumerate(LEVELS):
        c[:, C_LV + P * k:C_LV + P * k + P] = lower_left(n)
    hot = np.zeros((33, 512), np.float32)
    for m in range(512):
        n = T - 1 - m
        if n < 0:
            b = 32
        elif n < 16:
            b = n
        else:
            f = np.float32(np.log(np.float32(n) / np.float32(16))) / np.float32(math.log(128 / 16))
            b = min(16 + int(np.float32(f) * np.float32(16)), 31)
        hot[b, m] = 1
    return c, hot


def kernel(**inputs):
    import numpy as _np
    import concourse.bacc as _bacc
    from concourse import mybir as _mybir
    from concourse.bass_utils import run_bass_kernel_spmd as _run

    i = {k: _np.asarray(v) for k, v in inputs.items()}

    def units(w):
        n = w.shape[1] // P
        return _np.ascontiguousarray(w.reshape(KT, P, n, P).transpose(2, 1, 0, 3)).reshape(n, P, D)

    def cols(a):
        return a.reshape(-1, P).T

    w = i['w_in'][0]
    n_in = 3 * W + 3 * W + 2 * LORA + GLORA
    w_all = _np.zeros((D, (NB_IN + NB_GATE) * P), w.dtype)
    w_all[:, :n_in - 3 * W] = w[:, 3 * W:n_in]
    w_all[:, NB_R * P:NB_IN * P] = w[:, :3 * W]
    w_all[:, NB_IN * P:(NB_IN + 4) * P] = w[:, -4 * P:]
    w_all[:, (NB_IN + 4) * P:] = w[:, n_in:-4 * P]
    mu = _np.zeros((NMIX * P,), w.dtype)
    mu[:n_in - 3 * W] = i['rwkv_mu'][0]
    vecs = _np.concatenate([cols(a) for a in (
        i['norm1_g'][0], i['norm2_g'][0], i['w0'][0], i['a0'][0], i['k_k'][0], i['k_a'][0],
        i['r_k'][0].reshape(-1), i['lnx_g'][0], i['lnx_b'][0], mu)], axis=1)
    consts, hot = shape_constants(_np)
    arrays = {
        'x': i['x'][0],
        'w_in_units': units(w_all),
        'w_proj_units': units(_np.concatenate([i['w_proj_a'][0], i['w_proj_b'][0]], axis=0)),
        'w_out_units': units(i['w_out'][0]),
        'w_q_units': units(i['peer_wq'][0]),
        'u_units': i['peer_u'][0].reshape(NKEYS, NKEYS, KT, P).transpose(1, 3, 2, 0).reshape(NKEYS, P, D),
        'v_units': i['peer_v'][0].reshape(NKEYS, NKEYS, D).transpose(1, 0, 2),
        'vecs': vecs,
        'gain_row': i['normf_g'].reshape(1, D),
        'lora_wa': _np.concatenate([i['w_lora_up'][0], i['a_lora_up'][0]], axis=0),
        'lora_g': i['g_lora_up'][0],
        'rel_bias_t': i['rel_bias'].T,
        'bucket_onehot': hot,
        'consts': consts,
        'subkeys_t': i['peer_subkeys'][0].reshape(2 * HEADS, NKEYS, P).transpose(2, 0, 1),
    }
    nc = _bacc.Bacc("TRN2", target_bir_lowering=False, num_devices=1)
    sent, args = {}, []
    for name, a in arrays.items():
        a = _np.ascontiguousarray(a)
        sent[f"in_{name}"] = a
        args.append(nc.dram_tensor(f"in_{name}", a.shape, _mybir.dt.from_np(a.dtype), kind="ExternalInput").ap())
    args.append(nc.dram_tensor("out_0", (T, D), F32, kind="ExternalOutput").ap())
    block_program(nc, *args)
    r = _run(nc, [sent], core_ids=[0])
    return r.results[0]["out_0"].reshape(1, T, D)
```
